# Optimizing a Trainium2 kernel written in Bass

```python
import math
import jax, jax.numpy as jnp
from jax import lax
import numpy as np

D_MODEL = 1024
BATCH = 1
SEQ = 256
DEPTH = 2

N_CONV_LAYERS = DEPTH // 2
N_ATTN_LAYERS = DEPTH - N_CONV_LAYERS
N_HEADS = 8
HEAD_DIM = D_MODEL // (2 * N_HEADS)
V_HEAD_DIM = 2 * HEAD_DIM
CONV_WIDTH = 31
FFN_CONV_WIDTH = 3
D_FF = ((8 * D_MODEL // 3 + 255) // 256) * 256
N_BUCKETS = 32
MAX_DISTANCE = 128
MAX_EXACT = N_BUCKETS // 2
Q_BLOCK = 128
EPS = 1e-6


def rms_norm(x, g):
    x32 = x.astype(jnp.float32)
    y = x32 * lax.rsqrt(jnp.mean(x32 * x32, axis=-1, keepdims=True) + EPS)
    return (y * g.astype(jnp.float32)).astype(x.dtype)

def layer_norm(x, g, b):
    x32 = x.astype(jnp.float32)
    mu = jnp.mean(x32, axis=-1, keepdims=True)
    var = jnp.mean(jnp.square(x32 - mu), axis=-1, keepdims=True)
    y = (x32 - mu) * lax.rsqrt(var + EPS) * g.astype(jnp.float32) + b.astype(jnp.float32)
    return y.astype(x.dtype)

def causal_dwconv(x, w, b):
    width = w.shape[0]
    y = lax.conv_general_dilated(
        x, w[:, None, :].astype(x.dtype), window_strides=(1,), padding=[(width - 1, 0)],
        dimension_numbers=("NWC", "WIO", "NWC"), feature_group_count=x.shape[-1])
    return y + b

def conformer_conv(h, w1, b1, dw, dwb, ln_g, ln_b, w2, b2):
    u = h @ w1 + b1
    a, gt = jnp.split(u, 2, axis=-1)
    u = a * jax.nn.sigmoid(gt)
    u = causal_dwconv(u, dw, dwb)
    u = jax.nn.silu(layer_norm(u, ln_g, ln_b))
    return u @ w2 + b2

def conv_ffn(h, w_in, dw, dwb, w_out):
    u = causal_dwconv(h @ w_in, dw, dwb)
    g, v = jnp.split(u, 2, axis=-1)
    return (jax.nn.silu(g) * v) @ w_out

def t5_bucket(n):
    n_f = jnp.maximum(n, 1).astype(jnp.float32)
    large = MAX_EXACT + (jnp.log(n_f / MAX_EXACT) / math.log(MAX_DISTANCE / MAX_EXACT)
                         * (N_BUCKETS - MAX_EXACT)).astype(jnp.int32)
    large = jnp.minimum(large, N_BUCKETS - 1)
    return jnp.where(n < MAX_EXACT, n, large)

def diff_attention(h, k, v, w_q, lam_vec, subln_g, w_o, rel_bias, lambda_init):
    bsz, seq, _ = h.shape
    n_blocks = seq // Q_BLOCK
    q = (h @ w_q).reshape(bsz, n_blocks, Q_BLOCK, N_HEADS, 2, HEAD_DIM)
    q = jnp.moveaxis(q, 1, 0)
    lv = lam_vec.astype(jnp.float32)
    lam = jnp.exp(jnp.sum(lv[0] * lv[1])) - jnp.exp(jnp.sum(lv[2] * lv[3])) + lambda_init
    starts = jnp.arange(n_blocks, dtype=jnp.int32) * Q_BLOCK
    k_pos = jnp.arange(seq, dtype=jnp.int32)
    scale = HEAD_DIM ** -0.5

    def one_block(args):
        q_blk, start = args
        q_pos = start + jnp.arange(Q_BLOCK, dtype=jnp.int32)
        rel = q_pos[:, None] - k_pos[None, :]
        bias = jnp.transpose(rel_bias[t5_bucket(jnp.maximum(rel, 0))], (2, 0, 1)).astype(jnp.float32)
        s = jnp.einsum("bqhcd,bkhcd->bhcqk", q_blk, k).astype(jnp.float32) * scale + bias[None, :, None]
        s = jnp.where(rel >= 0, s, -jnp.inf)
        p = jax.nn.softmax(s, axis=-1)
        a = (p[:, :, 0] - lam * p[:, :, 1]).astype(v.dtype)
        return jnp.einsum("bhqk,bkhe->bqhe", a, v)

    o = lax.map(one_block, (q, starts))
    o = jnp.moveaxis(o, 0, 1).reshape(bsz, seq, N_HEADS, V_HEAD_DIM)
    o = rms_norm(o, subln_g) * (1.0 - lambda_init)
    return o.reshape(bsz, seq, N_HEADS * V_HEAD_DIM) @ w_o

def first_inputs(seed: int = 0) -> dict:
    key = jax.random.key(seed)
    ks = jax.random.split(key, 25)
    f32 = jnp.float32

    def nrm(k, shape, s):
        return jax.random.normal(k, shape, f32) * s

    D, F, H, A, Bn = D_MODEL, D_FF, N_HEADS, N_CONV_LAYERS, N_ATTN_LAYERS
    return {
        "x": nrm(ks[0], (BATCH, SEQ, D), 1.0),
        "c": nrm(ks[1], (BATCH, D), 1.0),
        "mod_w": nrm(ks[2], (DEPTH, D, 6 * D), D ** -0.5),
        "mod_b": nrm(ks[3], (DEPTH, 6 * D), 0.02),
        "norm_g": 1.0 + nrm(ks[4], (DEPTH, 4, D), 0.05),
        "cm_w1": nrm(ks[5], (A, D, 2 * D), D ** -0.5),
        "cm_b1": nrm(ks[6], (A, 2 * D), 0.02),
        "cm_dw": nrm(ks[7], (A, CONV_WIDTH, D), CONV_WIDTH ** -0.5),
        "cm_dwb": nrm(ks[8], (A, D), 0.02),
        "cm_ln_g": 1.0 + nrm(ks[9], (A, D), 0.05),
        "cm_ln_b": nrm(ks[10], (A, D), 0.02),
        "cm_w2": nrm(ks[11], (A, D, D), D ** -0.5),
        "cm_b2": nrm(ks[12], (A, D), 0.02),
        "kv_norm_g": 1.0 + nrm(ks[13], (D,), 0.05),
        "w_k": nrm(ks[14], (D, H * 2 * HEAD_DIM), D ** -0.5),
        "w_v": nrm(ks[15], (D, H * V_HEAD_DIM), D ** -0.5),
        "w_q": nrm(ks[16], (Bn, D, H * 2 * HEAD_DIM), D ** -0.5),
        "lam": nrm(ks[17], (Bn, 4, HEAD_DIM), 0.1),
        "subln_g": 1.0 + nrm(ks[18], (Bn, V_HEAD_DIM), 0.05),
        "w_o": nrm(ks[19], (Bn, H * V_HEAD_DIM, D), (H * V_HEAD_DIM) ** -0.5),
        "rel_bias": nrm(ks[20], (N_BUCKETS, H), 0.5),
        "ffn_w_in": nrm(ks[21], (DEPTH, D, 2 * F), D ** -0.5),
        "ffn_dw": nrm(ks[22], (DEPTH, FFN_CONV_WIDTH, 2 * F), FFN_CONV_WIDTH ** -0.5),
        "ffn_dwb": nrm(ks[23], (DEPTH, 2 * F), 0.02),
        "ffn_w_out": nrm(ks[24], (DEPTH, F, D), F ** -0.5),
    }

def first_block(x, c, mod_w, mod_b, norm_g, cm_w1, cm_b1, cm_dw, cm_dwb, cm_ln_g, cm_ln_b, cm_w2, cm_b2,
              kv_norm_g, w_k, w_v, w_q, lam, subln_g, w_o, rel_bias, ffn_w_in, ffn_dw, ffn_dwb, ffn_w_out):
    bsz, seq, _ = x.shape
    c_act = jax.nn.silu(c)
    k_shared = None
    v_shared = None
    for l in range(DEPTH):
        mod = c_act @ mod_w[l] + mod_b[l]
        sh_m, sc_m, g_m, sh_f, sc_f, g_f = [m[:, None, :] for m in jnp.split(mod, 6, axis=-1)]

        h = rms_norm(x, norm_g[l, 0]) * (1.0 + sc_m) + sh_m
        if l < N_CONV_LAYERS:
            y = conformer_conv(h, cm_w1[l], cm_b1[l], cm_dw[l], cm_dwb[l], cm_ln_g[l], cm_ln_b[l],
                               cm_w2[l], cm_b2[l])
        else:
            if l == N_CONV_LAYERS:
                hkv = rms_norm(x, kv_norm_g)
                k_shared = (hkv @ w_k).reshape(bsz, seq, N_HEADS, 2, HEAD_DIM)
                v_shared = (hkv @ w_v).reshape(bsz, seq, N_HEADS, V_HEAD_DIM)
            j = l - N_CONV_LAYERS
            lambda_init = 0.8 - 0.6 * math.exp(-0.3 * l)
            y = diff_attention(h, k_shared, v_shared, w_q[j], lam[j], subln_g[j], w_o[j], rel_bias, lambda_init)
        x = x + g_m * rms_norm(y, norm_g[l, 1])

        h = rms_norm(x, norm_g[l, 2]) * (1.0 + sc_f) + sh_f
        y = conv_ffn(h, ffn_w_in[l], ffn_dw[l], ffn_dwb[l], ffn_w_out[l])
        x = x + g_f * rms_norm(y, norm_g[l, 3])
    return x


N_MIXERS = 2
CHUNK = 64
RMS_EPS = 1e-6

RWKV_HEAD = 64
RWKV_HEADS = D_MODEL // RWKV_HEAD
DECAY_LORA = max(32, int(round(1.8 * D_MODEL ** 0.5 / 32)) * 32)
A_LORA = max(32, int(round(1.8 * D_MODEL ** 0.5 / 32)) * 32)
GATE_LORA = max(32, int(round(0.6 * D_MODEL ** 0.8 / 32)) * 32)
GN_EPS = 64e-5
N_SHIFT_MIX = 6

SGU_BLOCK = 128
D_SGU = D_MODEL
SGU_GROUPS = 8
SGU_GROUP_DIM = D_SGU // SGU_GROUPS
LN_EPS = 1e-5

D_FF_2 = -(-8 * D_MODEL // (3 * 256)) * 256

N_A = (DEPTH + 1) // N_MIXERS + (0 if N_MIXERS == 2 else 0)
N_B = DEPTH // N_MIXERS


def _rmsnorm(x, g):
    x32 = x.astype(jnp.float32)
    y = x32 * lax.rsqrt(jnp.mean(x32 * x32, axis=-1, keepdims=True) + RMS_EPS)
    return (y * g.astype(jnp.float32)).astype(x.dtype)

def _token_shift(x):
    return jnp.pad(x[:, :-1], ((0, 0), (1, 0), (0, 0)))

def _rwkv7_scan(r, w, k, v, a, b):
    B, T, H, N = r.shape

    def step(S, inp):
        r_t, w_t, k_t, v_t, a_t, b_t = inp
        sa = jnp.einsum('bhij,bhj->bhi', S, a_t)
        S = (S * w_t[:, :, None, :]
             + sa[..., None] * b_t[:, :, None, :]
             + v_t[..., None] * k_t[:, :, None, :])
        y = jnp.einsum('bhij,bhj->bhi', S, r_t)
        return S, y

    xs = tuple(jnp.moveaxis(t, 1, 0) for t in (r, w, k, v, a, b))
    S0 = jnp.zeros((B, H, N, N), jnp.float32)
    _, y = lax.scan(step, S0, xs)
    return jnp.moveaxis(y, 0, 1)

def _rwkv7_time_mix(x, mix, w_rkv, w0, w1, w2, a0, a1, a2, g1, g2,
                    k_k, k_a, r_k, gn_w, gn_b, w_o):
    B, T, D = x.shape
    H, N = RWKV_HEADS, RWKV_HEAD
    f32 = jnp.float32
    xx = _token_shift(x) - x
    xs = x[None] + xx[None] * mix[:, None, None, :]
    r, k, v = jnp.einsum('cbtd,cde->cbte', xs[:3], w_rkv)
    xw, xa, xg = xs[3], xs[4], xs[5]
    w_raw = (w0 + jnp.tanh(xw @ w1) @ w2).astype(f32)
    w_log = -jax.nn.softplus(-w_raw) - 0.5
    decay = jnp.exp(-jnp.exp(w_log))
    a = jax.nn.sigmoid(a0 + (xa @ a1) @ a2)
    g = jax.nn.sigmoid(xg @ g1) @ g2
    heads = lambda t: t.reshape(B, T, H, N).astype(f32)
    kk = heads(k * k_k)
    kk = kk / jnp.maximum(jnp.sqrt(jnp.sum(kk * kk, axis=-1, keepdims=True)), 1e-12)
    k = k * (1.0 + (a - 1.0) * k_a)
    r_h, k_h, v_h, a_h = heads(r), heads(k), heads(v), heads(a)
    y = _rwkv7_scan(r_h, decay.reshape(B, T, H, N), k_h, v_h, -kk, kk * a_h)
    mu = jnp.mean(y, axis=-1, keepdims=True)
    var = jnp.mean(jnp.square(y - mu), axis=-1, keepdims=True)
    y = (y - mu) * lax.rsqrt(var + GN_EPS)
    y = y * gn_w.reshape(H, N).astype(f32) + gn_b.reshape(H, N).astype(f32)
    y = y + jnp.sum(r_h * k_h * r_k.astype(f32), axis=-1, keepdims=True) * v_h
    y = y.reshape(B, T, D).astype(x.dtype)
    return (y * g) @ w_o

def _sgu_mixer(x, w_in, b_in, ln_w, ln_b, ws, bs, w_out):
    B, T, D = x.shape
    h = jax.nn.gelu(x @ w_in + b_in, approximate=False)
    u, v = jnp.split(h, 2, axis=-1)
    v32 = v.astype(jnp.float32)
    mu = jnp.mean(v32, axis=-1, keepdims=True)
    var = jnp.mean(jnp.square(v32 - mu), axis=-1, keepdims=True)
    v = ((v32 - mu) * lax.rsqrt(var + LN_EPS) * ln_w.astype(jnp.float32)
         + ln_b.astype(jnp.float32)).astype(x.dtype)
    n_blk = T // SGU_BLOCK
    vb = v.reshape(B, n_blk, SGU_BLOCK, SGU_GROUPS, SGU_GROUP_DIM)
    chunk_id = jnp.arange(SGU_BLOCK) // CHUNK
    mask = chunk_id[None, :] <= chunk_id[:, None]
    ws_m = jnp.where(mask[None], ws, jnp.zeros((), ws.dtype))
    s = jnp.einsum('gij,bnjgc->bnigc', ws_m, vb) + bs.T[None, None, :, :, None]
    s = s.reshape(B, T, D_SGU)
    return (u * s) @ w_out

def _swiglu(x, w_gate, w_up, w_down):
    return (jax.nn.silu(x @ w_gate) * (x @ w_up)) @ w_down

def second_inputs(seed: int = 0) -> dict:
    key = jax.random.key(seed)
    ks = jax.random.split(key, 32)
    D = D_MODEL
    nrm = lambda k, shape, scale: jax.random.normal(k, shape, jnp.float32) * scale
    return {
        "x": nrm(ks[0], (BATCH, SEQ, D), 1.0),
        "norm_gains": 1.0 + nrm(ks[1], (DEPTH, 4, D), 0.1),
        "rwkv_mix": jax.random.uniform(ks[2], (N_A, N_SHIFT_MIX, D), jnp.float32),
        "rwkv_w_rkv": nrm(ks[3], (N_A, 3, D, D), D ** -0.5),
        "rwkv_w0": jax.random.uniform(ks[4], (N_A, D), jnp.float32, -6.5, -1.5),
        "rwkv_w1": nrm(ks[5], (N_A, D, DECAY_LORA), D ** -0.5),
        "rwkv_w2": nrm(ks[6], (N_A, DECAY_LORA, D), 0.5 * DECAY_LORA ** -0.5),
        "rwkv_a0": nrm(ks[7], (N_A, D), 0.1),
        "rwkv_a1": nrm(ks[8], (N_A, D, A_LORA), D ** -0.5),
        "rwkv_a2": nrm(ks[9], (N_A, A_LORA, D), 0.5 * A_LORA ** -0.5),
        "rwkv_g1": nrm(ks[10], (N_A, D, GATE_LORA), D ** -0.5),
        "rwkv_g2": nrm(ks[11], (N_A, GATE_LORA, D), GATE_LORA ** -0.5),
        "rwkv_k_k": 0.85 + nrm(ks[12], (N_A, D), 0.05),
        "rwkv_k_a": 1.0 + nrm(ks[13], (N_A, D), 0.05),
        "rwkv_r_k": -0.04 + nrm(ks[14], (N_A, RWKV_HEADS, RWKV_HEAD), 0.02),
        "rwkv_gn_w": 1.0 + nrm(ks[15], (N_A, D), 0.1),
        "rwkv_gn_b": nrm(ks[16], (N_A, D), 0.02),
        "rwkv_w_o": nrm(ks[17], (N_A, D, D), D ** -0.5),
        "sgu_w_in": nrm(ks[18], (N_B, D, 2 * D_SGU), D ** -0.5),
        "sgu_b_in": nrm(ks[19], (N_B, 2 * D_SGU), 0.02),
        "sgu_ln_w": 1.0 + nrm(ks[20], (N_B, D_SGU), 0.1),
        "sgu_ln_b": nrm(ks[21], (N_B, D_SGU), 0.02),
        "sgu_ws": nrm(ks[22], (N_B, SGU_GROUPS, SGU_BLOCK, SGU_BLOCK), SGU_BLOCK ** -0.5),
        "sgu_bs": 1.0 + nrm(ks[23], (N_B, SGU_GROUPS, SGU_BLOCK), 0.1),
        "sgu_w_out": nrm(ks[24], (N_B, D_SGU, D), D_SGU ** -0.5),
        "ffn_w_gate": nrm(ks[25], (DEPTH, D, D_FF_2), D ** -0.5),
        "ffn_w_up": nrm(ks[26], (DEPTH, D, D_FF_2), D ** -0.5),
        "ffn_w_down": nrm(ks[27], (DEPTH, D_FF_2, D), D_FF_2 ** -0.5),
    }

def second_block(x, norm_gains,
              rwkv_mix, rwkv_w_rkv, rwkv_w0, rwkv_w1, rwkv_w2, rwkv_a0, rwkv_a1, rwkv_a2,
              rwkv_g1, rwkv_g2, rwkv_k_k, rwkv_k_a, rwkv_r_k, rwkv_gn_w, rwkv_gn_b, rwkv_w_o,
              sgu_w_in, sgu_b_in, sgu_ln_w, sgu_ln_b, sgu_ws, sgu_bs, sgu_w_out,
              ffn_w_gate, ffn_w_up, ffn_w_down):
    for i in range(DEPTH):
        j = i // N_MIXERS
        h = _rmsnorm(x, norm_gains[i, 0])
        if i % N_MIXERS == 0:
            h = _rwkv7_time_mix(h, rwkv_mix[j], rwkv_w_rkv[j], rwkv_w0[j], rwkv_w1[j],
                                rwkv_w2[j], rwkv_a0[j], rwkv_a1[j], rwkv_a2[j], rwkv_g1[j],
                                rwkv_g2[j], rwkv_k_k[j], rwkv_k_a[j], rwkv_r_k[j],
                                rwkv_gn_w[j], rwkv_gn_b[j], rwkv_w_o[j])
        else:
            h = _sgu_mixer(h, sgu_w_in[j], sgu_b_in[j], sgu_ln_w[j], sgu_ln_b[j],
                           sgu_ws[j], sgu_bs[j], sgu_w_out[j])
        x = x + _rmsnorm(h, norm_gains[i, 1])
        h = _rmsnorm(x, norm_gains[i, 2])
        h = _swiglu(h, ffn_w_gate[i], ffn_w_up[i], ffn_w_down[i])
        x = x + _rmsnorm(h, norm_gains[i, 3])
    return x


def setup_inputs(seed=0):
    out = dict(first_inputs(seed))
    for name, value in second_inputs(seed + 1).items():
        if name != "x":
            out[name + "_2"] = value
    return out


def reference(
    x, c, mod_w, mod_b, norm_g, cm_w1, cm_b1, cm_dw, cm_dwb, cm_ln_g, cm_ln_b, cm_w2, cm_b2,
    kv_norm_g, w_k, w_v, w_q, lam, subln_g, w_o, rel_bias, ffn_w_in, ffn_dw, ffn_dwb, ffn_w_out,
    norm_gains_2, rwkv_mix_2, rwkv_w_rkv_2, rwkv_w0_2, rwkv_w1_2, rwkv_w2_2, rwkv_a0_2,
    rwkv_a1_2, rwkv_a2_2, rwkv_g1_2, rwkv_g2_2, rwkv_k_k_2, rwkv_k_a_2, rwkv_r_k_2, rwkv_gn_w_2,
    rwkv_gn_b_2, rwkv_w_o_2, sgu_w_in_2, sgu_b_in_2, sgu_ln_w_2, sgu_ln_b_2, sgu_ws_2, sgu_bs_2,
    sgu_w_out_2, ffn_w_gate_2, ffn_w_up_2, ffn_w_down_2,
):
    x = first_block(
        x, c, mod_w, mod_b, norm_g, cm_w1, cm_b1, cm_dw, cm_dwb, cm_ln_g, cm_ln_b, cm_w2, cm_b2,
        kv_norm_g, w_k, w_v, w_q, lam, subln_g, w_o, rel_bias, ffn_w_in, ffn_dw, ffn_dwb,
        ffn_w_out,
    )
    return second_block(
        x, norm_gains_2, rwkv_mix_2, rwkv_w_rkv_2, rwkv_w0_2, rwkv_w1_2, rwkv_w2_2, rwkv_a0_2,
        rwkv_a1_2, rwkv_a2_2, rwkv_g1_2, rwkv_g2_2, rwkv_k_k_2, rwkv_k_a_2, rwkv_r_k_2,
        rwkv_gn_w_2, rwkv_gn_b_2, rwkv_w_o_2, sgu_w_in_2, sgu_b_in_2, sgu_ln_w_2, sgu_ln_b_2,
        sgu_ws_2, sgu_bs_2, sgu_w_out_2, ffn_w_gate_2, ffn_w_up_2, ffn_w_down_2,
    )


_drawn_inputs = setup_inputs


def setup_inputs(seed=0):
    import zlib

    import numpy as np

    out = dict(_drawn_inputs(seed))
    spreads = {}
    factors = {'cm_b1': 2.966, 'rwkv_gn_b_2': 3.584, 'sgu_b_in_2': 4.847, 'sgu_ln_b_2': 8.0}
    for name, (base, spread) in spreads.items():
        noise = np.random.default_rng([zlib.crc32(name.encode()), seed]).standard_normal(out[name].shape)
        drawn = base * np.exp(spread * noise) if base else spread * noise
        out[name] = __import__('jax').numpy.asarray(drawn.astype(out[name].dtype))
    for name, factor in factors.items():
        out[name] = (out[name] * factor).astype(out[name].dtype)
    return out
```

```python
from contextlib import ExitStack
import math

import numpy as np

import concourse.bass as bass
from concourse import mybir

F32 = mybir.dt.float32
F32R = mybir.dt.float32r
ALU = mybir.AluOpType
ACT = mybir.ActivationFunctionType
AX_X = mybir.AxisListType.X
ds = bass.ds

P = 128
D = 1024
T = 256
DC = D // P
DFF = 2816
FC = DFF // P
TAPS = 31
PE_TAPS = 12
PAD = TAPS - 1
HEADS = 8
HEAD_DIM = 64
EPS = 1e-6
LN_EPS = 1e-5
GN_EPS = 64e-5
LAMBDA_INIT = 0.8 - 0.6 * math.exp(-0.3)
KAPPA = math.exp(-0.5)
RH = 16
RN = 64
LORA = 64
GATE = 160
SLOTS = 4
LEAD = 2
KT, KT_DOWN = DC, FC // 2

PHASES = [
    ("conv_up", 16, KT), ("conv_down", 8, KT), ("ffn0_up", 2 * FC, KT), ("ffn0_down", 16, KT_DOWN),
    ("att_v", 8, KT), ("att_k", 8, KT), ("att_q", 8, KT), ("att_out", 8, KT),
    ("ffn1_up", 2 * FC, KT), ("ffn1_down", 16, KT_DOWN),
    ("rw_r", 8, KT), ("rw_k", 8, KT), ("rw_v", 8, KT), ("rw_out", 8, KT),
    ("glu0_up", 2 * FC, KT), ("glu0_down", 16, KT_DOWN),
    ("sgu_v", 8, KT), ("sgu_u", 8, KT), ("sgu_out", 8, KT),
    ("glu1_up", 2 * FC, KT), ("glu1_down", 16, KT_DOWN),
]
NAMES = [n for n, _, _ in PHASES]
START, COUNT, TILES, OWN = {}, {}, {}, {}
_at, _own = 0, {KT: 0, KT_DOWN: 0}
for _n, _c, _k in PHASES:
    START[_n], COUNT[_n], TILES[_n], OWN[_n] = _at, _c, _k, _own[_k]
    _at += _c
    _own[_k] += _c
UNITS = _at

MOD_START = 2 * DC
RIDES = {
    "conv_up": (MOD_START, 8, (0, 1, 2, 3)), "conv_down": (6 * DC, 2, (0, 1)), "ffn0_up": (6 * DC + 2, 2, (2, 3)),
    "ffn0_down": (9 * DC, 4, (0, 1, 2, 3)), "att_v": (11 * DC, 4, (0, 1, 2, 3)),
}
_loads = [MOD_START // SLOTS] * SLOTS
LOADS_BEFORE = {}
for _n, (_, _per, _slots) in RIDES.items():
    LOADS_BEFORE[_n] = list(_loads)
    for _s in _slots:
        _loads[_s] += _per // len(_slots) * (1 if _n == "conv_down" else COUNT[_n] // SLOTS)


SHARED = {"conv_up": MOD_START, "ffn0_up": RIDES["ffn0_up"][0] - (6 * DC - MOD_START)}


def riders(name, i, r):
    first, per, slots = RIDES[name]
    mine = {8: (2 * r, 2 * r + 1), 4: (r,), 2: (r // 2,) if r % 2 else ()}[per]
    return [(per * i + (first + j), slots[j % len(slots)],
             per // len(slots) * i + (LOADS_BEFORE[name][slots[j % len(slots)]] + j // len(slots) + 1)) for j in mine]

PARAMS = [
    ("mod_b", 96), ("norm_g", 64), ("cm_b1", 16), ("cm_dw", TAPS * 8), ("cm_dwb", 8),
    ("cm_ln_g", 8), ("cm_ln_b", 8), ("cm_b2", 8), ("kv_norm_g", 8), ("lam", 4), ("subln_g", 1),
    ("ffn_dw", 2 * 3 * 2 * FC), ("ffn_dwb", 2 * 2 * FC),
    ("norm_g2", 64), ("mix", 48), ("w0", 8), ("a0", 8), ("k_k", 8), ("k_a", 8), ("r_k", 8),
    ("gn_w", 8), ("gn_b", 8), ("sgu_b_in", 16), ("sgu_ln_w", 8), ("sgu_ln_b", 8),
]
COL = {}
_at = 0
for _n, _c in PARAMS:
    COL[_n] = _at
    _at += _c
NPAR = _at

CONSTS = [("ident", P), ("ones", P), ("heads", P), ("before", P), ("upto", P)] + [(f"level{n}", P) for n in range(7)] \
    + [("bucket", 384), ("future", 384)]
CCOL = {}
_at = 0
for _n, _c in CONSTS:
    CCOL[_n] = _at
    _at += _c
NCONST = _at


def constants():
    s, t = np.arange(P)[:, None], np.arange(P)[None, :]
    out = np.zeros((P, NCONST), np.float32)

    def put(name, value):
        out[:value.shape[0], CCOL[name]:CCOL[name] + value.shape[1]] = value

    put("ident", np.eye(P))
    put("ones", np.ones((P, P)))
    put("heads", (s // RN == t // RN) * 1.0)
    put("before", (s < t) * 1.0)
    put("upto", (s <= t) * 1.0)
    for n in range(7):
        put(f"level{n}", ((s >> n) % 2 == 0) * ((t >> n) == (s >> n) + 1) * 1.0)
    n = np.maximum(np.arange(384) - 127, 0)
    large = 16 + np.floor(np.log(np.maximum(n, 1) / 16) / math.log(8) * 16 + 1e-9)
    bucket = np.where(n < 16, n, np.minimum(large, 31)).astype(int)
    put("bucket", (np.arange(32)[:, None] == bucket[None, :]) * 1.0)
    put("future", np.repeat((np.arange(384)[None, :] < 127) * -1e30, 8, axis=0))
    return out


def program(nc, w8, w11, wmod, par, con, xin, relb, crow, lora_in, lora_out, sgu_ws, sgu_bs, out, debug=None):
    scratch = nc.dram_tensor("rel_bias_rows", (HEADS, 384), F32, kind="Internal").ap()

    with ExitStack() as ctx:
        used = {}

        def S(name):
            if name not in used:
                used[name] = ctx.enter_context(nc.semaphore(name))
            return used[name]

        base = nc.sbuf_base + (-nc.sbuf_base) % 32
        top = [base]

        def fixed(name, shape, dt=F32):
            n = 4 * int(np.prod(shape[1:]))
            t = nc.alloc_sbuf_tensor_at(name, shape, dt, offset=top[0])
            top[0] += n + (-n) % 32
            return t

        UW = KT_DOWN * P
        raw = fixed("raw", [P, SLOTS, UW])
        hi_at = top[0]
        hi = fixed("hi", [P, SLOTS, UW], F32R)
        lo_at = top[0]
        lo = fixed("lo", [P, SLOTS, UW], F32R)
        X = fixed("X", [P, DC, T])
        par_sb = fixed("par_sb", [P, NPAR])
        con_sb = fixed("con_sb", [P, NCONST])
        root = fixed("root", [P, 2, T])
        inv = fixed("inv", [P, 2, T])
        xt = fixed("xt", [P, 4, T])
        mods = fixed("mods", [P, 96])
        ngain = fixed("ngain", [P, 4, DC])
        rgain = fixed("rgain", [P, 4, DC])
        mod_sums = fixed("mod_sums", [P, 96])
        small = fixed("small", [P, 32])
        mid = fixed("mid", [P, 16])
        dec = fixed("dec", [P, DC])

        F = 8320
        arena = top[0]

        def at(place, name, shape, dt=F32, plus=0):
            return nc.alloc_sbuf_tensor_at(name, shape, dt, offset=arena + (int(place * F) + plus) // 32 * 32)

        Y = at(0, "Y", [P, DC, T])
        SQ = at(1, "SQ", [P, DC, T])
        HT = at(1, "HT", [P, DC, T])
        OH = at(2, "OH", [P, DC, T], F32R)
        OL = at(3, "OL", [P, DC, T], F32R)
        tmp = at(4, "tmp", [P, 4, 2, T])
        GH = at(5, "GH", [P, FC, T], F32R)
        GL = at(5, "GL", [P, FC, T], F32R, plus=4 * FC * T)
        modraw = at(5, "modraw", [P, SLOTS, D], plus=8 * FC * T)
        cond = at(5, "cond", [P, D], plus=8 * FC * T + 16 * D)
        upad = at(5, "upad", [P, DC, PAD + T])
        cv = at(7, "cv", [P, DC, T])
        diags = at(8, "diags", [P, 2, PE_TAPS, P])
        PH = at(5, "PH", [P, DC, T], F32R)
        PL = at(6, "PL", [P, DC, T], F32R)
        K = at(7, "K", [P, DC, T])
        Q = at(8, "Q", [P, DC, T])
        V = at(9, "V", [P, DC, T])
        VT = at(10, "VT", [P, 2, D])
        bias = at(11, "bias", [P, HEADS, T])
        biasrev = at(12, "biasrev", [P, HEADS, T])
        ss = at(2, "ss", [P, 2, 2, T])
        pr = at(2, "pr", [P, 2, 2, T], plus=4096)
        aa = at(3, "aa", [P, 2, T])
        aT = at(3, "aT", [P, 2, T], plus=2048)
        O = at(4, "O", [P, HEADS, T])
        H = HT
        XX = at(0, "XX", [P, DC, T])
        RH2 = at(4, "RH2", [P, DC, T], F32R)
        RL2 = at(5, "RL2", [P, DC, T], F32R)
        xs = at(6, "xs", [P, DC, T]), at(7, "xs_a", [P, DC, T]), at(8, "xs_g", [P, DC, T])
        l1 = at(10, "l1", [P, DC, 2 * LORA + 2 * P])
        l2 = at(12, "l2", [P, 3, D])
        R_ = at(6, "R_", [P, DC, T])
        K_ = at(7, "K_", [P, DC, T])
        V_ = at(8, "V_", [P, DC, T])
        W_ = at(9, "W_", [P, DC, T])
        A_ = at(10, "A_", [P, DC, T])
        G_ = at(11, "G_", [P, DC, T])
        cum = at(12, "cum", [P, 2 * DC, P + 1])
        E1 = at(9, "E1", [P, 2 * DC, P + 1])
        E2 = at(12, "E2", [P, 2 * DC, P + 1])
        KK = at(1, "KK", [P, DC, T])
        BON = at(0, "BON", [P, DC, T])
        AR = at(2, "AR", [P, DC, 2, 2, P])
        Bt_ = at(4, "Bt_", [P, DC, T])
        Kt_ = at(5, "Kt_", [P, DC, T])
        VR = at(6, "VR", [P, 2, D])
        Btok = at(7, "Btok", [P, 2, D])
        SZ = at(8, "SZ", [P, RH, RN])
        Zs = at(8, "Zs", [P, 2, 4 * RN], plus=4096)
        Us = at(8, "Us", [P, 2, 4 * RN], plus=6144)
        Yc = at(1, "Yc", [P, DC, T])
        AT = at(9, "AT", [P, 4, 4, P])
        Tm = at(10, "Tm", [P, 4, 4, P])
        TT = at(12, "TT", [P, 4, 4, P])
        apb = at(13, "apb", [P, 2, 4, P])
        half = 2 * 4 * UW
        Xs = nc.alloc_sbuf_tensor_at("Xs", [P, 2, 4, P], F32, offset=hi_at + half)
        ML = nc.alloc_sbuf_tensor_at("ML", [P, 2, 4, P], F32, offset=hi_at + half + 4096)
        apk = nc.alloc_sbuf_tensor_at("apk", [P, 2, 4, 2 * P], F32, offset=lo_at + half)
        GQ = at(9, "GQ", [P, DC, T])
        Us_ = at(5, "Us_", [P, DC, T])
        Vs_ = at(6, "Vs_", [P, DC, T])
        VNT = at(7, "VNT", [P, 2, DC, P])
        wsr = at(8, "wsr", [P, DC, P])
        wsT = at(8, "wsT", [P, DC, P], plus=4096)
        bsb = at(9, "bsb", [P, DC, P])

        PS = [ctx.enter_context(nc.psum_tensor(f"ps{n}", [P, 512], F32)) for n in range(8)]
        STAT = PS[4]

        def col(name, n=0):
            return par_sb[:, COL[name] + n:COL[name] + n + 1]

        def cols(name, n, m):
            return par_sb[:, COL[name] + n:COL[name] + n + m]

        def const(name, width=P):
            return con_sb[:, CCOL[name]:CCOL[name] + width]

        ident, ones, heads_ones = const("ident"), const("ones"), const("heads")

        raw_landed = [S(f"raw_landed{s}") for s in range(SLOTS)]
        mod_landed = [S(f"mod_landed{s}") for s in range(SLOTS)]
        hi_made, lo_made = S("hi_made"), S("lo_made")
        mm_done, evac_done = S("mm_done"), S("evac_done")
        mod_done = S("mod_done")
        par_landed, con_landed, x_landed = S("par_landed"), S("con_landed"), S("x_landed")
        operand_ready = S("operand_ready")

        ready_at, n = {}, 0
        for name in ("conv_up", "conv_down", "ffn0_up", "att_v", "att_q", "att_out", "ffn1_up", "rw_r", "rw_k",
                     "rw_v", "rw_out", "glu0_up", "sgu_v", "sgu_out", "glu1_up"):
            ready_at[name] = n
            n += DC
        ready_at["att_k"], ready_at["sgu_u"] = ready_at["att_v"], ready_at["sgu_v"]
        UP = ["ffn0_up", "ffn1_up", "glu0_up", "glu1_up"]
        for k, name in enumerate(("ffn0_down", "ffn1_down", "glu0_down", "glu1_down")):
            ready_at[name] = FC * k

        block = ctx.enter_context(nc.Block())

        def wait(eng, sem, value):
            if isinstance(value, int) and value <= 0:
                return
            eng.wait_ge(sem, value)

        def bodies(eng, name, body, peel_first=False, peel_last=False):
            n = COUNT[name] // SLOTS
            a, b = int(peel_first), n - int(peel_last)
            for i in range(min(a, n)):
                body(i, i == n - 1)
            if b - a > 1:
                with eng.Fori(a, b) as i:
                    body(i, False)
            elif b - a == 1:
                body(a, a == n - 1)
            if b < n and b >= a:
                body(b, True)

        def next_tiles(name):
            k = NAMES.index(name) + 1
            return TILES[NAMES[k]] if k < len(NAMES) else None

        class Chain:

            def __init__(self, eng, sem):
                self.eng, self.sem, self.n = eng, sem, 0

            def add(self, ins):
                ins.then_inc(self.sem, 1)
                self.n += 1

            def sync(self, but=0):
                self.eng.wait_ge(self.sem, self.n - but)

            def link(self, ins):
                self.add(ins)
                self.sync()

        @block.sync
        def _(sp):
            sp.dma_start(cond[:], crow.to_broadcast([P, D])).then_inc(S("c_landed"), 16)

            def load_mod(m, s, depth):
                wait(sp, mod_done, m - (depth - 1))
                sp.dma_start(modraw[:, s], wmod[ds(m, 1)].rearrange("a p n -> p (a n)")).then_inc(mod_landed[s], 16)

            def load_unit(name, i, r):
                kt = TILES[name]
                src = w8 if kt == KT else w11
                wait(sp, lo_made, START[name] - 3 + r + 4 * i)
                sp.dma_start(raw[:, r, 0:kt * P], src[ds(OWN[name] + 4 * i + r, 1)].rearrange("a p n -> p (a n)")
                             ).then_inc(raw_landed[r], 16)

            def load_riders(name, i, r):
                if name in RIDES and not (name == "conv_down" and i):
                    for m, s, _ in riders(name, i, r):
                        load_mod(m, s, len(RIDES[name][2]))

            def distance_biases():
                sp.wait_ge(S("bias_rows"), 1)
                sp.dma_start(scratch, xt[0:HEADS].rearrange("p a t -> p (a t)")[:, 0:384]).then_inc(S("rows_stored"), 16)
                sp.wait_ge(S("rows_stored"), 16)
                sp.wait_ge(mod_done, 96)
                skewed = bass.AP(tensor=scratch.tensor, offset=0, ap=[[1, P], [384, HEADS], [1, T]])
                sp.dma_start(biasrev[:], skewed).then_inc(S("bias_landed"), 16)

            def lora_weights():
                sp.wait_ge(evac_done, START["rw_r"])
                sp.dma_start(l1[:], lora_in.rearrange("p (c n) -> p c n", c=DC)).then_inc(S("lora_landed"), 16)
                sp.dma_start(l2[:], lora_out.rearrange("p (c n) -> p c n", c=3)).then_inc(S("lora_landed"), 16)

            def gating_weights():
                sp.wait_ge(evac_done, START["sgu_v"])
                sp.dma_start(wsr[:], sgu_ws.rearrange("p (g j) -> p g j", g=DC)).then_inc(S("sgu_landed"), 16)
                sp.dma_start(bsb[:].rearrange("p g i -> p (g i)"), sgu_bs.to_broadcast([P, D])
                             ).then_inc(S("sgu_landed"), 16)

            after_four = {"att_q": distance_biases, "rw_r": lora_weights,
                          "sgu_v": gating_weights}
            for m in range(16):
                load_mod(m, m % 4, SLOTS)
                if m == 3:
                    sp.dma_start(par_sb[:], par).then_inc(par_landed, 16)
                    sp.dma_start(X[:], xin.rearrange("p (c t) -> p c t", c=DC)).then_inc(x_landed, 16)
                if m == 7:
                    sp.dma_start(con_sb[:], con).then_inc(con_landed, 16)
                    sp.dma_start(small[0:32, 16:24], relb).then_inc(con_landed, 16)

            def body(name, i):
                for r in range(SLOTS):
                    load_unit(name, i, r)
                    if r == SLOTS - 1:
                        rides = name, i, 0
                    elif isinstance(i, int) and i == 0:
                        before = NAMES[max(NAMES.index(name) - 1, 0)]
                        rides = before, COUNT[before] // SLOTS - 1, r + 1
                    else:
                        rides = name, i - 1, r + 1
                    if rides[0] != name or r == SLOTS - 1 or not isinstance(i, int) or i:
                        load_riders(*rides)

            for name in NAMES:
                if name in after_four:
                    body(name, 0)
                    after_four[name]()
                    body(name, 1)
                else:
                    bodies(sp, name, lambda i, last: body(name, i), peel_first=True)
            for c in range(DC):
                sp.wait_ge(S("x_ready"), 7 * DC + c + 1)
                sp.dma_start(out[:, c * T:(c + 1) * T], X[:, c]).then_inc(S("stored"), 16)
            sp.wait_ge(S("stored"), 16 * DC)

        @block.tensor
        def _(pe):
            def early_taps(c, q):
                pe.wait_ge(S("diags_made"), c + 1)
                pe.wait_ge(evac_done, 2 * c + 2)
                wait(pe, S("cv_ready"), c - 1)
                for j in range(PE_TAPS):
                    ins = pe.matmul(PS[5 + 2 * q][:, 0:T], diags[:, q, j],
                                    upad[:].rearrange("p c t -> p (c t)")[:, ds((PAD + T) * c + j, T)],
                                    start=(j == 0), stop=(j == PE_TAPS - 1))
                ins.then_inc(S("taps_done"), 1)

            def between_conv_units(i, r):
                if r % 2 == 0 and not (isinstance(i, int) and 2 * i + r // 2 == 0):
                    early_taps(2 * i + (r // 2 - 1), (r // 2 + 1) % 2)

            def layer(name, oh, ol, between=None):
                kt, start = TILES[name], START[name]
                down = kt == KT_DOWN

                def body(i, last):
                    for r in range(SLOTS):
                        u = start + 4 * i + r
                        k0 = kt * (r % 2) if down else 0
                        bank = PS[r - r % 2 if down else r]
                        pe.wait_ge(lo_made, u + 1)
                        wait(pe, evac_done, u - 3)
                        for k in range(kt):
                            if r == 0 or (down and r == 1):
                                pe.wait_ge(S("hidden_split") if down else operand_ready, ready_at[name] + k0 + k + 1)
                            w = slice(k * P, (k + 1) * P)
                            first = k == 0 and (not down or r % 2 == 0)
                            final = k == kt - 1 and (not down or r % 2 == 1)
                            pe.matmul(bank[:, 0:T], lo[:, r, w], oh[:, k0 + k], start=first, stop=False)
                            pe.matmul(bank[:, 0:T], hi[:, r, w], ol[:, k0 + k], start=False, stop=False)
                            ins = pe.matmul(bank[:, 0:T], hi[:, r, w], oh[:, k0 + k], start=False, stop=final)
                        ins.then_inc(mm_done, 1)
                        if between:
                            between(i, r)
                bodies(pe, name, body, peel_first=(start == 0))

            def sum_chunks(ready, base, src, columns, done):
                for c in range(DC):
                    pe.wait_ge(ready, base + c + 1)
                    ins = pe.matmul(STAT[:, columns:columns + T], ones, src[:, c], start=(c == 0), stop=(c == DC - 1))
                ins.then_inc(done, 1)

            def norm(n):
                sum_chunks(S("xsq_ready"), DC * n, SQ, T, S("xstat_done"))

            def residual(n):
                sum_chunks(S("ysq_ready"), DC * n, SQ, 0, S("ystat_done"))

            pe.wait_ge(con_landed, 32)
            norm(0)
            pe.matmul(PS[6][0:HEADS, 0:384], small[0:32, 16:24], con_sb[0:32, CCOL["bucket"]:CCOL["bucket"] + 384],
                      start=True, stop=True).then_inc(S("rows_done"), 1)
            layer("conv_up", OH, OL, between_conv_units)
            early_taps(DC - 1, 1)
            for c in range(DC):
                pe.wait_ge(S("cv_ready"), c + 1)
                ins = pe.matmul(STAT[:, 0:T], ones, cv[:, c], start=(c == 0), stop=(c == DC - 1))
            ins.then_inc(S("cv_sum"), 1)
            for c in range(DC):
                pe.wait_ge(S("cvsq_ready"), c + 1)
                ins = pe.matmul(PS[6][:, 0:T], ones, SQ[:, c], start=(c == 0), stop=(c == DC - 1))
            ins.then_inc(S("cv_var"), 1)
            layer("conv_down", OH, OL)
            residual(0)
            norm(1)
            layer("ffn0_up", OH, OL)
            layer("ffn0_down", GH, GL)
            residual(1)
            norm(2)
            layer("att_v", OH, OL)
            layer("att_k", OH, OL)

            def transposes(count, src, banks, copied, done):
                for g in range(count):
                    wait(pe, copied, g - len(banks) + 1)
                    for q in range(4):
                        ins = pe.transpose(PS[banks[g % len(banks)]][:, q * P:(q + 1) * P], src(g, q), ident)
                    ins.then_inc(done, 1)

            pe.wait_ge(evac_done, START["att_k"])
            transposes(4, lambda g, q: V[:, 4 * (g % 2) + q, (g // 2) * P:(g // 2 + 1) * P], (6, 7),
                       S("vt_copied"), S("vt_done"))
            layer("att_q", PH, PL)
            pe.wait_ge(evac_done, START["att_out"])
            pe.wait_ge(S("vt_copied"), 4)
            pe.matmul(PS[5][:, 0:2], ones, small[:, 2:4], start=True, stop=True).then_inc(S("lam_sum"), 1)
            NA = 2 * HEADS
            for n in range(NA + 2):
                if n < NA:
                    h, qb = n // 2, n % 2
                    nk = P * (qb + 1)
                    wait(pe, S("att_scaled"), 2 * n - 2)
                    for c in range(2):
                        rows = slice(HEAD_DIM * c, HEAD_DIM * (c + 1))
                        pe.matmul(PS[2 * (n % 2) + c][:, 0:nk], Q[rows, h, qb * P:(qb + 1) * P], K[rows, h, 0:nk],
                                  start=True, stop=True).then_inc(S("att_scores"), 1)
                if 1 <= n <= NA:
                    m = n - 1
                    pe.wait_ge(S("att_probs"), m + 1)
                    if m == 1:
                        pe.wait_ge(S("lam_ready"), 1)
                    wait(pe, S("aT_copied"), m - 1)
                    for kb in range(m % 2 + 1):
                        ins = pe.transpose(PS[4 + m % 2][:, kb * P:(kb + 1) * P], aa[:, m % 2, kb * P:(kb + 1) * P], ident)
                    ins.then_inc(S("aT_done"), 1)
                if n >= 2:
                    m = n - 2
                    pe.wait_ge(S("aT_copied"), m + 1)
                    wait(pe, S("o_copied"), m - 1)
                    for kb in range(m % 2 + 1):
                        ins = pe.matmul(PS[6 + m % 2][:, 0:P], VT[:, kb, (m // 2) * P:(m // 2 + 1) * P],
                                        aT[:, m % 2, kb * P:(kb + 1) * P], start=(kb == 0), stop=(kb == m % 2))
                    ins.then_inc(S("pv_done"), 1)
            for g in range(4):
                pe.wait_ge(S("osq_ready"), g + 1)
                pe.matmul(PS[g][:, :], ones, SQ[:, 2 * g:2 * g + 2].rearrange("p c t -> p (c t)"),
                          start=True, stop=True).then_inc(S("ostat_done"), 1)
            layer("att_out", OH, OL)
            residual(2)
            norm(3)
            layer("ffn1_up", OH, OL)
            layer("ffn1_down", GH, GL)
            residual(3)
            norm(4)

            pe.wait_ge(S("lora_landed"), 32)
            for j, (c0, width, bank, p0) in enumerate([(0, LORA, 0, 0), (LORA, LORA, 1, LORA), (2 * LORA, P, 2, 0),
                                                       (2 * LORA + P, P, 3, 0)]):
                src = min(j, 2)
                for k in range(DC):
                    pe.wait_ge(S("xs_ready"), DC * src + k + 1)
                    ins = pe.matmul(PS[bank][p0:p0 + width, 0:T], l1[:, k, c0:c0 + width], xs[src][:, k],
                                    start=(k == 0), stop=(k == DC - 1))
                ins.then_inc(S("lora1_done"), 1)
            for j in range(3 * DC):
                b, c = divmod(j, DC)
                bank = PS[4 + j % 4]
                pe.wait_ge(S("lora1_used"), [1, 2, 4][b])
                wait(pe, S("lora2_used"), j - 3)
                if b == 0:
                    ins = pe.matmul(bank[:, 0:T], l2[0:LORA, 0, c * P:(c + 1) * P], root[0:LORA, 0], start=True, stop=True)
                elif b == 1:
                    ins = pe.matmul(bank[:, 0:T], l2[LORA:P, 0, c * P:(c + 1) * P], root[LORA:P, 0], start=True, stop=True)
                else:
                    pe.matmul(bank[:, 0:T], l2[:, 1, c * P:(c + 1) * P], root[:, 1], start=True, stop=False)
                    ins = pe.matmul(bank[:, 0:T], l2[:, 2, c * P:(c + 1) * P], inv[:, 0], start=False, stop=True)
                ins.then_inc(S("lora2_done"), 1)
            layer("rw_r", OH, OL)
            layer("rw_k", RH2, RL2)
            layer("rw_v", OH, OL)
            pe.wait_ge(S("lora2_used"), 3 * DC)
            for g in range(4):
                pe.wait_ge(S("kksq_ready"), g + 1)
                pe.matmul(PS[4 + g][:, :], heads_ones, BON[:, 2 * g:2 * g + 2].rearrange("p c t -> p (c t)"),
                          start=True, stop=True).then_inc(S("kkstat_done"), 1)
            for g in range(4):
                pe.wait_ge(S("bp_ready"), 2 * g + 2)
                pe.matmul(PS[4 + g][:, :], heads_ones, BON[:, 2 * g:2 * g + 2].rearrange("p c t -> p (c t)"),
                          start=True, stop=True).then_inc(S("bpsum_done"), 1)
            pe.wait_ge(evac_done, START["rw_out"])

            def rw_src(g, q):
                if g < 4:
                    return V_[:, 4 * (g % 2) + q, (g // 2) * P:(g // 2 + 1) * P]
                return (Bt_ if g < 6 else Kt_)[:, 4 * (g % 2) + q, 0:P]

            pe.wait_ge(S("rw_tilde"), 1)
            transposes(8, rw_src, (0, 1, 2, 3), S("rwt_copied"), S("rwt_done"))
            pe.wait_ge(S("bon_ready"), 4)
            pe.wait_ge(S("rwt_copied"), 8)

            for tb in range(2):
                tok = slice(tb * P, (tb + 1) * P)
                wait(pe, S("yc_copied"), 4 * tb)
                wait(pe, S("state_made"), 4 * tb)
                for b in range(4):
                    n = 4 * tb + b
                    rows = slice(RN * (b % 2), RN * (b % 2 + 1))
                    wait(pe, S("at_made"), n - 1)
                    for q in range(4):
                        c = 4 * (b // 2) + q
                        ins = pe.matmul(PS[6 + b % 2][:, q * P:(q + 1) * P], Bt_[rows, c, tok], AR[rows, c, tb, 0],
                                        start=True, stop=True)
                    ins.then_inc(S("at_done"), 1)
                for b in range(4):
                    n = 4 * tb + b
                    pe.wait_ge(S("tt0_made"), n + 1)
                    wait(pe, S("t0_copied"), n - 1)
                    for q in range(4):
                        ins = pe.transpose(PS[4 + b % 2][:, q * P:(q + 1) * P], TT[:, b, q], ident)
                    ins.then_inc(S("t0_done"), 1)

                def x_part(n, b):
                    pe.wait_ge(S("ml_made"), n + 1)
                    if isinstance(n, int) and n < 4 + 24 * tb:
                        pe.wait_ge(S("t0_copied"), 4 * tb + b + 1)
                    wait(pe, S("t_added"), n - 3 if not (isinstance(n, int) and n < 4 + 24 * tb) else 0)
                    wait(pe, S("x_copied"), n - 1)
                    for q in range(4):
                        ins = pe.matmul(PS[b % 2][:, q * P:(q + 1) * P], ML[:, b % 2, q], Tm[:, b, q], start=True, stop=True)
                    ins.then_inc(S("x_done"), 1)

                def tx_part(n, b):
                    pe.wait_ge(S("x_copied"), n + 1)
                    wait(pe, S("tt_copied"), n - 3 if not (isinstance(n, int) and n < 4 + 24 * tb) else 0)
                    wait(pe, S("t_added"), n - 1)
                    for q in range(4):
                        ins = pe.matmul(PS[2 + b % 2][:, q * P:(q + 1) * P], TT[:, b, q], Xs[:, b % 2, q], start=True, stop=True)
                    ins.then_inc(S("tx_done"), 1)

                def tr_part(n, b):
                    pe.wait_ge(S("t_added"), n + 1)
                    wait(pe, S("tt_copied"), n - 1)
                    for q in range(4):
                        ins = pe.transpose(PS[4 + b % 2][:, q * P:(q + 1) * P], Tm[:, b, q], ident)
                    ins.then_inc(S("tr_done"), 1)

                n0 = 24 * tb
                for b in range(4):
                    x_part(n0 + b, b)
                    if b >= 1:
                        tx_part(n0 + b - 1, b - 1)
                    if b >= 2:
                        tr_part(n0 + b - 2, b - 2)
                with pe.Fori(1, 6) as i:
                    for b in range(4):
                        x_part(4 * i + (n0 + b), b)
                        tx_part(4 * i + (n0 + b - 1), (b - 1) % 4)
                        tr_part(4 * i + (n0 + b - 2), (b - 2) % 4)
                tx_part(n0 + 23, 3)
                tr_part(n0 + 22, 2)
                tr_part(n0 + 23, 3)

                def gram(b):
                    n = 4 * tb + b
                    rows = slice(RN * (b % 2), RN * (b % 2 + 1))
                    wait(pe, S("apb_made"), n)
                    for q in range(4):
                        c = 4 * (b // 2) + q
                        pe.matmul(PS[q // 2][:, (q % 2) * T:(q % 2 + 1) * T], Kt_[rows, c, tok],
                                  AR[rows, c, tb].rearrange("p a t -> p (a t)"), start=True, stop=True)
                        ins = pe.matmul(PS[2][:, q * P:(q + 1) * P], Bt_[rows, c, tok], AR[rows, c, tb, 1],
                                        start=True, stop=True)
                    ins.then_inc(S("gram_done"), 1)

                def head(b, q):
                    return 8 * (b // 2) + b % 2 + 2 * q

                pe.wait_ge(S("tt_copied"), 24 * tb + 24)
                gram(0)
                for b in range(4):
                    n = 4 * tb + b
                    pe.wait_ge(S("apb_made"), n + 1)
                    if tb == 1 and b == 0:
                        pe.wait_ge(S("state_made"), 4)
                    for q in range(4):
                        v = VR[:, tb, head(b, q) * RN:(head(b, q) + 1) * RN]
                        ins = pe.matmul(PS[3][:, q * RN:(q + 1) * RN], apk[:, b % 2, q, 0:P], v, start=True, stop=(tb == 0))
                        if tb:
                            ins = pe.matmul(PS[3][:, q * RN:(q + 1) * RN], AR[:, 4 * (b // 2) + q, 1, 0], SZ[:, head(b, q)],
                                            start=False, stop=True)
                    ins.then_inc(S("z_done"), 1)
                    if b < 3:
                        gram(b + 1)
                    pe.wait_ge(S("z_copied"), n + 1)
                    for q in range(4):
                        ins = pe.matmul(PS[4][:, q * RN:(q + 1) * RN], TT[:, b, q], Zs[:, b % 2, q * RN:(q + 1) * RN],
                                        start=True, stop=True)
                    ins.then_inc(S("u_done"), 1)
                    pe.wait_ge(S("u_copied"), n + 1)
                    wait(pe, S("yc_copied"), n - 1)
                    out_rows = slice(RN * (b % 2), RN * (b % 2 + 1))
                    for q in range(4):
                        v = VR[:, tb, head(b, q) * RN:(head(b, q) + 1) * RN]
                        dst = PS[5 + b % 2][out_rows, q * P:(q + 1) * P]
                        pe.matmul(dst, Us[:, b % 2, q * RN:(q + 1) * RN], apb[:, b % 2, q], start=True, stop=False)
                        ins = pe.matmul(dst, v, apk[:, b % 2, q, P:2 * P], start=False, stop=(tb == 0))
                        if tb:
                            ins = pe.matmul(dst, SZ[:, head(b, q)], AR[:, 4 * (b // 2) + q, 1, 1], start=False, stop=True)
                    ins.then_inc(S("yc_done"), 1)
                    if tb == 0:
                        wait(pe, S("state_made"), b)
                        for q in range(4):
                            hd = slice(head(b, q) * RN, (head(b, q) + 1) * RN)
                            dst = PS[7][out_rows, q * RN:(q + 1) * RN]
                            pe.matmul(dst, Btok[:, 0, hd], Us[:, b % 2, q * RN:(q + 1) * RN], start=True, stop=False)
                            ins = pe.matmul(dst, Btok[:, 1, hd], VR[:, 0, hd], start=False, stop=True)
                        ins.then_inc(S("state_done"), 1)
            pe.wait_ge(S("yc_copied"), 8)
            pe.wait_ge(S("apb_made"), 8)
            for g in range(4):
                pe.matmul(PS[g][:, :], heads_ones, Yc[:, 2 * g:2 * g + 2].rearrange("p c t -> p (c t)"),
                          start=True, stop=True).then_inc(S("gnsum_done"), 1)
            for g in range(4):
                pe.wait_ge(S("gnsq_ready"), g + 1)
                pe.matmul(PS[4 + g][:, :], heads_ones, GQ[:, 2 * g:2 * g + 2].rearrange("p c t -> p (c t)"),
                          start=True, stop=True).then_inc(S("gnvar_done"), 1)
            layer("rw_out", OH, OL)
            residual(4)
            norm(5)
            layer("glu0_up", OH, OL)
            layer("glu0_down", GH, GL)
            residual(5)
            norm(6)
            layer("sgu_v", OH, OL)
            pe.wait_ge(S("sgu_landed"), 32)
            transposes(2, lambda g, q: wsr[:, 4 * g + q], (6, 7), S("ws_copied"), S("ws_done"))
            layer("sgu_u", OH, OL)
            for c in range(DC):
                ins = pe.matmul(STAT[:, 0:T], ones, Vs_[:, c], start=(c == 0), stop=(c == DC - 1))
            ins.then_inc(S("sv_sum"), 1)
            for c in range(DC):
                pe.wait_ge(S("svsq_ready"), c + 1)
                ins = pe.matmul(PS[6][:, 0:T], ones, SQ[:, c], start=(c == 0), stop=(c == DC - 1))
            ins.then_inc(S("sv_var"), 1)
            pe.wait_ge(S("ws_copied"), 2)
            pe.wait_ge(S("vn_ready"), DC)
            transposes(4, lambda g, q: Vs_[:, 4 * (g % 2) + q, (g // 2) * P:(g // 2 + 1) * P], (6, 7),
                       S("vnt_copied"), S("vnt_done"))
            pe.wait_ge(S("vnt_copied"), 4)
            pe.wait_ge(S("wsT_ready"), 1)
            for g in range(DC):
                wait(pe, S("sgu_used"), g - 1)
                for n in range(2):
                    ins = pe.matmul(PS[6 + g % 2][:, n * P:(n + 1) * P], VNT[:, n, g], wsT[:, g], start=True, stop=True)
                ins.then_inc(S("spatial_done"), 1)
            layer("sgu_out", OH, OL)
            residual(6)
            norm(7)
            layer("glu1_up", OH, OL)
            layer("glu1_down", GH, GL)
            residual(7)

        @block.scalar
        def _(act):
            def weights_hi(name, i, r, kt):
                u = START[name] + 4 * i + r + LEAD
                s = (r + LEAD) % SLOTS
                act.wait_ge(raw_landed[s], 16 * (START[name] // 4 + (r + LEAD) // SLOTS + 1) + 16 * i)
                wait(act, mm_done, u - 3)
                act.activation(hi[:, s, 0:kt * P], raw[:, s, 0:kt * P], ACT.Copy).then_inc(hi_made, 1)

            def mod_sum(m, s, n):
                act.wait_ge(S("mod_product"), n + 1)
                act.activation(modraw[:, s], modraw[:, s], ACT.Copy, accum_out=mod_sums[:, ds(m, 1)]).then_inc(mod_done, 1)

            def layer(name, evacuate, peel_first=False):
                start, kt, nxt = START[name], TILES[name], next_tiles(name)

                def body(i, last):
                    for r in range(SLOTS):
                        if not (last and r >= LEAD):
                            weights_hi(name, i, r, kt)
                        elif nxt:
                            weights_hi(name, i, r, nxt)
                        evacuate(i, r, start + 4 * i + r)
                        if name in SHARED:
                            for m, s, _ in riders(name, i, r):
                                mod_sum(m, s, m - SHARED[name])
                bodies(act, name, body, peel_first=peel_first or start == 0, peel_last=(nxt != kt or start == 0))

            def copy_out(dst, func=ACT.Copy, b=None):
                def evacuate(i, r, u):
                    act.wait_ge(mm_done, u + 1)
                    c = 4 * i + r
                    o = dst[:].rearrange("p c t -> p (c t)")[:, ds(T * c, T)]
                    if b is None:
                        ins = act.activation(o, PS[r][:, 0:T], func)
                    else:
                        ins = act.activation(o, PS[r][:, 0:T], func, bias=par_sb[:, ds(COL[b[0]] + b[1] + c, 1)])
                    ins.then_inc(evac_done, 1)
                return evacuate

            flatY, flatSQ = (x[:].rearrange("p c t -> p (c t)") for x in (Y, SQ))

            def with_square(down, biased=False):
                def evacuate(i, r, u):
                    if down and r % 2 == 0:
                        return
                    act.wait_ge(mm_done, u + 1)
                    c = 2 * i + r // 2 if down else 4 * i + r
                    src = PS[r - 1 if down else r][:, 0:T]
                    if biased:
                        b = par_sb[:, ds(COL["cm_b2"] + c, 1)]
                        act.activation(flatSQ[:, ds(T * c, T)], src, ACT.Square, bias=b).then_inc(S("ysq_ready"), 1)
                        act.activation(flatY[:, ds(T * c, T)], src, ACT.Identity, bias=b).then_inc(evac_done, 1)
                    else:
                        act.activation(flatSQ[:, ds(T * c, T)], src, ACT.Square).then_inc(S("ysq_ready"), 1)
                        act.activation(flatY[:, ds(T * c, T)], src, ACT.Copy).then_inc(evac_done, 2 if down else 1)
                return evacuate

            def take_root(k, ready, count, done):
                act.wait_ge(ready, count)
                act.activation(root[:, k], inv[:, k], ACT.Sqrt).then_inc(done, 1)

            def residual(n):
                take_root(0, S("yinv_ready"), n + 1, S("yroot_ready"))

            def norm(n, shifts=()):
                for c in range(DC):
                    if n:
                        act.wait_ge(S("x_ready"), DC * (n - 1) + c + 1)
                    act.activation(SQ[:, c], X[:, c], ACT.Square).then_inc(S("xsq_ready"), 1)
                take_root(1, S("xinv_ready"), n + 1, S("xroot_ready"))
                for dst, shift, base in shifts:
                    for c in range(DC):
                        act.wait_ge(S("ht_ready"), base + c + 1)
                        if shift is None:
                            ins = act.activation(dst[:, c], HT[:, c], ACT.Copy)
                        else:
                            ins = act.activation(dst[:, c], HT[:, c], ACT.Identity, bias=mods[:, shift + c:shift + c + 1])
                        ins.then_inc(S("oh_ready"), 1)

            pair0 = {n: FC * k for k, n in enumerate(UP)}
            flatpar = par_sb

            def conv_ffn_up(name, l):
                def evacuate(i, r, u):
                    q, kind = r // 2, r % 2
                    pair = pair0[name] + 2 * i + q
                    w = COL["ffn_dw"] + (3 * l + 2) * 2 * FC + kind * FC + 2 * i + q
                    b = COL["ffn_dwb"] + l * 2 * FC + kind * FC + 2 * i + q
                    act.wait_ge(mm_done, u + 1)
                    wait(act, S("prod_made"), pair - 1)
                    act.activation(tmp[:, kind, q], PS[r][:, 0:T], ACT.Identity, scale=flatpar[:, ds(w, 1)],
                                   bias=flatpar[:, ds(b, 1)]).then_inc(S("tap2_made"), 1)
                    if kind == 1:
                        act.wait_ge(evac_done, u)
                        act.activation(tmp[:, 2, q], tmp[:, 0, q], ACT.Silu).then_inc(S("silu_made"), 1)
                act.preload_act_table(ACT.Silu)
                if name in RIDES:
                    act.wait_ge(mod_done, RIDES[name][0])
                layer(name, evacuate, peel_first=(l == 0))

            def glu_up(name):
                def evacuate(i, r, u):
                    q = r // 2
                    pair = pair0[name] + 2 * i + q
                    if r % 2 == 0:
                        act.wait_ge(mm_done, u + 1)
                        act.wait_ge(S("prod_made"), pair - 1)
                        act.activation(tmp[:, 2, q], PS[r][:, 0:T], ACT.Silu).then_inc(S("silu_made"), 1)
                act.preload_act_table(ACT.Silu)
                layer(name, evacuate)

            act.wait_ge(S("c_landed"), 16)
            act.activation(cond[:], cond[:], ACT.Silu).then_inc(S("cond_ready"), 1)
            act.wait_ge(par_landed, 16)
            act.wait_ge(x_landed, 16)
            for s in range(LEAD):
                act.wait_ge(raw_landed[s], 16)
                act.activation(hi[:, s, 0:KT * P], raw[:, s, 0:KT * P], ACT.Copy).then_inc(hi_made, 1)
            norm(0, [(OH, 0, 0)])

            def diagonals(c, q):
                wait(act, S("taps_done"), c - 1)
                for j in range(PE_TAPS):
                    ins = act.activation(diags[:, q, j], ident, ACT.Copy, scale=par_sb[:, ds(COL["cm_dw"] + j * DC + c, 1)])
                ins.then_inc(S("diags_made"), 1)

            act.wait_ge(con_landed, 32)
            diagonals(0, 0)

            def conv_up(i, r, u):
                if r % 2:
                    act.wait_ge(mm_done, u + 1)
                    c = 2 * i + r // 2
                    wait(act, evac_done, START["conv_up"] + 4 * i + r - 3)
                    act.activation(tmp[:, 0, r // 2], PS[r][:, 0:T], ACT.Sigmoid,
                                   bias=par_sb[:, ds(COL["cm_b1"] + DC + c, 1)]).then_inc(S("glu_gate"), 1)
                    if not (isinstance(i, int) and c == DC - 1):
                        diagonals(c + 1, (r // 2 + 1) % 2)
            act.preload_act_table(ACT.Sigmoid)
            act.wait_ge(mod_done, MOD_START)
            layer("conv_up", conv_up)
            for c in range(DC):
                act.wait_ge(S("cv_centred"), c + 1)
                act.activation(SQ[:, c], cv[:, c], ACT.Square).then_inc(S("cvsq_ready"), 1)
            take_root(0, S("cvinv_ready"), 1, S("cvroot_ready"))
            for c in range(DC):
                act.wait_ge(S("cv_scaled"), c + 1)
                act.activation(Y[:, c], cv[:, c], ACT.Silu, bias=col("cm_ln_b", c)).then_inc(S("cv_silu"), 1)
            layer("conv_down", with_square(False, True))
            residual(0)
            norm(1, [(OH, 24, DC)])
            conv_ffn_up("ffn0_up", 0)
            layer("ffn0_down", with_square(True))
            residual(1)
            norm(2, [(OH, None, 2 * DC), (PH, 48, 3 * DC)])
            layer("att_v", copy_out(V))
            layer("att_k", copy_out(K))
            layer("att_q", copy_out(Q))
            act.wait_ge(S("lam_sum"), 1)
            act.activation(small[:, 4:6], PS[5][:, 0:2], ACT.Exp).then_inc(S("lam_exp"), 1)
            NA = 2 * HEADS
            for n in range(NA + 2):
                if n < NA:
                    nk, s = P * (n % 2 + 1), n % 2
                    act.wait_ge(S("att_negmax"), n + 1)
                    wait(act, S("att_probs"), n - 1)
                    for c in range(2):
                        act.activation(pr[:, s, c, 0:nk], ss[:, s, c, 0:nk], ACT.Exp,
                                       bias=small[:, 8 + 2 * s + c:9 + 2 * s + c],
                                       accum_out=small[:, 12 + 2 * s + c:13 + 2 * s + c]).then_inc(S("att_exp"), 1)
                if 1 <= n <= NA:
                    m = n - 1
                    nk = P * (m % 2 + 1)
                    act.wait_ge(S("aT_done"), m + 1)
                    wait(act, S("pv_done"), m - 1)
                    act.activation(aT[:, m % 2, 0:nk], PS[4 + m % 2][:, 0:nk], ACT.Copy).then_inc(S("aT_copied"), 1)
                if n >= 2:
                    m = n - 2
                    act.wait_ge(S("pv_done"), m + 1)
                    act.activation(O[:, m // 2, (m % 2) * P:(m % 2 + 1) * P], PS[6 + m % 2][:, 0:P], ACT.Copy
                                   ).then_inc(S("o_copied"), 1)
            for g in range(4):
                act.wait_ge(S("o_copied"), 4 * g + 4)
                act.activation(SQ[:, 2 * g:2 * g + 2], O[:, 2 * g:2 * g + 2], ACT.Square).then_inc(S("osq_ready"), 1)
            for g in range(4):
                act.wait_ge(S("oinv_ready"), g + 1)
                act.activation(SQ[:, 2 * g:2 * g + 2], SQ[:, 2 * g:2 * g + 2], ACT.Sqrt).then_inc(S("oroot_ready"), 1)
            for c in range(DC):
                act.wait_ge(S("o_normed"), c + 1)
                act.activation(OH[:, c], O[:, c], ACT.Copy).then_inc(S("oh_ready"), 1)
            layer("att_out", with_square(False))
            residual(2)
            norm(3, [(OH, 48 + 24, 4 * DC)])
            conv_ffn_up("ffn1_up", 1)
            layer("ffn1_down", with_square(True))
            residual(3)
            norm(4)

            for j, dst in enumerate([OH, RH2]):
                for c in range(DC):
                    act.wait_ge(S("xt_ready"), DC * j + c + 1)
                    act.activation(dst[:, c], xt[:, c % 4], ACT.Copy).then_inc(S("xh_ready"), 1)
            act.wait_ge(S("lora1_done"), 1)
            act.activation(root[0:LORA, 0], PS[0][0:LORA, 0:T], ACT.Tanh).then_inc(S("lora1_used"), 1)
            act.wait_ge(S("lora1_done"), 2)
            act.activation(root[LORA:P, 0], PS[1][LORA:P, 0:T], ACT.Copy).then_inc(S("lora1_used"), 1)
            act.wait_ge(S("lora1_done"), 3)
            act.activation(root[:, 1], PS[2][:, 0:T], ACT.Sigmoid).then_inc(S("lora1_used"), 1)
            act.wait_ge(S("lora1_done"), 4)
            act.activation(inv[:, 0], PS[3][:, 0:T], ACT.Sigmoid).then_inc(S("lora1_used"), 1)
            for j in range(3 * DC):
                b, c = divmod(j, DC)
                act.wait_ge(S("lora2_done"), j + 1)
                src = PS[4 + j % 4][:, 0:T]
                if b == 0:
                    ins = act.activation(W_[:, c], src, ACT.Sigmoid, bias=col("w0", c))
                elif b == 1:
                    ins = act.activation(A_[:, c], src, ACT.Sigmoid, bias=col("a0", c))
                else:
                    ins = act.activation(G_[:, c], src, ACT.Copy)
                ins.then_inc(S("lora2_used"), 1)
            layer("rw_r", copy_out(R_))
            for c in range(DC):
                act.wait_ge(S("xt_ready"), 2 * DC + c + 1)
                act.activation(OH[:, c], xt[:, c % 4], ACT.Copy).then_inc(S("xh_ready"), 1)
            layer("rw_k", copy_out(K_))
            layer("rw_v", copy_out(V_))
            for g in range(4):
                act.wait_ge(S("kk_raw"), 2 * g + 2)
                act.activation(BON[:, 2 * g:2 * g + 2], KK[:, 2 * g:2 * g + 2], ACT.Square).then_inc(S("kksq_ready"), 1)
            for j in range(2 * DC):
                act.wait_ge(S("cum_ready"), 1)
                act.activation(E1[:, j], cum[:, j], ACT.Exp, scale=-KAPPA, bias=mid[:, j:j + 1]).then_inc(S("e1_ready"), 1)
            for g in range(4):
                act.wait_ge(S("kkinv_ready"), g + 1)
                act.activation(BON[:, 2 * g:2 * g + 2], BON[:, 2 * g:2 * g + 2], ACT.Sqrt).then_inc(S("kkroot_ready"), 1)
            for g in range(8):
                act.wait_ge(S("rwt_done"), g + 1)
                if g < 4:
                    dst = VR[:, g // 2, (g % 2) * 512:(g % 2 + 1) * 512]
                else:
                    dst = Btok[:, (g - 4) // 2, (g % 2) * 512:(g % 2 + 1) * 512]
                act.activation(dst, PS[g % 4][:, :], ACT.Copy).then_inc(S("rwt_copied"), 1)

            def flat(x):
                return x.rearrange("p q t -> p (q t)")

            for tb in range(2):
                for b in range(4):
                    n = 4 * tb + b
                    act.wait_ge(S("t0_done"), n + 1)
                    act.activation(flat(Tm[:, b]), PS[4 + b % 2][:, :], ACT.Copy).then_inc(S("t0_copied"), 1)
                n0 = 24 * tb

                def x_copy(n, b):
                    act.wait_ge(S("x_done"), n + 1)
                    wait(act, S("tx_done"), n - 1)
                    act.activation(flat(Xs[:, b % 2]), PS[b % 2][:, :], ACT.Copy).then_inc(S("x_copied"), 1)

                def tt_copy(n, b):
                    act.wait_ge(S("tr_done"), n + 1)
                    act.activation(flat(TT[:, b]), PS[4 + b % 2][:, :], ACT.Copy).then_inc(S("tt_copied"), 1)

                for b in range(4):
                    x_copy(n0 + b, b)
                    if b >= 2:
                        tt_copy(n0 + b - 2, b - 2)
                with act.Fori(1, 6) as i:
                    for b in range(4):
                        x_copy(4 * i + (n0 + b), b)
                        tt_copy(4 * i + (n0 + b - 2), (b - 2) % 4)
                tt_copy(n0 + 22, 2)
                tt_copy(n0 + 23, 3)
                for b in range(4):
                    n = 4 * tb + b
                    act.wait_ge(S("z_done"), n + 1)
                    wait(act, S("u_done"), n - 1)
                    act.activation(Zs[:, b % 2], PS[3][:, 0:4 * RN], ACT.Copy).then_inc(S("z_copied"), 1)
                    act.wait_ge(S("u_done"), n + 1)
                    wait(act, S("yc_done"), n - 1)
                    if tb == 0:
                        wait(act, S("state_done"), n - 1)
                    act.activation(Us[:, b % 2], PS[4][:, 0:4 * RN], ACT.Copy).then_inc(S("u_copied"), 1)
                    act.wait_ge(S("yc_done"), n + 1)
                    rows = slice(RN * (b % 2), RN * (b % 2 + 1))
                    act.activation(Yc[rows, 4 * (b // 2):4 * (b // 2) + 4, tb * P:(tb + 1) * P],
                                   PS[5 + b % 2][rows, :].rearrange("p (q t) -> p q t", q=4), ACT.Copy
                                   ).then_inc(S("yc_copied"), 1)
            for g in range(4):
                act.wait_ge(S("gn_centred"), g + 1)
                act.activation(GQ[:, 2 * g:2 * g + 2], Yc[:, 2 * g:2 * g + 2], ACT.Square).then_inc(S("gnsq_ready"), 1)
            for g in range(4):
                act.wait_ge(S("gninv_ready"), g + 1)
                act.activation(GQ[:, 2 * g:2 * g + 2], GQ[:, 2 * g:2 * g + 2], ACT.Sqrt).then_inc(S("gnroot_ready"), 1)
            for c in range(DC):
                act.wait_ge(S("yg_ready"), c + 1)
                act.activation(OH[:, c], Yc[:, c], ACT.Copy).then_inc(S("oh_ready"), 1)
            layer("rw_out", with_square(False))
            residual(4)
            norm(5, [(OH, None, 6 * DC)])
            glu_up("glu0_up")
            layer("glu0_down", with_square(True))
            residual(5)
            norm(6, [(OH, None, 7 * DC)])
            act.preload_act_table(ACT.Gelu)
            layer("sgu_v", copy_out(Vs_, ACT.Gelu, ("sgu_b_in", DC)))
            layer("sgu_u", copy_out(Us_, ACT.Gelu, ("sgu_b_in", 0)))
            for c in range(DC):
                act.wait_ge(S("sv_centred"), c + 1)
                act.activation(SQ[:, c], Vs_[:, c], ACT.Square).then_inc(S("svsq_ready"), 1)
            take_root(0, S("svinv_ready"), 1, S("svroot_ready"))
            for c in range(DC):
                act.wait_ge(S("v_scaled"), c + 1)
                act.activation(Vs_[:, c], Vs_[:, c], ACT.Identity, bias=col("sgu_ln_b", c)).then_inc(S("vn_ready"), 1)
            for g in range(4):
                act.wait_ge(S("vnt_done"), g + 1)
                act.activation(VNT[:, g // 2, 4 * (g % 2):4 * (g % 2) + 4].rearrange("p g c -> p (g c)"),
                               PS[6 + g % 2][:, :], ACT.Copy).then_inc(S("vnt_copied"), 1)
            for c in range(DC):
                act.wait_ge(S("us_ready"), c + 1)
                act.activation(OH[:, c], Us_[:, c], ACT.Copy).then_inc(S("oh_ready"), 1)
            layer("sgu_out", with_square(False))
            residual(6)
            norm(7, [(OH, None, 8 * DC)])
            glu_up("glu1_up")
            layer("glu1_down", with_square(True))
            residual(7)

        @block.vector
        def _(dve):
            chain = Chain(dve, S("dve_chain"))
            stt = dve.scalar_tensor_tensor

            def weights_lo(name, i, r, kt):
                u = START[name] + 4 * i + r + LEAD
                s = (r + LEAD) % SLOTS
                dve.wait_ge(hi_made, u + 1)
                dve.tensor_tensor(lo[:, s, 0:kt * P], raw[:, s, 0:kt * P], hi[:, s, 0:kt * P].bitcast(F32), ALU.subtract
                                  ).then_inc(lo_made, 1)

            def mod_unit(m, s, landed):
                dve.wait_ge(mod_landed[s], 16 * landed)
                stt(out=modraw[:, s], in0=modraw[:, s], scalar=1.0, in1=cond[:], op0=ALU.mult, op1=ALU.mult,
                    accum_out=mod_sums[:, ds(m, 1)]).then_inc(mod_done, 1)

            def layer(name, evacuate=None, peel_all=False, peel_first=False):
                start, kt, nxt = START[name], TILES[name], next_tiles(name)

                def body(i, last):
                    for r in range(SLOTS):
                        if not (last and r >= LEAD):
                            weights_lo(name, i, r, kt)
                        elif nxt:
                            weights_lo(name, i, r, nxt)
                        if evacuate:
                            evacuate(i, r, start + 4 * i + r)
                        if name in RIDES and name not in SHARED and not (name == "conv_down" and i):
                            for m, s, landed in riders(name, i, r):
                                mod_unit(m, s, landed)
                if peel_all:
                    for i in range(COUNT[name] // SLOTS):
                        body(i, i == COUNT[name] // SLOTS - 1)
                else:
                    bodies(dve, name, body, peel_first=peel_first, peel_last=(nxt != kt))

            def invert(src, dst, scale, eps, summed, count, done):
                dve.wait_ge(summed, count)
                chain.link(dve.tensor_scalar(dst, src, scale, eps, ALU.mult, ALU.add))
                dve.reciprocal(dst, dst).then_inc(done, 1)

            def residual(n, gain):
                invert(STAT[:, 0:T], inv[:, 0], 1 / D, EPS, S("ystat_done"), n + 1, S("yinv_ready"))
                dve.wait_ge(S("yroot_ready"), n + 1)
                for c in range(DC):
                    stt(out=Y[:, c], in0=Y[:, c], scalar=gain(c), in1=root[:, 0], op0=ALU.mult, op1=ALU.mult
                        ).then_inc(S("y_scaled"), 1)

            oh_count = [0]

            def low_part(src, h, l, c, shift=None):
                oh_count[0] += 1
                dve.wait_ge(S("oh_ready"), oh_count[0])
                if shift is None:
                    ins = dve.tensor_tensor(l[:, c], src[:, c], h[:, c].bitcast(F32), ALU.subtract)
                else:
                    ins = stt(out=l[:, c], in0=src[:, c], scalar=mods[:, shift + c:shift + c + 1],
                              in1=h[:, c].bitcast(F32), op0=ALU.add, op1=ALU.subtract)
                ins.then_inc(operand_ready, 1)

            def norm(n, uses):
                invert(STAT[:, T:2 * T], inv[:, 1], 1 / D, EPS, S("xstat_done"), n + 1, S("xinv_ready"))
                dve.wait_ge(S("xroot_ready"), n + 1)
                for k, (gain, h, l, shift) in enumerate(uses):
                    if k:
                        dve.wait_ge(operand_ready, ready_at["att_v"] + DC)
                    for c in range(DC):
                        stt(out=HT[:, c], in0=X[:, c], scalar=gain(c), in1=root[:, 1], op0=ALU.mult, op1=ALU.mult
                            ).then_inc(S("ht_ready"), 1)
                    if h is not None:
                        for c in range(DC):
                            low_part(HT, h, l, c, shift)

            def par_gain(name, n):
                return lambda c: col(name, n + c)

            def own_gain(tile, n):
                return lambda c: tile[:, n, c:c + 1]

            def modulation(first, count, done):
                dve.wait_ge(mod_done, done)
                chain.link(dve.tensor_tensor(mods[:, first:first + count], mod_sums[:, first:first + count],
                                             cols("mod_b", first, count), ALU.add))

            def scale_gain(n, which):
                l, k = divmod(n, 2)
                chain.link(stt(out=ngain[:, n], in0=mods[:, 48 * l + 8 + 24 * k:48 * l + 16 + 24 * k], scalar=1.0,
                               in1=cols("norm_g", which, DC), op0=ALU.add, op1=ALU.mult))

            def gate_gain(n, which):
                l, k = divmod(n, 2)
                chain.link(dve.tensor_tensor(rgain[:, n], mods[:, 48 * l + 16 + 24 * k:48 * l + 24 + 24 * k],
                                             cols("norm_g", which, DC), ALU.mult))

            dve.wait_ge(S("cond_ready"), 1)
            for m in range(MOD_START):
                mod_unit(m, m % SLOTS, m // SLOTS + 1)
            dve.wait_ge(par_landed, 16)
            dve.wait_ge(x_landed, 16)
            chain.link(dve.tensor_tensor(small[:, 2:3], col("lam", 0), col("lam", 1), ALU.mult))
            chain.link(dve.tensor_tensor(small[:, 3:4], col("lam", 2), col("lam", 3), ALU.mult))
            dve.memset(upad[:, :, 0:PAD], 0.0).then_inc(S("upad_zero"), 1)
            for s in range(LEAD):
                dve.wait_ge(hi_made, s + 1)
                dve.tensor_tensor(lo[:, s, 0:KT * P], raw[:, s, 0:KT * P], hi[:, s, 0:KT * P].bitcast(F32), ALU.subtract
                                  ).then_inc(lo_made, 1)
            modulation(0, 16, 16)
            scale_gain(0, 0)
            norm(0, [(own_gain(ngain, 0), OH, OL, 0)])
            dve.wait_ge(S("rows_done"), 1)
            dve.tensor_tensor(xt[0:HEADS].rearrange("p a t -> p (a t)")[:, 0:384], PS[6][0:HEADS, 0:384],
                              con_sb[0:HEADS, CCOL["future"]:CCOL["future"] + 384], ALU.add).then_inc(S("bias_rows"), 1)

            def conv_up(i, r, u):
                if r % 2 == 0:
                    return
                c = 2 * i + r // 2
                dve.wait_ge(S("glu_gate"), c + 1)
                stt(out=upad[:, c, PAD:], in0=PS[r - 1][:, 0:T], scalar=col("cm_b1", c), in1=tmp[:, 0, r // 2],
                    op0=ALU.add, op1=ALU.mult).then_inc(evac_done, 2)
                dve.wait_ge(evac_done, u + 1)
                if c == 0:
                    dve.wait_ge(S("upad_zero"), 1)
                sums = cv[:, c], tmp[:, 1, r // 2]
                first = PE_TAPS
                chain.add(dve.tensor_scalar(sums[0], upad[:, c, first:first + T], col("cm_dw", first * DC + c),
                                            col("cm_dwb", c), ALU.mult, ALU.add))
                chain.add(dve.tensor_scalar(sums[1], upad[:, c, first + 1:first + 1 + T],
                                            col("cm_dw", (first + 1) * DC + c), None, ALU.mult))
                for j in range(first + 2, TAPS):
                    to = sums[(j - first) % 2]
                    chain.sync(1)
                    chain.add(stt(out=to, in0=upad[:, c, j:j + T], scalar=col("cm_dw", j * DC + c), in1=to,
                                  op0=ALU.mult, op1=ALU.add))
                chain.sync()
                chain.link(dve.tensor_tensor(cv[:, c], cv[:, c], sums[1], ALU.add))
                dve.wait_ge(S("taps_done"), c + 1)
                dve.tensor_tensor(cv[:, c], PS[5 + 2 * (r // 2)][:, 0:T], cv[:, c], ALU.add).then_inc(S("cv_ready"), 1)

            layer("conv_up", conv_up, peel_all=True)
            dve.wait_ge(S("cv_sum"), 1)
            for c in range(DC):
                stt(out=cv[:, c], in0=STAT[:, 0:T], scalar=-1 / D, in1=cv[:, c], op0=ALU.mult, op1=ALU.add
                    ).then_inc(S("cv_centred"), 1)
            invert(PS[6][:, 0:T], inv[:, 0], 1 / D, EPS, S("cv_var"), 1, S("cvinv_ready"))
            dve.wait_ge(S("cvroot_ready"), 1)
            for c in range(DC):
                stt(out=cv[:, c], in0=cv[:, c], scalar=col("cm_ln_g", c), in1=root[:, 0], op0=ALU.mult, op1=ALU.mult
                    ).then_inc(S("cv_scaled"), 1)
            for c in range(DC):
                low_part(Y, OH, OL, c)
            modulation(16, 32, 48)
            scale_gain(1, 2 * DC)
            gate_gain(0, DC)
            gate_gain(1, 3 * DC)
            layer("conv_down", peel_all=True)
            residual(0, own_gain(rgain, 0))
            norm(1, [(own_gain(ngain, 1), OH, OL, 24)])

            pair0 = {n: FC * k for k, n in enumerate(UP)}

            def product(q, pair, a, b):
                dve.wait_ge(S("silu_made"), pair + 1)
                wait(dve, S("hidden_split"), pair - 1)
                dve.tensor_tensor(tmp[:, 3, q], a, b, ALU.mult).then_inc(S("prod_made"), 1)

            def conv_ffn_up(name, l):
                units0 = 2 * FC * l

                def evacuate(i, r, u):
                    q, kind = r // 2, r % 2
                    unit = units0 + 4 * i + r
                    t = tmp[:, kind, q]
                    w = COL["ffn_dw"] + 3 * l * 2 * FC + kind * FC + 2 * i + q
                    dve.wait_ge(S("tap2_made"), unit + 1)
                    stt(out=t[:, 1:], in0=PS[r][:, 0:T - 1], scalar=par_sb[:, ds(w + 2 * FC, 1)], in1=t[:, 1:],
                        op0=ALU.mult, op1=ALU.add).then_inc(S("tap1_made"), 1)
                    dve.wait_ge(S("tap1_made"), unit + 1)
                    stt(out=t[:, 2:], in0=PS[r][:, 0:T - 2], scalar=par_sb[:, ds(w, 1)], in1=t[:, 2:],
                        op0=ALU.mult, op1=ALU.add).then_inc(evac_done, 1)
                    if kind == 1:
                        dve.wait_ge(evac_done, u + 1)
                        product(q, pair0[name] + 2 * i + q, tmp[:, 2, q], tmp[:, 1, q])
                layer(name, evacuate, peel_first=(l == 0))

            def glu_up(name):
                def evacuate(i, r, u):
                    q = r // 2
                    if r % 2 == 0:
                        return
                    pair = pair0[name] + 2 * i + q
                    dve.wait_ge(mm_done, u + 1)
                    product(q, pair, tmp[:, 2, q], PS[r][:, 0:T])
                    dve.wait_ge(S("prod_made"), pair + 1)
                    dve.sem_inc(evac_done, 2)
                layer(name, evacuate)

            conv_ffn_up("ffn0_up", 0)
            dve.wait_ge(mod_done, 9 * DC)
            layer("ffn0_down")
            modulation(48, 24, 72)
            scale_gain(2, 4 * DC)
            gate_gain(2, 5 * DC)
            residual(1, own_gain(rgain, 1))
            norm(2, [(par_gain("kv_norm_g", 0), OH, OL, None), (own_gain(ngain, 2), PH, PL, 48)])
            layer("att_v")
            modulation(72, 24, 96)
            scale_gain(3, 6 * DC)
            gate_gain(3, 7 * DC)
            layer("att_k")
            for g in range(4):
                dve.wait_ge(S("vt_done"), g + 1)
                dve.tensor_copy(VT[:, g // 2, (g % 2) * 512:(g % 2 + 1) * 512], PS[6 + g % 2][:, :]
                                ).then_inc(S("vt_copied"), 1)
            layer("att_q")
            dve.wait_ge(S("bias_landed"), 16)
            chain.link(dve.tensor_copy(bias[:], biasrev[:, :, ::-1]))
            dve.wait_ge(S("lam_exp"), 1)
            chain.link(dve.tensor_tensor(small[:, 6:7], small[:, 5:6], small[:, 4:5], ALU.subtract))
            dve.tensor_scalar(small[:, 7:8], small[:, 6:7], -LAMBDA_INIT, None, ALU.add).then_inc(S("lam_ready"), 1)
            dve.wait_ge(S("lam_ready"), 1)
            neg_lam = small[:, 7:8]
            NA = 2 * HEADS
            rs = small[:, 24:28]
            for n in range(NA + 1):
                if n < NA:
                    h, qb, s = n // 2, n % 2, n % 2
                    nk = P * (qb + 1)
                    wait(dve, S("att_exp"), 2 * n - 2)
                    for c in range(2):
                        dve.wait_ge(S("att_scores"), 2 * n + c + 1)
                        stt(out=ss[:, s, c, 0:nk], in0=PS[2 * s + c][:, 0:nk], scalar=HEAD_DIM ** -0.5,
                            in1=bias[:, h, T - nk:T], op0=ALU.mult, op1=ALU.add).then_inc(S("att_scaled"), 1)
                    dve.wait_ge(S("att_scaled"), 2 * n + 2)
                    chain.link(dve.reduce_max(small[:, 28 + 2 * s:30 + 2 * s], ss[:, s, :, 0:nk], AX_X))
                    dve.tensor_scalar(small[:, 8 + 2 * s:10 + 2 * s], small[:, 28 + 2 * s:30 + 2 * s], -1.0, None, ALU.mult
                                      ).then_inc(S("att_negmax"), 1)
                if n >= 1:
                    m, s = n - 1, (n - 1) % 2
                    nk = P * (s + 1)
                    dve.wait_ge(S("att_exp"), 2 * m + 2)
                    chain.link(dve.reciprocal(rs[:, 2 * s:2 * s + 2], small[:, 12 + 2 * s:14 + 2 * s]))
                    chain.link(dve.tensor_tensor(rs[:, 2 * s + 1:2 * s + 2], rs[:, 2 * s + 1:2 * s + 2], neg_lam, ALU.mult))
                    wait(dve, S("aT_done"), m - 1)
                    chain.link(dve.tensor_scalar(aa[:, s, 0:nk], pr[:, s, 0, 0:nk], rs[:, 2 * s:2 * s + 1], None, ALU.mult))
                    stt(out=aa[:, s, 0:nk], in0=pr[:, s, 1, 0:nk], scalar=rs[:, 2 * s + 1:2 * s + 2], in1=aa[:, s, 0:nk],
                        op0=ALU.mult, op1=ALU.add).then_inc(S("att_probs"), 1)
            chain.link(dve.tensor_scalar(small[:, 0:1], col("subln_g"), 1.0 - LAMBDA_INIT, None, ALU.mult))
            for g in range(4):
                invert(PS[g][:, :], SQ[:, 2 * g:2 * g + 2].rearrange("p c t -> p (c t)"), 1 / P, EPS,
                       S("ostat_done"), g + 1, S("oinv_ready"))
            for c in range(DC):
                dve.wait_ge(S("oroot_ready"), c // 2 + 1)
                stt(out=O[:, c], in0=O[:, c], scalar=small[:, 0:1], in1=SQ[:, c], op0=ALU.mult, op1=ALU.mult
                    ).then_inc(S("o_normed"), 1)
            for c in range(DC):
                low_part(O, OH, OL, c)
            layer("att_out")
            residual(2, own_gain(rgain, 2))
            norm(3, [(own_gain(ngain, 3), OH, OL, 48 + 24)])
            conv_ffn_up("ffn1_up", 1)
            layer("ffn1_down")
            residual(3, own_gain(rgain, 3))
            norm(4, [(par_gain("norm_g2", 0), None, None, None)])

            def mixed(dst, j, c, sem):
                stt(out=dst, in0=XX[:, c], scalar=col("mix", DC * j + c), in1=H[:, c], op0=ALU.mult, op1=ALU.add
                    ).then_inc(sem, 1)

            def mixed_operand(j, n, h, l):
                for c in range(DC + 2):
                    if c < DC:
                        dve.wait_ge(operand_ready, ready_at["rw_r"] + DC * n + c - 3)
                        mixed(xt[:, c % 4], j, c, S("xt_ready"))
                    if c >= 2:
                        dve.wait_ge(S("xh_ready"), DC * n + c - 1)
                        dve.tensor_tensor(l[:, c - 2], xt[:, (c - 2) % 4], h[:, c - 2].bitcast(F32), ALU.subtract
                                          ).then_inc(operand_ready, 1)

            for c in range(DC):
                dve.wait_ge(S("xx_ready"), c + 1)
                mixed(xs[0][:, c], 3, c, S("xs_ready"))
            for c in range(DC):
                mixed(xs[1][:, c], 4, c, S("xs_ready"))
            for c in range(DC):
                mixed(xs[2][:, c], 5, c, S("xs_ready"))
            mixed_operand(0, 0, OH, OL)
            mixed_operand(1, 1, RH2, RL2)
            layer("rw_r")
            dve.wait_ge(mm_done, START["rw_k"])
            mixed_operand(2, 2, OH, OL)
            layer("rw_k")
            dve.wait_ge(S("lora2_used"), 3 * DC)
            chain.link(dve.memset(cum[:, :, 0:1], 0.0))
            for j in range(2 * DC):
                chain.add(dve.tensor_tensor_scan(cum[:, j, 1:P + 1], ones, W_[:, j // 2, (j % 2) * P:(j % 2 + 1) * P], 0.0,
                                                 ALU.mult, ALU.add))
            chain.sync()
            dve.tensor_scalar(mid[:], cum[:, :, P // 2], KAPPA, None, ALU.mult).then_inc(S("cum_ready"), 1)
            layer("rw_v")
            for g in range(4):
                dve.wait_ge(S("kkstat_done"), g + 1)
                b = BON[:, 2 * g:2 * g + 2].rearrange("p c t -> p (c t)")
                chain.link(dve.tensor_scalar(b, PS[4 + g][:, :], 1e-24, None, ALU.max))
                dve.reciprocal(b, b).then_inc(S("kkinv_ready"), 1)
            dve.wait_ge(S("e1_ready"), 2 * DC)
            e1, e2 = (x[:].rearrange("p j t -> p (j t)") for x in (E1, E2))
            chain.link(dve.reciprocal(e2, e1))
            chain.link(dve.tensor_tensor(dec[:], E1[:, 0::2, P], E2[:, 1::2, 0], ALU.mult))

            def blocks(x, c):
                return x[:, c].rearrange("p (b t) -> p b t", b=2)

            dve.wait_ge(S("kk_raw"), DC)
            for c in range(DC):
                chain.link(dve.tensor_scalar(xt[:, c % 4], A_[:, c], -1.0, col("k_a", c), ALU.add, ALU.mult))
                chain.link(stt(out=K_[:, c], in0=xt[:, c % 4], scalar=1.0, in1=K_[:, c], op0=ALU.add, op1=ALU.mult))
                dve.tensor_tensor(blocks(Kt_, c), blocks(K_, c), E2[:, 2 * c:2 * c + 2, 1:P + 1], ALU.mult
                                  ).then_inc(S("kt_ready"), 1)
            dve.wait_ge(S("kk_ready"), DC)
            for c in range(DC):
                chain.add(stt(out=AR[:, c, :, 0], in0=blocks(KK, c), scalar=-1.0, in1=E1[:, 2 * c:2 * c + 2, 0:P],
                              op0=ALU.mult, op1=ALU.mult))
            for c in range(DC):
                stt(out=BON[:, c], in0=R_[:, c], scalar=col("r_k", c), in1=K_[:, c], op0=ALU.mult, op1=ALU.mult
                    ).then_inc(S("bp_ready"), 1)
            dve.wait_ge(evac_done, START["rw_out"])
            for g in range(4):
                dve.wait_ge(S("bpsum_done"), g + 1)
                b = BON[:, 2 * g:2 * g + 2].rearrange("p c t -> p (c t)")
                dve.tensor_tensor(b, PS[4 + g][:, :], V_[:, 2 * g:2 * g + 2].rearrange("p c t -> p (c t)"), ALU.mult
                                  ).then_inc(S("bon_ready"), 1)
            dve.wait_ge(S("rt_ready"), 2 * DC)
            chain.sync()
            dve.wait_ge(S("bon_ready"), 4)
            dve.sem_inc(S("rw_tilde"), 1)
            dve.wait_ge(S("rwt_copied"), 4)
            chain.link(dve.memset(SZ[:], 0.0))

            def flat(x):
                return x.rearrange("p q t -> p (q t)")

            def over_heads(m):
                return m.unsqueeze(1).to_broadcast([P, 4, P])

            def state_out(b):
                rows = slice(RN * (b % 2), RN * (b % 2 + 1))
                dve.wait_ge(S("state_done"), b + 1)
                first = 8 * (b // 2) + b % 2
                dve.tensor_tensor(SZ[rows, first:first + 7:2], PS[7][rows, 0:4 * RN].rearrange("p (q i) -> p q i", q=4),
                                  dec[rows, 4 * (b // 2):4 * (b // 2) + 4].unsqueeze(2).to_broadcast([RN, 4, RN]),
                                  ALU.mult).then_inc(S("state_made"), 1)

            for tb in range(2):
                for b in range(4):
                    n = 4 * tb + b
                    dve.wait_ge(S("at_done"), n + 1)
                    dve.tensor_tensor(AT[:, b], PS[6 + b % 2][:, :].rearrange("p (q t) -> p q t", q=4),
                                      over_heads(const("before")), ALU.mult).then_inc(S("at_made"), 1)
                n0 = 24 * tb

                def t_add(n, b):
                    dve.wait_ge(S("tx_done"), n + 1)
                    dve.tensor_tensor(flat(Tm[:, b]), PS[2 + b % 2][:, :], flat(Tm[:, b]), ALU.add
                                      ).then_inc(S("t_added"), 1)
                for b in range(4):
                    t_add(n0 + b, b)
                with dve.Fori(1, 6) as i:
                    for b in range(4):
                        t_add(4 * i + (n0 + b), b)
                both = con_sb[:, CCOL["before"]:CCOL["before"] + 2 * P].unsqueeze(1).to_broadcast([P, 2, 2 * P])
                for b in range(4):
                    n = 4 * tb + b
                    dve.wait_ge(S("gram_done"), n + 1)
                    wait(dve, S("yc_done"), n - 1)
                    for g in range(2):
                        chain.add(dve.tensor_tensor(apk[:, b % 2, 2 * g:2 * g + 2],
                                                    PS[g][:, :].rearrange("p (q t) -> p q t", q=2), both, ALU.mult))
                    dve.tensor_tensor(apb[:, b % 2], PS[2][:, :].rearrange("p (q t) -> p q t", q=4),
                                      over_heads(const("upto")), ALU.mult).then_inc(S("apb_made"), 1)
                    if tb == 0 and b >= 1:
                        state_out(b - 1)
                    if tb == 0 and b == 3:
                        state_out(3)
            for g in range(4):
                dve.wait_ge(S("gnsum_done"), g + 1)
                y = Yc[:, 2 * g:2 * g + 2].rearrange("p c t -> p (c t)")
                stt(out=y, in0=PS[g][:, :], scalar=-1 / RN, in1=y, op0=ALU.mult, op1=ALU.add).then_inc(S("gn_centred"), 1)
            for g in range(4):
                invert(PS[4 + g][:, :], GQ[:, 2 * g:2 * g + 2].rearrange("p c t -> p (c t)"), 1 / RN, GN_EPS,
                       S("gnvar_done"), g + 1, S("gninv_ready"))
            for c in range(DC):
                dve.wait_ge(S("gnroot_ready"), c // 2 + 1)
                chain.link(stt(out=Yc[:, c], in0=Yc[:, c], scalar=col("gn_w", c), in1=GQ[:, c], op0=ALU.mult, op1=ALU.mult))
                chain.link(stt(out=Yc[:, c], in0=Yc[:, c], scalar=col("gn_b", c), in1=BON[:, c], op0=ALU.add, op1=ALU.add))
                dve.tensor_tensor(Yc[:, c], Yc[:, c], G_[:, c], ALU.mult).then_inc(S("yg_ready"), 1)
            for c in range(DC):
                low_part(Yc, OH, OL, c)
            layer("rw_out")
            residual(4, par_gain("norm_g2", DC))
            norm(5, [(par_gain("norm_g2", 2 * DC), OH, OL, None)])
            glu_up("glu0_up")
            layer("glu0_down")
            residual(5, par_gain("norm_g2", 3 * DC))
            norm(6, [(par_gain("norm_g2", 4 * DC), OH, OL, None)])
            layer("sgu_v")
            for g in range(2):
                dve.wait_ge(S("ws_done"), g + 1)
                dve.tensor_copy(wsT[:, 4 * g:4 * g + 4].rearrange("p g i -> p (g i)"), PS[6 + g][:, :]
                                ).then_inc(S("ws_copied"), 1)
            dve.wait_ge(S("ws_copied"), 2)
            dve.memset(wsT[P // 2:P, :, 0:P // 2], 0.0).then_inc(S("wsT_ready"), 1)
            layer("sgu_u")
            dve.wait_ge(S("sv_sum"), 1)
            for c in range(DC):
                stt(out=Vs_[:, c], in0=STAT[:, 0:T], scalar=-1 / D, in1=Vs_[:, c], op0=ALU.mult, op1=ALU.add
                    ).then_inc(S("sv_centred"), 1)
            invert(PS[6][:, 0:T], inv[:, 0], 1 / D, LN_EPS, S("sv_var"), 1, S("svinv_ready"))
            dve.wait_ge(S("svroot_ready"), 1)
            for c in range(DC):
                stt(out=Vs_[:, c], in0=Vs_[:, c], scalar=col("sgu_ln_w", c), in1=root[:, 0], op0=ALU.mult, op1=ALU.mult
                    ).then_inc(S("v_scaled"), 1)
            for g in range(DC):
                dve.wait_ge(S("spatial_done"), g + 1)
                t = xt[:, g % 2].rearrange("p (n i) -> p n i", n=2)
                dve.tensor_tensor(t, PS[6 + g % 2][:, 0:T].rearrange("p (n i) -> p n i", n=2),
                                  bsb[:, g].unsqueeze(1).to_broadcast([P, 2, P]), ALU.add).then_inc(S("sgu_used"), 1)
                dve.wait_ge(S("sgu_used"), g + 1)
                dve.tensor_tensor(Us_[:, g], Us_[:, g], xt[:, g % 2], ALU.mult).then_inc(S("us_ready"), 1)
            for c in range(DC):
                low_part(Us_, OH, OL, c)
            layer("sgu_out")
            residual(6, par_gain("norm_g2", 5 * DC))
            norm(7, [(par_gain("norm_g2", 6 * DC), OH, OL, None)])
            glu_up("glu1_up")
            layer("glu1_down")
            residual(7, par_gain("norm_g2", 7 * DC))

        @block.gpsimd
        def _(pool):
            def add_up(n):
                for c in range(DC):
                    pool.wait_ge(S("y_scaled"), DC * n + c + 1)
                    pool.tensor_tensor(X[:, c], X[:, c], Y[:, c], ALU.add).then_inc(S("x_ready"), 1)
                if debug is not None:
                    pool.wait_ge(S("x_ready"), DC * n + DC)
                    pool.dma_start(debug[n], X[:].rearrange("p c t -> p (c t)")).then_inc(S("dbg"), 16)
                    pool.wait_ge(S("dbg"), 16 * (n + 1))

            def mod_product(s, landed):
                pool.wait_ge(mod_landed[s], 16 * landed)
                pool.tensor_tensor(modraw[:, s], modraw[:, s], cond[:], ALU.mult).then_inc(S("mod_product"), 1)

            flatH, flatL = (x[:].rearrange("p c t -> p (c t)") for x in (GH, GL))

            pool.wait_ge(S("cond_ready"), 1)
            with pool.Fori(0, COUNT["conv_up"] // SLOTS) as i:
                for r in range(SLOTS):
                    for m, s, landed in riders("conv_up", i, r):
                        mod_product(s, landed)

            def split_hidden(k):
                def step(i, q):
                    pair = FC * k + 2 * i + q
                    pool.wait_ge(S("prod_made"), pair + 1)
                    pool.tensor_copy(flatH[:, ds(2 * T * i + q * T, T)], tmp[:, 3, q]).then_inc(S("hidden_hi"), 1)
                    pool.wait_ge(S("hidden_hi"), pair + 1)
                    pool.tensor_tensor(flatL[:, ds(2 * T * i + q * T, T)], tmp[:, 3, q],
                                       flatH[:, ds(2 * T * i + q * T, T)].bitcast(F32), ALU.subtract
                                       ).then_inc(S("hidden_split"), 1)
                with pool.Fori(0, FC // 2) as i:
                    for q in range(2):
                        if k == 0:
                            for m, s, landed in riders("ffn0_up", i, 2 * q + 1):
                                mod_product(s, landed)
                        step(i, q)

            for c in range(DC):
                pool.wait_ge(S("cv_silu"), c + 1)
                pool.tensor_copy(OH[:, c], Y[:, c]).then_inc(S("oh_ready"), 1)
            add_up(0)
            split_hidden(0)
            add_up(1)
            add_up(2)
            split_hidden(1)
            add_up(3)
            pool.wait_ge(S("ht_ready"), 5 * DC + DC)
            for c in range(DC):
                pool.tensor_tensor(XX[:, c, 1:], H[:, c, 0:T - 1], H[:, c, 1:], ALU.subtract).then_inc(S("xx_part"), 1)
                pool.tensor_scalar(XX[:, c, 0:1], H[:, c, 0:1], -1.0, None, ALU.mult).then_inc(S("xx_ready"), 1)
            pool.wait_ge(operand_ready, ready_at["rw_v"] + DC)
            pool.wait_ge(evac_done, START["rw_v"])
            for c in range(DC):
                pool.tensor_scalar(KK[:, c], K_[:, c], col("k_k", c), None, ALU.mult).then_inc(S("kk_raw"), 1)
            for c in range(DC):
                pool.wait_ge(S("kkroot_ready"), c // 2 + 1)
                pool.tensor_tensor(KK[:, c], KK[:, c], BON[:, c], ALU.mult).then_inc(S("kk_ready"), 1)
            pool.wait_ge(S("kk_ready"), DC)
            pool.wait_ge(S("kt_ready"), DC)

            def blocks(x, c):
                return x[:, c].rearrange("p (b t) -> p b t", b=2)

            for c in range(DC):
                pool.tensor_tensor(A_[:, c], KK[:, c], A_[:, c], ALU.mult).then_inc(S("ka_ready"), 1)
                pool.wait_ge(S("ka_ready"), c + 1)
                pool.tensor_tensor(blocks(Bt_, c), blocks(A_, c), E2[:, 2 * c:2 * c + 2, 1:P + 1], ALU.mult
                                   ).then_inc(S("rt_ready"), 1)
                pool.tensor_tensor(AR[:, c, :, 1], blocks(R_, c), E1[:, 2 * c:2 * c + 2, 1:P + 1], ALU.mult
                                   ).then_inc(S("rt_ready"), 1)

            def over_heads(m):
                return m.unsqueeze(1).to_broadcast([P, 4, P])

            for tb in range(2):
                n0 = 24 * tb
                for b in range(4):
                    n = 4 * tb + b
                    pool.wait_ge(S("at_made"), n + 1)
                    if n == 0:
                        pool.wait_ge(S("rw_tilde"), 1)
                    pool.tensor_tensor(TT[:, b], AT[:, b], over_heads(const("level0")), ALU.mult).then_inc(S("tt_part"), 1)
                    pool.wait_ge(S("tt_part"), n + 1)
                    pool.tensor_tensor(TT[:, b], TT[:, b], over_heads(ident), ALU.add).then_inc(S("tt0_made"), 1)

                def mask(n, b, level):
                    wait(pool, S("x_done"), n - 1)
                    pool.tensor_tensor(ML[:, b % 2], AT[:, b],
                                       con_sb[:, ds(CCOL["level0"] + P + P * level, P)].unsqueeze(1).to_broadcast([P, 4, P]),
                                       ALU.mult).then_inc(S("ml_made"), 1)
                for i in range(6):
                    for b in range(4):
                        mask(4 * i + (n0 + b), b, i)
                if tb == 0:
                    pool.wait_ge(S("tx_done"), 24)
            add_up(4)
            split_hidden(2)
            add_up(5)
            add_up(6)
            split_hidden(3)
            add_up(7)


def _columns(x):
    x = np.asarray(x).reshape(-1)
    return x.reshape(-1, P).T


def _units(w, order, parts):
    k, n = w.shape
    t = w.reshape(parts, k // P // parts, P, n // P, P).transpose(3, 0, 2, 1, 4)
    return t[order].reshape(len(order) * parts, P, k // parts)


def _paired(n):
    return [c + n * h for c in range(n) for h in range(2)]


def kernel(**inputs):
    import concourse.bacc as bacc
    from concourse.bass_utils import run_bass_kernel_spmd

    a = {k: np.asarray(v) for k, v in inputs.items()}
    eight = list(range(DC))
    w8 = np.concatenate([
        _units(a["cm_w1"][0], _paired(DC), 1), _units(a["cm_w2"][0], eight, 1),
        _units(a["ffn_w_in"][0], _paired(FC), 1),
        _units(a["w_v"], eight, 1), _units(a["w_k"], eight, 1), _units(a["w_q"][0], eight, 1),
        _units(a["w_o"][0], eight, 1), _units(a["ffn_w_in"][1], _paired(FC), 1),
        _units(a["rwkv_w_rkv_2"][0, 0], eight, 1), _units(a["rwkv_w_rkv_2"][0, 1], eight, 1),
        _units(a["rwkv_w_rkv_2"][0, 2], eight, 1), _units(a["rwkv_w_o_2"][0], eight, 1),
        _units(np.concatenate([a["ffn_w_gate_2"][0], a["ffn_w_up_2"][0]], 1), _paired(FC), 1),
        _units(a["sgu_w_in_2"][0], [c + DC for c in eight], 1), _units(a["sgu_w_in_2"][0], eight, 1),
        _units(a["sgu_w_out_2"][0], eight, 1),
        _units(np.concatenate([a["ffn_w_gate_2"][1], a["ffn_w_up_2"][1]], 1), _paired(FC), 1),
    ])
    w11 = np.concatenate([_units(w, eight, 2) for w in (a["ffn_w_out"][0], a["ffn_w_out"][1],
                                                        a["ffn_w_down_2"][0], a["ffn_w_down_2"][1])])
    wmod = np.concatenate([w.reshape(D, 6 * DC, P).transpose(1, 2, 0) for w in a["mod_w"]])
    lam = np.zeros((P, 4), np.float32)
    lam[:HEAD_DIM] = a["lam"][0].T
    given = {
        "mod_b": _columns(a["mod_b"]), "norm_g": _columns(a["norm_g"]),
        "cm_b1": _columns(a["cm_b1"]), "cm_dw": _columns(a["cm_dw"]), "cm_dwb": _columns(a["cm_dwb"]),
        "cm_ln_g": _columns(a["cm_ln_g"]), "cm_ln_b": _columns(a["cm_ln_b"]), "cm_b2": _columns(a["cm_b2"]),
        "kv_norm_g": _columns(a["kv_norm_g"]), "lam": lam, "subln_g": _columns(a["subln_g"]),
        "ffn_dw": _columns(a["ffn_dw"]), "ffn_dwb": _columns(a["ffn_dwb"]), "norm_g2": _columns(a["norm_gains_2"]),
        "mix": _columns(a["rwkv_mix_2"]), "w0": _columns(a["rwkv_w0_2"]), "a0": _columns(a["rwkv_a0_2"]),
        "k_k": _columns(a["rwkv_k_k_2"]), "k_a": _columns(a["rwkv_k_a_2"]), "r_k": _columns(a["rwkv_r_k_2"]),
        "gn_w": _columns(a["rwkv_gn_w_2"]), "gn_b": _columns(a["rwkv_gn_b_2"]), "sgu_b_in": _columns(a["sgu_b_in_2"]),
        "sgu_ln_w": _columns(a["sgu_ln_w_2"]), "sgu_ln_b": _columns(a["sgu_ln_b_2"]),
    }
    rest = 2 * P - GATE
    first = np.concatenate([a["rwkv_w1_2"][0], a["rwkv_a1_2"][0], np.pad(a["rwkv_g1_2"][0], ((0, 0), (0, rest)))], 1)
    g2 = np.pad(a["rwkv_g2_2"][0], ((0, rest), (0, 0)))
    arrays = {
        "w8": w8, "w11": w11, "wmod": wmod,
        "par": np.concatenate([given[n] for n, _ in PARAMS], 1),
        "con": constants(),
        "xin": a["x"][0].T.reshape(DC, P, T).transpose(1, 0, 2).reshape(P, DC * T),
        "relb": a["rel_bias"],
        "crow": a["c"].reshape(1, D),
        "lora_in": first.reshape(DC, P, 2 * LORA + 2 * P).transpose(1, 0, 2).reshape(P, -1),
        "lora_out": np.concatenate([np.concatenate([a["rwkv_w2_2"][0], a["rwkv_a2_2"][0]], 0), g2[:P], g2[P:]], 1),
        "sgu_ws": a["sgu_ws_2"][0].transpose(1, 0, 2).reshape(P, -1),
        "sgu_bs": a["sgu_bs_2"][0].reshape(1, -1),
    }
    nc = bacc.Bacc("TRN2", target_bir_lowering=False, num_devices=1)
    sent, args = {}, []
    for name, x in arrays.items():
        x = np.ascontiguousarray(x)
        sent[f"in_{name}"] = x
        args.append(nc.dram_tensor(f"in_{name}", x.shape, mybir.dt.from_np(x.dtype), kind="ExternalInput").ap())
    args.append(nc.dram_tensor("out", (P, DC * T), F32, kind="ExternalOutput").ap())
    program(nc, *args)
    r = run_bass_kernel_spmd(nc, [sent], core_ids=[0])
    got = r.results[0]["out"]
    return np.ascontiguousarray(got.reshape(P, DC, T).transpose(2, 1, 0).reshape(1, T, D))
```

```python
from contextlib import ExitStack
import math

import numpy as np

import concourse.bass as bass
from concourse import mybir

F32 = mybir.dt.float32
F32R = mybir.dt.float32r
ALU = mybir.AluOpType
ACT = mybir.ActivationFunctionType
AX_X = mybir.AxisListType.X
ds = bass.ds

P = 128
D = 1024
T = 256
DC = D // P
DFF = 2816
FC = DFF // P
TAPS = 31
PE_TAPS = 13
PAD = TAPS - 1
HEADS = 8
HEAD_DIM = 64
EPS = 1e-6
LN_EPS = 1e-5
GN_EPS = 64e-5
LAMBDA_INIT = 0.8 - 0.6 * math.exp(-0.3)
KAPPA = math.exp(-0.5)
RH = 16
RN = 64
LORA = 64
GATE = 160
SLOTS = 4
LEAD = 2
LATE_NORMS = (2, 5, 6, 7)
ADDED_BY_VECTOR = (2, 5, 7)
KT, KT_DOWN = DC, FC // 2

PHASES = [
    ("conv_up", 16, KT), ("conv_down", 8, KT), ("ffn0_up", 2 * FC, KT), ("ffn0_down", 16, KT_DOWN),
    ("att_v", 8, KT), ("att_k", 8, KT), ("att_q", 8, KT), ("att_out", 8, KT),
    ("ffn1_up", 2 * FC, KT), ("ffn1_down", 16, KT_DOWN),
    ("rw_r", 8, KT), ("rw_k", 8, KT), ("rw_v", 8, KT), ("rw_out", 8, KT),
    ("glu0_up", 2 * FC, KT), ("glu0_down", 16, KT_DOWN),
    ("sgu_v", 8, KT), ("sgu_u", 8, KT), ("sgu_out", 8, KT),
    ("glu1_up", 2 * FC, KT), ("glu1_down", 16, KT_DOWN),
]
NAMES = [n for n, _, _ in PHASES]
START, COUNT, TILES, OWN = {}, {}, {}, {}
_at, _own = 0, {KT: 0, KT_DOWN: 0}
for _n, _c, _k in PHASES:
    START[_n], COUNT[_n], TILES[_n], OWN[_n] = _at, _c, _k, _own[_k]
    _at += _c
    _own[_k] += _c
UNITS = _at

MOD_START = 2 * DC
RIDES = {
    "conv_up": (MOD_START, 8, (0, 1, 2, 3)), "conv_down": (6 * DC, 2, (0, 1)), "ffn0_up": (6 * DC + 2, 2, (2, 3)),
    "ffn0_down": (9 * DC, 4, (0, 1, 2, 3)), "att_v": (11 * DC, 4, (0, 1, 2, 3)),
}
_loads = [MOD_START // SLOTS] * SLOTS
LOADS_BEFORE = {}
for _n, (_, _per, _slots) in RIDES.items():
    LOADS_BEFORE[_n] = list(_loads)
    for _s in _slots:
        _loads[_s] += _per // len(_slots) * (1 if _n == "conv_down" else COUNT[_n] // SLOTS)


SHARED = {"conv_up": MOD_START, "ffn0_up": RIDES["ffn0_up"][0] - (6 * DC - MOD_START)}


def riders(name, i, r):
    first, per, slots = RIDES[name]
    mine = {8: (2 * r, 2 * r + 1), 4: (r,), 2: (r // 2,) if r % 2 else ()}[per]
    return [(per * i + (first + j), slots[j % len(slots)],
             per // len(slots) * i + (LOADS_BEFORE[name][slots[j % len(slots)]] + j // len(slots) + 1)) for j in mine]

PARAMS = [
    ("mod_b", 96), ("norm_g", 64), ("cm_b1", 16), ("cm_dw", TAPS * 8), ("cm_dwb", 8),
    ("cm_ln_g", 8), ("cm_ln_b", 8), ("cm_b2", 8), ("kv_norm_g", 8), ("lam", 4), ("subln_g", 1),
    ("ffn_dw", 2 * 3 * 2 * FC), ("ffn_dwb", 2 * 2 * FC),
    ("norm_g2", 64), ("mix", 48), ("w0", 8), ("a0", 8), ("k_k", 8), ("k_a", 8), ("r_k", 8),
    ("gn_w", 8), ("gn_b", 8), ("sgu_b_in", 16), ("sgu_ln_w", 8), ("sgu_ln_b", 8),
]
COL = {}
_at = 0
for _n, _c in PARAMS:
    COL[_n] = _at
    _at += _c
NPAR = _at

CONSTS = [("ident", P), ("ones", P), ("eps", 3), ("heads", P), ("before", P), ("upto", P)] + [(f"level{n}", P) for n in range(7)] \
    + [("bucket", 384), ("future", 384), ("half_row", 30), ("whole_row", 15)]
CCOL = {}
_at = 0
for _n, _c in CONSTS:
    CCOL[_n] = _at
    _at += _c
NCONST = _at
EARLY = CCOL["heads"]


def constants():
    s, t = np.arange(P)[:, None], np.arange(P)[None, :]
    out = np.zeros((P, NCONST), np.float32)

    def put(name, value):
        out[:value.shape[0], CCOL[name]:CCOL[name] + value.shape[1]] = value

    put("ident", np.eye(P))
    put("ones", np.ones((P, P)))
    put("heads", (s // RN == t // RN) * 1.0)
    put("before", (s < t) * 1.0)
    put("upto", (s <= t) * 1.0)
    for n in range(7):
        put(f"level{n}", ((s >> n) % 2 == 0) * ((t >> n) == (s >> n) + 1) * 1.0)
    n = np.maximum(np.arange(384) - 127, 0)
    large = 16 + np.floor(np.log(np.maximum(n, 1) / 16) / math.log(8) * 16 + 1e-9)
    bucket = np.where(n < 16, n, np.minimum(large, 31)).astype(int)
    put("bucket", (np.arange(32)[:, None] == bucket[None, :]) * 1.0)
    put("eps", np.tile([[EPS, LN_EPS, GN_EPS]], (P, 1)))
    put("half_row", (np.arange(30)[None, :] == 14 + s // RN) * 1.0)
    put("whole_row", (np.arange(15)[None, :] == 7) * np.ones((P, 1)))
    put("future", np.repeat((np.arange(384)[None, :] < 127) * -1e30, 8, axis=0))
    return out


def program(nc, w8, w11, wmod, par, con, xin, relb, crow, lora_in, lora_out, sgu_ws, sgu_bs, out):
    scratch = nc.dram_tensor("rel_bias_rows", (HEADS, 384), F32, kind="Internal").ap()

    with ExitStack() as ctx:
        used = {}

        def S(name):
            if name not in used:
                used[name] = ctx.enter_context(nc.semaphore(name))
            return used[name]

        base = nc.sbuf_base + (-nc.sbuf_base) % 32
        top = [base]

        def fixed(name, shape, dt=F32):
            n = 4 * int(np.prod(shape[1:]))
            t = nc.alloc_sbuf_tensor_at(name, shape, dt, offset=top[0])
            top[0] += n + (-n) % 32
            return t

        UW = KT_DOWN * P
        raw = fixed("raw", [P, SLOTS, UW])
        hi_at = top[0]
        hi = fixed("hi", [P, SLOTS, UW], F32R)
        lo_at = top[0]
        lo = fixed("lo", [P, SLOTS, UW], F32R)
        X = fixed("X", [P, DC, T])
        par_sb = fixed("par_sb", [P, NPAR])
        con_sb = fixed("con_sb", [P, NCONST])
        root_at = top[0]
        root = fixed("root", [P, 2, T])
        inv = fixed("inv", [P, 2, T])
        xt = fixed("xt", [P, 4, T])
        mods = fixed("mods", [P, 96])
        ngain = fixed("ngain", [P, 4, DC])
        rgain = fixed("rgain", [P, 4, DC])
        mod_sums = fixed("mod_sums", [P, 96])
        small = fixed("small", [P, 32])
        mid = fixed("mid", [P, 2, 16])
        mid_ka = fixed("mid_ka", [P, DC])
        dec = fixed("dec", [P, DC])

        F = 8320
        arena = top[0]

        def at(place, name, shape, dt=F32, plus=0):
            return nc.alloc_sbuf_tensor_at(name, shape, dt, offset=arena + (int(place * F) + plus) // 32 * 32)

        Y = at(0, "Y", [P, DC, T])
        SQ = at(1, "SQ", [P, DC, T])
        HT = at(1, "HT", [P, DC, T])
        OH = at(2, "OH", [P, DC, T], F32R)
        OL = at(3, "OL", [P, DC, T], F32R)
        tmp = at(4, "tmp", [P, 4, 2, T])
        GH = at(5, "GH", [P, FC, T], F32R)
        GL = at(5, "GL", [P, FC, T], F32R, plus=4 * FC * T)
        modraw = at(5, "modraw", [P, SLOTS, D], plus=8 * FC * T)
        cond = at(5, "cond", [P, D], plus=8 * FC * T + 16 * D)
        upad = at(5, "upad", [P, DC, PAD + T])
        cv = at(7, "cv", [P, DC, T])
        diags = at(8, "diags", [P, 2, PE_TAPS, P])
        PH = at(5, "PH", [P, DC, T], F32R)
        PL = at(6, "PL", [P, DC, T], F32R)
        K = at(7, "K", [P, DC, T])
        Q = at(8, "Q", [P, DC, T])
        V = at(9, "V", [P, DC, T])
        VT = at(10, "VT", [P, 2, D])
        bias = at(11, "bias", [P, HEADS, T])
        biasrev = at(12, "biasrev", [P, HEADS, T])
        ss = at(2, "ss", [P, 2, 2, T])
        pr = at(2, "pr", [P, 2, 2, T], plus=4096)
        aa = at(3, "aa", [P, 2, T])
        aT = at(3, "aT", [P, 2, T], plus=2048)
        O = at(4, "O", [P, HEADS, T])
        H = HT
        XX = at(0, "XX", [P, DC, T])
        RH2 = at(4, "RH2", [P, DC, T], F32R)
        RL2 = at(5, "RL2", [P, DC, T], F32R)
        xs = at(9, "xs", [P, DC, T]), at(7, "xs_a", [P, DC, T]), at(8, "xs_g", [P, DC, T])
        l1 = at(10, "l1", [P, DC, 2 * LORA + 2 * P])
        l2 = at(12, "l2", [P, 3, D])
        R_ = at(6, "R_", [P, DC, T])
        K_ = at(7, "K_", [P, DC, T])
        V_ = at(8, "V_", [P, DC, T])
        W_ = at(9, "W_", [P, DC, T])
        A_ = at(10, "A_", [P, DC, T])
        G_ = at(11, "G_", [P, DC, T])
        cum = at(12, "cum", [P, 2 * DC, P + 1])
        E1 = at(9, "E1", [P, 2 * DC, P + 1])
        E2 = cum
        KK = at(1, "KK", [P, DC, T])
        BON = at(0, "BON", [P, DC, T])
        AR = at(2, "AR", [P, DC, 2, 2, P])
        Bt_ = at(4, "Bt_", [P, DC, T])
        Kt_ = at(5, "Kt_", [P, DC, T])
        VR = at(6, "VR", [P, 2, D])
        Btok = at(7, "Btok", [P, 2, D])
        SZ = at(8, "SZ", [P, RH, RN])
        Zs = at(8, "Zs", [P, 2, 4 * RN], plus=4096)
        Us = at(8, "Us", [P, 2, 4 * RN], plus=6144)
        Yc = at(1, "Yc", [P, DC, T])
        AT = at(9, "AT", [P, 4, 4, P])
        Tm = at(10, "Tm", [P, 4, 4, P])
        TT = (at(12, "TT", [P, 4, 4, P]), nc.alloc_sbuf_tensor_at("TT_b", [P, 4, 4, P], F32, offset=root_at))
        apb = at(13, "apb", [P, 2, 4, P])
        head_rows_k = at(13, "head_rows_k", [RH, D])
        head_rows_y = at(10, "head_rows_y", [RH, D])
        half = 2 * 4 * UW
        Xs = nc.alloc_sbuf_tensor_at("Xs", [P, 2, 4, P], F32, offset=hi_at + half)
        ML = nc.alloc_sbuf_tensor_at("ML", [P, 2, 4, P], F32, offset=hi_at + half + 4096)
        apk = nc.alloc_sbuf_tensor_at("apk", [P, 2, 4, 2 * P], F32, offset=lo_at + half)
        GQ = at(9, "GQ", [P, DC, T])
        Us_ = at(5, "Us_", [P, DC, T])
        Vs_ = at(6, "Vs_", [P, DC, T])
        VNT = at(7, "VNT", [P, 2, DC, P])
        wsr = at(8, "wsr", [P, DC, P])
        wsT = at(8, "wsT", [P, DC, P], plus=4096)
        bsb = at(9, "bsb", [P, DC, P])

        PS = [ctx.enter_context(nc.psum_tensor(f"ps{n}", [P, 512], F32)) for n in range(8)]
        STAT = PS[4]

        def col(name, n=0):
            return par_sb[:, COL[name] + n:COL[name] + n + 1]

        def cols(name, n, m):
            return par_sb[:, COL[name] + n:COL[name] + n + m]

        def const(name, width=P):
            return con_sb[:, CCOL[name]:CCOL[name] + width]

        eps, ln_eps, gn_eps = (con_sb[:, CCOL["eps"] + n:CCOL["eps"] + n + 1] for n in range(3))
        ident, ones, heads_ones = const("ident"), const("ones"), const("heads")

        raw_landed = [S(f"raw_landed{s}") for s in range(SLOTS)]
        mod_landed = [S(f"mod_landed{s}") for s in range(SLOTS)]
        hi_made, lo_made = S("hi_made"), S("lo_made")
        mm_done, evac_done = S("mm_done"), S("evac_done")
        mod_done = S("mod_done")
        par_landed, con_landed, x_landed = S("par_landed"), S("con_landed"), S("x_landed")
        operand_ready = S("operand_ready")

        ready_at, n = {}, 0
        for name in ("conv_up", "conv_down", "ffn0_up", "att_v", "att_q", "att_out", "ffn1_up", "rw_r", "rw_k",
                     "rw_v", "rw_out", "glu0_up", "sgu_v", "sgu_out", "glu1_up"):
            ready_at[name] = n
            n += DC
        ready_at["att_k"], ready_at["sgu_u"] = ready_at["att_v"], ready_at["sgu_v"]
        UP = ["ffn0_up", "ffn1_up", "glu0_up", "glu1_up"]
        for k, name in enumerate(("ffn0_down", "ffn1_down", "glu0_down", "glu1_down")):
            ready_at[name] = FC * k

        BESIDE = {0: "gram", 2: "z", 3: "u", 4: "y"}
        SECOND_BLOCK = [(what, g + b) for g in (0, 2) for what in ("gram", "z", "u", "y") for b in range(2)]

        def bank_set(tb, b):
            return 4 * (tb == 0 or b % 2 == 0) + 0

        def banks_free(eng, tb, b):
            n = 4 * tb + b
            if tb == 0 or b == 0:
                eng.wait_ge(S("yc_copied"), n)
                eng.wait_ge(S("state_made"), min(n, 4))
            elif b == 1:
                eng.wait_ge(S("t_added"), 48)
                eng.wait_ge(S("x_copied"), 48)
            else:
                eng.wait_ge(S("yc_copied"), n - 1)

        block = ctx.enter_context(nc.Block())

        def wait(eng, sem, value):
            if isinstance(value, int) and value <= 0:
                return
            eng.wait_ge(sem, value)

        def bodies(eng, name, body, peel_first=False, peel_last=False):
            n = COUNT[name] // SLOTS
            a, b = int(peel_first), n - int(peel_last)
            for i in range(min(a, n)):
                body(i, i == n - 1)
            if b - a > 1:
                with eng.Fori(a, b) as i:
                    body(i, False)
            elif b - a == 1:
                body(a, a == n - 1)
            if b < n and b >= a:
                body(b, True)

        def next_tiles(name):
            k = NAMES.index(name) + 1
            return TILES[NAMES[k]] if k < len(NAMES) else None

        def squares_added(n, of_x):
            return (DC - 2) * (n + len([m for m in LATE_NORMS if m < n or (m == n and not of_x)]))

        def wait_x(eng, n, c):
            mine = c in ADDED_BY_VECTOR
            of = [k for k in range(DC) if (k in ADDED_BY_VECTOR) == mine]
            eng.wait_ge(S("x_added_vector" if mine else "x_added_gpsimd"), len(of) * n + of.index(c) + 1)

        class Chain:

            def __init__(self, eng, sem):
                self.eng, self.sem, self.n = eng, sem, 0

            def add(self, ins):
                ins.then_inc(self.sem, 1)
                self.n += 1

            def sync(self, but=0):
                self.eng.wait_ge(self.sem, self.n - but)

            def link(self, ins):
                self.add(ins)
                self.sync()

        @block.sync
        def _(sp):
            sp.dma_start(cond[:], crow.to_broadcast([P, D])).then_inc(S("c_landed"), 16)

            def load_mod(m, s, depth):
                wait(sp, mod_done, m - (depth - 1))
                sp.dma_start(modraw[:, s], wmod[ds(m, 1)].rearrange("a p n -> p (a n)")).then_inc(mod_landed[s], 16)

            def load_unit(name, i, r):
                kt = TILES[name]
                src = w8 if kt == KT else w11
                wait(sp, lo_made, START[name] - 3 + r + 4 * i)
                sp.dma_start(raw[:, r, 0:kt * P], src[ds(OWN[name] + 4 * i + r, 1)].rearrange("a p n -> p (a n)")
                             ).then_inc(raw_landed[r], 16)

            def load_riders(name, i, r):
                if name in RIDES and not (name == "conv_down" and i):
                    for m, s, _ in riders(name, i, r):
                        load_mod(m, s, len(RIDES[name][2]))

            def distance_biases():
                sp.wait_ge(S("bias_rows"), 1)
                sp.dma_start(scratch, xt[0:HEADS].rearrange("p a t -> p (a t)")[:, 0:384]).then_inc(S("rows_stored"), 16)
                sp.wait_ge(S("rows_stored"), 16)
                sp.wait_ge(mod_done, 96)
                skewed = bass.AP(tensor=scratch.tensor, offset=0, ap=[[1, P], [384, HEADS], [1, T]])
                sp.dma_start(biasrev[:], skewed).then_inc(S("bias_landed"), 16)

            def lora_weights():
                sp.wait_ge(evac_done, START["rw_r"])
                sp.dma_start(l1[:], lora_in.rearrange("p (c n) -> p c n", c=DC)).then_inc(S("lora_landed"), 16)
                sp.dma_start(l2[:], lora_out.rearrange("p (c n) -> p c n", c=3)).then_inc(S("lora_landed"), 16)

            def gating_weights():
                sp.wait_ge(evac_done, START["sgu_v"])
                sp.dma_start(wsr[:], sgu_ws.rearrange("p (g j) -> p g j", g=DC)).then_inc(S("sgu_landed"), 16)
                sp.dma_start(bsb[:].rearrange("p g i -> p (g i)"), sgu_bs.to_broadcast([P, D])
                             ).then_inc(S("sgu_landed"), 16)

            after_four = {"att_q": distance_biases, "rw_r": lora_weights,
                          "sgu_v": gating_weights}
            for m in range(16):
                load_mod(m, m % 4, SLOTS)
                if m == 3:
                    sp.dma_start(par_sb[:], par).then_inc(par_landed, 16)
                    sp.dma_start(X[:], xin.rearrange("p (c t) -> p c t", c=DC)).then_inc(x_landed, 16)
                if m == 7:
                    sp.dma_start(con_sb[:, 0:EARLY], con[:, 0:EARLY]).then_inc(con_landed, 16)
                if m == MOD_START - SLOTS - 1:
                    for r in range(LEAD):
                        load_unit("conv_up", 0, r)

            def body(name, i):
                for r in range(SLOTS):
                    if r >= LEAD or name != "conv_up" or not isinstance(i, int):
                        load_unit(name, i, r)
                    if r == SLOTS - 1:
                        rides = name, i, 0
                    elif isinstance(i, int) and i == 0:
                        before = NAMES[max(NAMES.index(name) - 1, 0)]
                        rides = before, COUNT[before] // SLOTS - 1, r + 1
                    else:
                        rides = name, i - 1, r + 1
                    if rides[0] != name or r == SLOTS - 1 or not isinstance(i, int) or i:
                        load_riders(*rides)

            for name in NAMES:
                if name == "conv_down":
                    sp.dma_start(con_sb[:, EARLY:NCONST], con[:, EARLY:NCONST]).then_inc(S("rest_landed"), 16)
                    sp.dma_start(small[0:32, 16:24], relb).then_inc(S("rest_landed"), 16)
                if name in after_four:
                    body(name, 0)
                    after_four[name]()
                    body(name, 1)
                else:
                    bodies(sp, name, lambda i, last: body(name, i), peel_first=True)
            for c in range(DC):
                wait_x(sp, 7, c)
                sp.dma_start(out[:, c * T:(c + 1) * T], X[:, c]).then_inc(S("stored"), 16)
            sp.wait_ge(S("stored"), 16 * DC)

        @block.tensor
        def _(pe):
            def early_taps(c, q):
                pe.wait_ge(S("diags_made"), c + 1)
                pe.wait_ge(evac_done, 2 * c + 2)
                wait(pe, S("cv_ready"), c - 1)
                for j in range(PE_TAPS):
                    ins = pe.matmul(PS[5 + 2 * q][:, 0:T], diags[:, q, j],
                                    upad[:].rearrange("p c t -> p (c t)")[:, ds((PAD + T) * c + j, T)],
                                    start=(j == 0), stop=(j == PE_TAPS - 1))
                ins.then_inc(S("taps_done"), 1)

            def between_conv_units(i, r):
                if r % 2 == 0 and not (isinstance(i, int) and 2 * i + r // 2 == 0):
                    early_taps(2 * i + (r // 2 - 1), (r // 2 + 1) % 2)

            def layer(name, oh, ol, between=None, peel_first=False, fresh=False):
                kt, start = TILES[name], START[name]
                down = kt == KT_DOWN

                def body(i, last):
                    for r in range(SLOTS):
                        u = start + 4 * i + r
                        k0 = kt * (r % 2) if down else 0
                        bank = PS[r - r % 2 if down else r]
                        pe.wait_ge(lo_made, u + 1)
                        if not (fresh and isinstance(i, int) and i == 0):
                            wait(pe, evac_done, u - 3)
                        elif r == 0:
                            pe.wait_ge(evac_done, start)
                        for k in range(kt):
                            if r == 0 or (down and r == 1):
                                pe.wait_ge(S("hidden_split") if down else operand_ready, ready_at[name] + k0 + k + 1)
                            w = slice(k * P, (k + 1) * P)
                            first = k == 0 and (not down or r % 2 == 0)
                            final = k == kt - 1 and (not down or r % 2 == 1)
                            pe.matmul(bank[:, 0:T], lo[:, r, w], oh[:, k0 + k], start=first, stop=False)
                            pe.matmul(bank[:, 0:T], hi[:, r, w], ol[:, k0 + k], start=False, stop=False)
                            ins = pe.matmul(bank[:, 0:T], hi[:, r, w], oh[:, k0 + k], start=False, stop=final)
                        ins.then_inc(mm_done, 1)
                        if between:
                            between(i, r)
                bodies(pe, name, body, peel_first=(start == 0) or peel_first)

            def sum_chunks(ready, base, src, columns, done):
                for c in range(DC):
                    pe.wait_ge(ready, base + c + 1)
                    ins = pe.matmul(STAT[:, columns:columns + T], ones, src[:, c], start=(c == 0), stop=(c == DC - 1))
                ins.then_inc(done, 1)

            def norm(n):
                sum_chunks(S("xsq_ready"), DC * n, SQ, T, S("xstat_done"))

            def first_layer(name, n):
                def between(i, r):
                    if isinstance(i, int) and i == 0 and r == 1:
                        pe.wait_ge(S("sq_added"), squares_added(n, True) + DC - 2)
                        pe.matmul(STAT[:, T:2 * T], ones, Y[:, 0], start=True, stop=False)
                        pe.wait_ge(S("xsq_ready"), DC * (n + 1))
                        pe.matmul(STAT[:, T:2 * T], ones, Y[:, DC - 1], start=False, stop=True
                                  ).then_inc(S("xstat_done"), 1)
                layer(name, OH, OL, between, peel_first=True, fresh=True)

            def out_layer(name, oh, ol, n):
                layer(name, oh, ol)
                pe.wait_ge(S("sq_added"), squares_added(n, False) + DC - 2)
                pe.matmul(STAT[:, 0:T], ones, SQ[:, 0], start=True, stop=False)
                pe.wait_ge(S("ysq_ready"), DC * (n + 1))
                pe.matmul(STAT[:, 0:T], ones, SQ[:, DC - 1], start=False, stop=True).then_inc(S("ystat_done"), 1)

            pe.wait_ge(con_landed, 16)
            norm(0)
            layer("conv_up", OH, OL, between_conv_units)
            early_taps(DC - 1, 1)
            for c in range(DC):
                pe.wait_ge(S("cv_ready"), c + 1)
                ins = pe.matmul(STAT[:, 0:T], ones, cv[:, c], start=(c == 0), stop=(c == DC - 1))
            ins.then_inc(S("cv_sum"), 1)
            for c in range(DC):
                pe.wait_ge(S("cvsq_ready"), c + 1)
                ins = pe.matmul(PS[6][:, 0:T], ones, SQ[:, c], start=(c == 0), stop=(c == DC - 1))
            ins.then_inc(S("cv_var"), 1)
            out_layer("conv_down", OH, OL, 0)
            pe.wait_ge(S("rest_landed"), 32)
            pe.matmul(PS[6][0:HEADS, 0:384], small[0:32, 16:24], con_sb[0:32, CCOL["bucket"]:CCOL["bucket"] + 384],
                      start=True, stop=True).then_inc(S("rows_done"), 1)
            norm(1)
            layer("ffn0_up", OH, OL)
            out_layer("ffn0_down", GH, GL, 1)
            first_layer("att_v", 2)
            layer("att_k", OH, OL)

            def transposes(count, src, banks, copied, done):
                for g in range(count):
                    wait(pe, copied, g - len(banks) + 1)
                    for q in range(4):
                        ins = pe.transpose(PS[banks[g % len(banks)]][:, q * P:(q + 1) * P], src(g, q), ident)
                    ins.then_inc(done, 1)

            pe.wait_ge(evac_done, START["att_k"])
            transposes(4, lambda g, q: V[:, 4 * (g % 2) + q, (g // 2) * P:(g // 2 + 1) * P], (4, 5, 6, 7),
                       S("vt_copied"), S("vt_done"))
            layer("att_q", PH, PL)
            pe.wait_ge(evac_done, START["att_out"])
            pe.wait_ge(S("vt_copied"), 4)
            pe.matmul(PS[5][:, 0:2], ones, small[:, 2:4], start=True, stop=True).then_inc(S("lam_sum"), 1)
            NA = 2 * HEADS
            def scores(n):
                h, qb = n // 2, n % 2
                nk = P * (qb + 1)
                wait(pe, S("att_scaled"), n - 1)
                for c in range(2):
                    rows = slice(HEAD_DIM * c, HEAD_DIM * (c + 1))
                    ins = pe.matmul(PS[2 * (n % 2) + c][:, 0:nk], Q[rows, h, qb * P:(qb + 1) * P], K[rows, h, 0:nk],
                                    start=True, stop=True)
                ins.then_inc(S("att_scores"), 1)

            scores(0)
            for n in range(NA + 2):
                if n + 1 < NA:
                    scores(n + 1)
                if 1 <= n <= NA:
                    m = n - 1
                    pe.wait_ge(S("att_probs"), m + 1)
                    if m == 1:
                        pe.wait_ge(S("lam_ready"), 1)
                    wait(pe, S("aT_copied"), m - 1)
                    for kb in range(m % 2 + 1):
                        ins = pe.transpose(PS[4 + m % 2][:, kb * P:(kb + 1) * P], aa[:, m % 2, kb * P:(kb + 1) * P], ident)
                    ins.then_inc(S("aT_done"), 1)
                if n >= 2:
                    m = n - 2
                    pe.wait_ge(S("aT_copied"), m + 1)
                    wait(pe, S("o_copied"), m - 1)
                    for kb in range(m % 2 + 1):
                        ins = pe.matmul(PS[6 + m % 2][:, 0:P], VT[:, kb, (m // 2) * P:(m // 2 + 1) * P],
                                        aT[:, m % 2, kb * P:(kb + 1) * P], start=(kb == 0), stop=(kb == m % 2))
                    ins.then_inc(S("pv_done"), 1)
            for c in range(HEADS):
                pe.wait_ge(S("osq_ready"), c + 1)
                w = CCOL["whole_row"] + 7 - c
                ins = pe.matmul(PS[0][0:HEADS, 0:T], con_sb[:, w:w + HEADS], SQ[:, c], start=(c == 0), stop=(c == HEADS - 1))
            ins.then_inc(S("ostat_done"), 1)
            pe.wait_ge(S("oinv_ready"), 1)
            for c in range(HEADS):
                wait(pe, S("o_normed"), c - 2)
                pe.matmul(PS[1 + c % 3][:, 0:T], ident[0:HEADS, c:c + 1].to_broadcast([HEADS, P]), inv[0:HEADS, 0],
                          start=True, stop=True).then_inc(S("o_spread"), 1)
            out_layer("att_out", OH, OL, 2)
            norm(3)
            layer("ffn1_up", OH, OL)
            out_layer("ffn1_down", GH, GL, 3)
            norm(4)

            layer("rw_r", OH, OL)
            pe.wait_ge(S("lora_landed"), 32)
            pe.wait_ge(evac_done, START["rw_k"])
            for j, (c0, width, bank, p0) in enumerate([(0, LORA, 0, 0), (LORA, LORA, 1, LORA), (2 * LORA, P, 2, 0),
                                                       (2 * LORA + P, P, 3, 0)]):
                src = min(j, 2)
                for k in range(DC):
                    pe.wait_ge(S("xs_ready"), 3 * k + src + 1)
                    ins = pe.matmul(PS[bank][p0:p0 + width, 0:T], l1[:, k, c0:c0 + width], xs[src][:, k],
                                    start=(k == 0), stop=(k == DC - 1))
                ins.then_inc(S("lora1_done"), 1)
            for j in range(3 * DC):
                b, c = divmod(j, DC)
                bank = PS[4 + j % 4]
                pe.wait_ge(S("lora1_used"), [1, 2, 4][b])
                wait(pe, S("lora2_used"), j - 3)
                if b == 0:
                    ins = pe.matmul(bank[:, 0:T], l2[0:LORA, 0, c * P:(c + 1) * P], root[0:LORA, 0], start=True, stop=True)
                elif b == 1:
                    ins = pe.matmul(bank[:, 0:T], l2[LORA:P, 0, c * P:(c + 1) * P], root[LORA:P, 0], start=True, stop=True)
                else:
                    pe.matmul(bank[:, 0:T], l2[:, 1, c * P:(c + 1) * P], root[:, 1], start=True, stop=False)
                    ins = pe.matmul(bank[:, 0:T], l2[:, 2, c * P:(c + 1) * P], inv[:, 0], start=False, stop=True)
                ins.then_inc(S("lora2_done"), 1)
            layer("rw_k", RH2, RL2)
            pe_groups = [slice(2 * g, 2 * g + 2) for g in range(4)]

            def half_sums(dst, src, c):
                w = CCOL["half_row"] + 14 - 2 * c
                return pe.matmul(dst, con_sb[:, w:w + RH], src, start=(c == 0), stop=(c == DC - 1))

            def spread_halves(dst, head_rows, rows, c):
                return pe.matmul(dst, head_rows[:, c * P:(c + 1) * P], rows, start=True, stop=True)

            def kk_squares(i, r):
                k = 4 * i + r
                if 1 <= k < 5:
                    pe.wait_ge(S("lora2_used"), 3 * DC)
                    pe.wait_ge(S("kksq_ready"), k)
                    for c in (2 * k - 2, 2 * k - 1):
                        ins = half_sums(PS[4][0:RH, 0:T], BON[:, c], c)
                    if k == 4:
                        ins.then_inc(S("kkstat_done"), 1)
                if 6 <= k:
                    pe.wait_ge(S("kkinv_ready"), 1)
                    pe.wait_ge(S("head_rows_made"), 1)
                    for c in range(4 * (k - 6), 4 * (k - 6) + 4):
                        wait(pe, S("kk_ready"), c - 2)
                        spread_halves(PS[5 + c % 3][:, 0:T], head_rows_k, inv[0:RH, 0], c).then_inc(S("kk_spread"), 1)
            layer("rw_v", OH, OL, kk_squares, peel_first=True)
            pe.wait_ge(evac_done, START["rw_out"])

            def rw_src(g, q):
                if g < 4:
                    return V_[:, 4 * (g % 2) + q, (g // 2) * P:(g // 2 + 1) * P]
                return (Bt_ if g < 6 else Kt_)[:, 4 * (g % 2) + q, 0:P]

            def turn(g):
                wait(pe, S("rwt_copied"), g - 3)
                for q in range(4):
                    ins = pe.transpose(PS[g % 4][:, q * P:(q + 1) * P], rw_src(g, q), ident)
                ins.then_inc(S("rwt_done"), 1)
            for g in range(4):
                turn(g)
            pe.wait_ge(S("kk_ready"), DC)
            for g in range(4):
                pe.wait_ge(S("bp_ready"), 2 * g + 2)
                pe.matmul(PS[4 + g][:, :], heads_ones, BON[:, pe_groups[g]].rearrange("p c t -> p (c t)"),
                          start=True, stop=True).then_inc(S("bpsum_done"), 1)
            pe.wait_ge(S("rw_tilde"), 1)
            for g in range(4, 8):
                turn(g)
            pe.wait_ge(S("rwt_copied"), 8)

            def start_inverse(tb):
                for b in range(4):
                    n = 4 * tb + b
                    rows = slice(RN * (b % 2), RN * (b % 2 + 1))
                    if b < 2:
                        wait(pe, S("x_copied"), 24 * tb)
                    wait(pe, S("at_made"), n - 1)
                    for q in range(4):
                        c = 4 * (b // 2) + q
                        ins = pe.matmul(PS[b % 2][:, q * P:(q + 1) * P], Bt_[rows, c, tb * P:(tb + 1) * P],
                                        AR[rows, c, tb, 0], start=True, stop=True)
                    ins.then_inc(S("at_done"), 1)
                for b in range(4):
                    n = 4 * tb + b
                    pe.wait_ge(S("tt0_made"), n + 1)
                    if b < 2:
                        wait(pe, S("t_added"), 24 * tb)
                    wait(pe, S("t0_copied"), n - 1)
                    for q in range(4):
                        ins = pe.transpose(PS[2 + b % 2][:, q * P:(q + 1) * P], TT[tb][:, b, q], ident)
                    ins.then_inc(S("t0_done"), 1)

            def x_part(tb, step):
                n, b = 24 * tb + step, step % 4
                pe.wait_ge(S("ml_made"), n + 1)
                if step < 4:
                    pe.wait_ge(S("t0_copied"), 4 * tb + b + 1)
                else:
                    pe.wait_ge(S("t_added"), n - 3)
                wait(pe, S("x_copied"), n - 1)
                for q in range(4):
                    ins = pe.matmul(PS[b % 2][:, q * P:(q + 1) * P], ML[:, b % 2, q], Tm[:, b, q], start=True, stop=True)
                ins.then_inc(S("x_done"), 1)

            def tx_part(tb, step):
                n, b, w = 24 * tb + step, step % 4, 2 << (step // 4)
                pe.wait_ge(S("x_copied"), n + 1)
                wait(pe, S("t_added"), n - 1)
                if step < 4:
                    pe.wait_ge(S("t0_copied"), 4 * tb + 4)
                for q in range(4):
                    x, tt = Xs[:, b % 2, q], TT[tb][:, b, q]
                    dst = [PS[2 + b % 2][:, 256 * h + q * RN:256 * h + (q + 1) * RN].rearrange("p (m w) -> p m w", w=w)
                           for h in range(2)]
                    if step < 20:
                        pe.matmul(dst[0], tt, x.rearrange("p (m two w) -> p m two w", two=2, w=w)[:, :, 0],
                                  start=True, stop=True)
                    ins = pe.matmul(dst[1], x, tt.rearrange("p (m two w) -> p m two w", two=2, w=w)[:, :, 1],
                                    start=True, stop=True)
                ins.then_inc(S("tx_done"), 1)

            def inverse_step(tb, step):
                x_part(tb, step)
                if step:
                    tx_part(tb, step - 1)

            def head(b, q):
                return 8 * (b // 2) + b % 2 + 2 * q

            def rows_of(b):
                return slice(RN * (b % 2), RN * (b % 2 + 1))

            def gram(tb, b):
                n, p = 4 * tb + b, bank_set(tb, b)
                if n:
                    banks_free(pe, tb, b)
                rows, tok = rows_of(b), slice(tb * P, (tb + 1) * P)
                for q in range(4):
                    c = 4 * (b // 2) + q
                    pe.matmul(PS[p + q // 2][:, (q % 2) * T:(q % 2 + 1) * T], Kt_[rows, c, tok],
                              AR[rows, c, tb].rearrange("p a t -> p (a t)"), start=True, stop=True)
                    ins = pe.matmul(PS[p + 2][:, q * P:(q + 1) * P], Bt_[rows, c, tok], AR[rows, c, tb, 1],
                                    start=True, stop=True)
                ins.then_inc(S("gram_done"), 1)

            def z_part(tb, b):
                n, zb = 4 * tb + b, PS[bank_set(tb, b) + 3]
                pe.wait_ge(S("apb_made"), n + 1)
                if tb:
                    pe.wait_ge(S("state_made"), 4)
                for q in range(4):
                    v = VR[:, tb, head(b, q) * RN:(head(b, q) + 1) * RN]
                    ins = pe.matmul(zb[:, q * RN:(q + 1) * RN], apk[:, b % 2, q, 0:P], v, start=True, stop=(tb == 0))
                    if tb:
                        ins = pe.matmul(zb[:, q * RN:(q + 1) * RN], AR[:, 4 * (b // 2) + q, 1, 0], SZ[:, head(b, q)],
                                        start=False, stop=True)
                ins.then_inc(S("z_done"), 1)

            def u_part(tb, b):
                n, ub = 4 * tb + b, PS[bank_set(tb, b) + 3]
                pe.wait_ge(S("z_copied"), n + 1)
                if b == 0:
                    pe.wait_ge(S("t_added"), 24 * tb + 24)
                for q in range(4):
                    ins = pe.matmul(ub[:, 256 + q * RN:256 + (q + 1) * RN], TT[tb][:, b, q],
                                    Zs[:, b % 2, q * RN:(q + 1) * RN], start=True, stop=True)
                ins.then_inc(S("u_done"), 1)

            def y_part(tb, b):
                n, p = 4 * tb + b, bank_set(tb, b)
                pe.wait_ge(S("u_copied"), n + 1)
                rows = rows_of(b)
                for q in range(4):
                    v = VR[:, tb, head(b, q) * RN:(head(b, q) + 1) * RN]
                    dst = PS[p][rows, q * P:(q + 1) * P]
                    pe.matmul(dst, Us[:, b % 2, q * RN:(q + 1) * RN], apb[:, b % 2, q], start=True, stop=False)
                    ins = pe.matmul(dst, v, apk[:, b % 2, q, P:2 * P], start=False, stop=(tb == 0))
                    if tb:
                        ins = pe.matmul(dst, SZ[:, head(b, q)], AR[:, 4 * (b // 2) + q, 1, 1], start=False, stop=True)
                ins.then_inc(S("yc_done"), 1)
                if tb == 0:
                    for q in range(4):
                        hd = slice(head(b, q) * RN, (head(b, q) + 1) * RN)
                        dst = PS[p + 1][rows, q * RN:(q + 1) * RN]
                        pe.matmul(dst, Btok[:, 0, hd], Us[:, b % 2, q * RN:(q + 1) * RN], start=True, stop=False)
                        ins = pe.matmul(dst, Btok[:, 1, hd], VR[:, 0, hd], start=False, stop=True)
                    ins.then_inc(S("state_done"), 1)

            part = {"gram": gram, "z": z_part, "u": u_part, "y": y_part}
            start_inverse(0)
            for step in range(24):
                inverse_step(0, step)
            tx_part(0, 23)
            start_inverse(1)
            pe.wait_ge(S("bon_ready"), 4)
            for step in range(24):
                inverse_step(1, step)
                if step % 6 in BESIDE:
                    part[BESIDE[step % 6]](0, step // 6)
            tx_part(1, 23)
            for what, b in SECOND_BLOCK:
                part[what](1, b)
            pe.wait_ge(S("yc_copied"), 8)
            for g in range(4):
                pe.matmul(PS[g][:, :], heads_ones, Yc[:, 2 * g:2 * g + 2].rearrange("p c t -> p (c t)"),
                          start=True, stop=True).then_inc(S("gnsum_done"), 1)
            for c in range(DC):
                pe.wait_ge(S("gnsq_ready"), c // 2 + 1)
                ins = half_sums(PS[4][0:RH, 0:T], GQ[:, c], c)
            ins.then_inc(S("gnvar_done"), 1)
            pe.wait_ge(S("gninv_ready"), 1)
            pe.wait_ge(S("head_rows_made"), 2)
            for c in range(DC):
                wait(pe, S("gn_scaled"), c - 2)
                spread_halves(PS[5 + c % 3][:, 0:T], head_rows_y, inv[0:RH, 0], c).then_inc(S("gn_spread"), 1)
            out_layer("rw_out", OH, OL, 4)
            first_layer("glu0_up", 5)
            out_layer("glu0_down", GH, GL, 5)
            first_layer("sgu_v", 6)
            pe.wait_ge(S("sgu_landed"), 32)
            transposes(2, lambda g, q: wsr[:, 4 * g + q], (6, 7), S("ws_copied"), S("ws_done"))

            def gate_sums(i, r):
                if 4 * i + r == 0:
                    pe.wait_ge(evac_done, START["sgu_u"])
                    for c in range(DC):
                        ins = pe.matmul(STAT[:, 0:T], ones, Vs_[:, c], start=(c == 0), stop=(c == DC - 1))
                    ins.then_inc(S("sv_sum"), 1)
                if 4 * i + r == 3:
                    pe.wait_ge(S("ws_copied"), 2)
                    for c in range(DC):
                        pe.wait_ge(S("svsq_ready"), c + 1)
                        ins = pe.matmul(PS[6][:, 0:T], ones, SQ[:, c], start=(c == 0), stop=(c == DC - 1))
                    ins.then_inc(S("sv_var"), 1)
            layer("sgu_u", OH, OL, gate_sums, peel_first=True)
            pe.wait_ge(S("vn_ready"), DC)
            transposes(4, lambda g, q: Vs_[:, 4 * (g % 2) + q, (g // 2) * P:(g // 2 + 1) * P], (4, 5, 6, 7),
                       S("vnt_copied"), S("vnt_done"))
            pe.wait_ge(S("vnt_copied"), 4)
            pe.wait_ge(S("wsT_ready"), 1)
            for g in range(DC):
                wait(pe, S("sgu_used"), g - 1)
                for n in range(2):
                    ins = pe.matmul(PS[6 + g % 2][:, n * P:(n + 1) * P], VNT[:, n, g], wsT[:, g], start=True, stop=True)
                ins.then_inc(S("spatial_done"), 1)
            out_layer("sgu_out", OH, OL, 6)
            first_layer("glu1_up", 7)
            out_layer("glu1_down", GH, GL, 7)

        @block.scalar
        def _(act):
            def weights_hi(name, i, r, kt):
                u = START[name] + 4 * i + r + LEAD
                s = (r + LEAD) % SLOTS
                act.wait_ge(raw_landed[s], 16 * (START[name] // 4 + (r + LEAD) // SLOTS + 1) + 16 * i)
                wait(act, mm_done, u - 3)
                act.activation(hi[:, s, 0:kt * P], raw[:, s, 0:kt * P], ACT.Copy).then_inc(hi_made, 1)

            def mod_sum(m, s, n):
                act.wait_ge(S("mod_product"), n + 1)
                act.activation(modraw[:, s], modraw[:, s], ACT.Copy, accum_out=mod_sums[:, ds(m, 1)]).then_inc(mod_done, 1)

            def layer(name, evacuate, peel_first=False):
                start, kt, nxt = START[name], TILES[name], next_tiles(name)

                def body(i, last):
                    for r in range(SLOTS):
                        if not (last and r >= LEAD):
                            weights_hi(name, i, r, kt)
                        elif nxt:
                            weights_hi(name, i, r, nxt)
                        evacuate(i, r, start + 4 * i + r)
                        if name == "conv_up":
                            for m, s, _ in riders(name, i, r):
                                mod_sum(m, s, m - SHARED[name])
                        elif name == "ffn0_up" and r % 2 == 0 and not (isinstance(i, int) and i == r == 0):
                            for m, s, _ in riders(name, i, 1) if r else riders(name, i - 1, 3):
                                mod_sum(m, s, m - SHARED[name])
                bodies(act, name, body, peel_first=peel_first or start == 0, peel_last=(nxt != kt or start == 0))

            def copy_out(dst, func=ACT.Copy, b=None):
                def evacuate(i, r, u):
                    act.wait_ge(mm_done, u + 1)
                    c = 4 * i + r
                    o = dst[:].rearrange("p c t -> p (c t)")[:, ds(T * c, T)]
                    if b is None:
                        ins = act.activation(o, PS[r][:, 0:T], func)
                    else:
                        ins = act.activation(o, PS[r][:, 0:T], func, bias=par_sb[:, ds(COL[b[0]] + b[1] + c, 1)])
                    ins.then_inc(evac_done, 1)
                return evacuate

            flatY, flatSQ = (x[:].rearrange("p c t -> p (c t)") for x in (Y, SQ))

            def with_square(down, biased=False):
                act.preload_act_table(ACT.Sqrt)

                def evacuate(i, r, u):
                    if down and r % 2 == 0:
                        return
                    act.wait_ge(mm_done, u + 1)
                    c = 2 * i + r // 2 if down else 4 * i + r
                    src = PS[r - 1 if down else r][:, 0:T]
                    if biased:
                        b = par_sb[:, ds(COL["cm_b2"] + c, 1)]
                        act.activation(flatSQ[:, ds(T * c, T)], src, ACT.Square, bias=b).then_inc(S("ysq_ready"), 1)
                        act.activation(flatY[:, ds(T * c, T)], src, ACT.Identity, bias=b).then_inc(evac_done, 1)
                    else:
                        act.activation(flatSQ[:, ds(T * c, T)], src, ACT.Square).then_inc(S("ysq_ready"), 1)
                        act.activation(flatY[:, ds(T * c, T)], src, ACT.Copy).then_inc(evac_done, 2 if down else 1)
                return evacuate

            def take_root(dst, sums, mean, e, summed, count, done):
                act.wait_ge(summed, count)
                act.activation(dst, sums, ACT.Sqrt, scale=mean, bias=e).then_inc(done, 1)

            def scaled_hi(n, gain):
                for c in range(DC):
                    wait_x(act, n - 1, c)
                    act.activation(OH[:, c], X[:, c], ACT.Copy, scale=gain(c)).then_inc(S("oh_ready"), 1)
                    act.activation(Y[:, c], X[:, c], ACT.Square).then_inc(S("xsq_ready"), 1)

            def late_root(n):
                take_root(root[:, 1], STAT[:, T:2 * T], 1 / D, eps, S("xstat_done"), n + 1, S("xroot_ready"))

            def residual(n):
                take_root(root[:, 0], STAT[:, 0:T], 1 / D, eps, S("ystat_done"), n + 1, S("yroot_ready"))

            def x_root(n):
                for c in range(DC):
                    if n:
                        wait_x(act, n - 1, c)
                    act.activation(SQ[:, c], X[:, c], ACT.Square).then_inc(S("xsq_ready"), 1)
                take_root(root[:, 1], STAT[:, T:2 * T], 1 / D, eps, S("xstat_done"), n + 1, S("xroot_ready"))

            def norm(n, shifts=()):
                if n:
                    x_root(n)
                for dst, shift, base in shifts:
                    for c in range(DC):
                        act.wait_ge(S("ht_ready"), base + c + 1)
                        if shift is None:
                            ins = act.activation(dst[:, c], HT[:, c], ACT.Copy)
                        else:
                            ins = act.activation(dst[:, c], HT[:, c], ACT.Identity, bias=mods[:, shift + c:shift + c + 1])
                        ins.then_inc(S("oh_ready"), 1)

            pair0 = {n: FC * k for k, n in enumerate(UP)}
            flatpar = par_sb

            def conv_ffn_up(name, l):
                def evacuate(i, r, u):
                    q, kind = r // 2, r % 2
                    pair = pair0[name] + 2 * i + q
                    w = COL["ffn_dw"] + (3 * l + 2) * 2 * FC + kind * FC + 2 * i + q
                    b = COL["ffn_dwb"] + l * 2 * FC + kind * FC + 2 * i + q
                    act.wait_ge(mm_done, u + 1)
                    wait(act, S("prod_made"), pair - 1)
                    act.activation(tmp[:, kind, q], PS[r][:, 0:T], ACT.Identity, scale=flatpar[:, ds(w, 1)],
                                   bias=flatpar[:, ds(b, 1)]).then_inc(S("tap2_made"), 1)
                    if kind == 1:
                        act.wait_ge(evac_done, u)
                        act.activation(tmp[:, 2, q], tmp[:, 0, q], ACT.Silu).then_inc(S("silu_made"), 1)
                act.preload_act_table(ACT.Silu)
                if name in RIDES:
                    act.wait_ge(mod_done, RIDES[name][0])
                layer(name, evacuate, peel_first=(l == 0))

            def glu_up(name, n):
                def evacuate(i, r, u):
                    q = r // 2
                    pair = pair0[name] + 2 * i + q
                    if r % 2:
                        if isinstance(i, int) and i == 0 and r == 1:
                            late_root(n)
                            act.preload_act_table(ACT.Silu)
                        act.wait_ge(S("gate_scaled"), pair + (1 - pair0["glu0_up"]))
                        act.activation(tmp[:, 2, q], tmp[:, 0, q], ACT.Silu).then_inc(S("silu_made"), 1)
                layer(name, evacuate, peel_first=True)

            act.wait_ge(S("c_landed"), 16)
            act.activation(cond[:], cond[:], ACT.Silu).then_inc(S("cond_ready"), 1)
            act.wait_ge(par_landed, 16)
            act.wait_ge(x_landed, 16)
            act.wait_ge(con_landed, 16)
            x_root(0)
            for s in range(LEAD):
                act.wait_ge(raw_landed[s], 16)
                act.activation(hi[:, s, 0:KT * P], raw[:, s, 0:KT * P], ACT.Copy).then_inc(hi_made, 1)
            norm(0, [(OH, 0, 0)])

            def diagonals(c, q):
                wait(act, S("taps_done"), c - 1)
                for j in range(PE_TAPS):
                    ins = act.activation(diags[:, q, j], ident, ACT.Copy, scale=par_sb[:, ds(COL["cm_dw"] + j * DC + c, 1)])
                ins.then_inc(S("diags_made"), 1)

            diagonals(0, 0)

            def conv_up(i, r, u):
                if r % 2:
                    act.wait_ge(mm_done, u + 1)
                    c = 2 * i + r // 2
                    wait(act, evac_done, START["conv_up"] + 4 * i + r - 3)
                    act.activation(tmp[:, 0, r // 2], PS[r][:, 0:T], ACT.Sigmoid,
                                   bias=par_sb[:, ds(COL["cm_b1"] + DC + c, 1)]).then_inc(S("glu_gate"), 1)
                    if not (isinstance(i, int) and c == DC - 1):
                        diagonals(c + 1, (r // 2 + 1) % 2)
            act.preload_act_table(ACT.Sigmoid)
            act.wait_ge(mod_done, MOD_START)
            layer("conv_up", conv_up)
            for c in range(DC):
                act.wait_ge(S("cv_centred"), c + 1)
                act.activation(SQ[:, c], cv[:, c], ACT.Square).then_inc(S("cvsq_ready"), 1)
            take_root(root[:, 0], PS[6][:, 0:T], 1 / D, eps, S("cv_var"), 1, S("cvroot_ready"))
            for c in range(DC):
                act.wait_ge(S("cv_scaled"), c + 1)
                act.activation(Y[:, c], cv[:, c], ACT.Silu, bias=col("cm_ln_b", c)).then_inc(S("cv_silu"), 1)
                act.wait_ge(S("cv_silu"), c + 1)
                act.activation(OH[:, c], Y[:, c], ACT.Copy).then_inc(S("oh_ready"), 1)
            layer("conv_down", with_square(False, True))
            residual(0)
            norm(1, [(OH, 24, DC)])
            conv_ffn_up("ffn0_up", 0)
            for m, s, _ in riders("ffn0_up", FC // 2 - 1, 3):
                mod_sum(m, s, m - SHARED["ffn0_up"])
            layer("ffn0_down", with_square(True))
            residual(1)
            scaled_hi(2, lambda c: col("kv_norm_g", c))

            def values_root(i, r, u):
                if 4 * i + r == 1:
                    late_root(2)
            layer("att_v", values_root, peel_first=True)

            def query_hi(c):
                act.wait_ge(S("ht_ready"), 2 * DC + c + 1)
                act.activation(PH[:, c], HT[:, c], ACT.Identity, bias=mods[:, 48 + c:49 + c]).then_inc(S("oh_ready"), 1)

            def queries_hi(i, r, u):
                if 4 * i + r:
                    query_hi(4 * i + r - 1)
            layer("att_k", queries_hi, peel_first=True)
            query_hi(DC - 1)
            act.wait_ge(evac_done, START["att_q"])
            layer("att_q", copy_out(Q))
            act.wait_ge(S("lam_sum"), 1)
            act.activation(small[:, 4:6], PS[5][:, 0:2], ACT.Exp).then_inc(S("lam_exp"), 1)
            NA = 2 * HEADS
            for n in range(NA + 2):
                if n < NA:
                    nk, s = P * (n % 2 + 1), n % 2
                    act.wait_ge(S("att_negmax"), n + 1)
                    wait(act, S("att_probs"), n - 1)
                    for c in range(2):
                        act.activation(pr[:, s, c, 0:nk], ss[:, s, c, 0:nk], ACT.Exp, scale=-1.0,
                                       bias=small[:, 8 + 2 * s + c:9 + 2 * s + c],
                                       accum_out=small[:, 12 + 2 * s + c:13 + 2 * s + c]).then_inc(S("att_exp"), 1)
                if 1 <= n <= NA:
                    m = n - 1
                    nk = P * (m % 2 + 1)
                    act.wait_ge(S("aT_done"), m + 1)
                    wait(act, S("pv_done"), m - 1)
                    act.activation(aT[:, m % 2, 0:nk], PS[4 + m % 2][:, 0:nk], ACT.Copy).then_inc(S("aT_copied"), 1)
                if n >= 2:
                    m = n - 2
                    act.wait_ge(S("pv_done"), m + 1)
                    act.activation(O[:, m // 2, (m % 2) * P:(m % 2 + 1) * P], PS[6 + m % 2][:, 0:P], ACT.Copy
                                   ).then_inc(S("o_copied"), 1)
                    if m % 2:
                        act.wait_ge(S("o_copied"), m + 1)
                        act.activation(SQ[:, m // 2], O[:, m // 2], ACT.Square).then_inc(S("osq_ready"), 1)
            take_root(root[0:HEADS, 0], PS[0][0:HEADS, 0:T], 1 / P, eps[0:HEADS], S("ostat_done"), 1, S("oroot_ready"))
            for c in range(DC):
                act.wait_ge(S("o_normed"), c + 1)
                act.activation(OH[:, c], O[:, c], ACT.Copy).then_inc(S("oh_ready"), 1)
            layer("att_out", with_square(False))
            residual(2)
            norm(3, [(OH, 48 + 24, 3 * DC)])
            conv_ffn_up("ffn1_up", 1)
            layer("ffn1_down", with_square(True))
            residual(3)
            norm(4)

            def mixed_hi(n, dst):
                for c in range(DC):
                    act.wait_ge(S("xt_ready"), DC * n + c + 1)
                    act.activation(dst[:, c], xt[:, c % 4], ACT.Copy).then_inc(S("xh_ready"), 1)
            mixed_hi(0, OH)
            layer("rw_r", copy_out(R_))
            mixed_hi(1, RH2)
            mixed_hi(2, OH)
            act.wait_ge(S("lora1_done"), 1)
            act.activation(root[0:LORA, 0], PS[0][0:LORA, 0:T], ACT.Tanh).then_inc(S("lora1_used"), 1)
            act.wait_ge(S("lora1_done"), 2)
            act.activation(root[LORA:P, 0], PS[1][LORA:P, 0:T], ACT.Copy).then_inc(S("lora1_used"), 1)
            act.wait_ge(S("lora1_done"), 3)
            act.activation(root[:, 1], PS[2][:, 0:T], ACT.Sigmoid).then_inc(S("lora1_used"), 1)
            act.wait_ge(S("lora1_done"), 4)
            act.activation(inv[:, 0], PS[3][:, 0:T], ACT.Sigmoid).then_inc(S("lora1_used"), 1)
            for j in range(3 * DC):
                b, c = divmod(j, DC)
                act.wait_ge(S("lora2_done"), j + 1)
                src = PS[4 + j % 4][:, 0:T]
                if b == 0:
                    ins = act.activation(W_[:, c], src, ACT.Sigmoid, bias=col("w0", c))
                elif b == 1:
                    ins = act.activation(A_[:, c], src, ACT.Sigmoid, bias=col("a0", c))
                else:
                    ins = act.activation(G_[:, c], src, ACT.Copy)
                ins.then_inc(S("lora2_used"), 1)
            def decays(i, r, u):
                copy_out(K_)(i, r, u)
                act.wait_ge(S("cum_ready"), 1)
                js = 2 * (4 * i + r), 2 * (4 * i + r) + 1
                for j in js:
                    act.activation(E1[:, j], cum[:, j], ACT.Exp, scale=-KAPPA, bias=mid[:, 0, j:j + 1]
                                   ).then_inc(S("e1_ready"), 1)
                for j in js:
                    act.wait_ge(S("e1_ready"), j + 1)
                    act.activation(E2[:, j], cum[:, j], ACT.Exp, scale=KAPPA, bias=mid[:, 1, j:j + 1]
                                   ).then_inc(S("e2_ready"), 1)

            def key_norms(i, r, u):
                copy_out(V_)(i, r, u)
                k = 4 * i + r
                act.activation(Kt_[:, k], A_[:, k], ACT.Identity, scale=col("k_a", k), bias=mid_ka[:, k:k + 1]
                               ).then_inc(S("key_scale"), 1)
                if k < 4:
                    act.wait_ge(S("kk_raw"), 2 * k + 2)
                    act.activation(BON[:, 2 * k:2 * k + 2], KK[:, 2 * k:2 * k + 2], ACT.Square).then_inc(S("kksq_ready"), 1)
                if k == 5:
                    act.wait_ge(S("kkstat_done"), 1)
                    act.activation(root[0:RH, 0], PS[4][0:RH, 0:T], ACT.Sqrt).then_inc(S("kkroot_ready"), 1)
            act.preload_act_table(ACT.Exp)
            layer("rw_k", decays, peel_first=True)
            act.preload_act_table(ACT.Sqrt)
            layer("rw_v", key_norms, peel_first=True)
            act.wait_ge(S("bp_ready"), DC)
            for g in range(8):
                act.wait_ge(S("rwt_done"), g + 1)
                if g < 4:
                    dst = VR[:, g // 2, (g % 2) * 512:(g % 2 + 1) * 512]
                else:
                    dst = Btok[:, (g - 4) // 2, (g % 2) * 512:(g % 2 + 1) * 512]
                act.activation(dst, PS[g % 4][:, :], ACT.Copy).then_inc(S("rwt_copied"), 1)

            def flat(x):
                return x.rearrange("p q t -> p (q t)")

            def start_inverse(tb):
                for b in range(4):
                    act.wait_ge(S("t0_done"), 4 * tb + b + 1)
                    act.activation(flat(Tm[:, b]), PS[2 + b % 2][:, :], ACT.Copy).then_inc(S("t0_copied"), 1)

            def x_copy(tb, step):
                n, b = 24 * tb + step, step % 4
                act.wait_ge(S("x_done"), n + 1)
                wait(act, S("tx_done"), n - 1)
                act.activation(flat(Xs[:, b % 2]), PS[b % 2][:, :], ACT.Copy).then_inc(S("x_copied"), 1)

            def z_copy(tb, b):
                n = 4 * tb + b
                act.wait_ge(S("z_done"), n + 1)
                wait(act, S("u_done"), n - 1)
                act.activation(Zs[:, b % 2], PS[bank_set(tb, b) + 3][:, 0:256], ACT.Copy).then_inc(S("z_copied"), 1)

            def u_copy(tb, b):
                n = 4 * tb + b
                act.wait_ge(S("u_done"), n + 1)
                wait(act, S("yc_done"), n - 1)
                wait(act, S("state_done"), min(n - 1, 4))
                act.activation(Us[:, b % 2], PS[bank_set(tb, b) + 3][:, 256:512], ACT.Copy).then_inc(S("u_copied"), 1)

            def y_copy(tb, b):
                act.wait_ge(S("yc_done"), 4 * tb + b + 1)
                rows = slice(RN * (b % 2), RN * (b % 2 + 1))
                act.activation(Yc[rows, 4 * (b // 2):4 * (b // 2) + 4, tb * P:(tb + 1) * P],
                               PS[bank_set(tb, b)][rows, :].rearrange("p (q t) -> p q t", q=4), ACT.Copy
                               ).then_inc(S("yc_copied"), 1)

            part = {"gram": lambda tb, b: None, "z": z_copy, "u": u_copy, "y": y_copy}
            start_inverse(0)
            for step in range(24):
                x_copy(0, step)
            start_inverse(1)
            for step in range(24):
                x_copy(1, step)
                if step % 6 in BESIDE:
                    part[BESIDE[step % 6]](0, step // 6)
            for what, b in SECOND_BLOCK:
                part[what](1, b)
            for g in range(4):
                act.wait_ge(S("gn_centred"), g + 1)
                act.activation(GQ[:, 2 * g:2 * g + 2], Yc[:, 2 * g:2 * g + 2], ACT.Square).then_inc(S("gnsq_ready"), 1)
            take_root(root[0:RH, 0], PS[4][0:RH, 0:T], 1 / RN, gn_eps[0:RH], S("gnvar_done"), 1, S("gnroot_ready"))
            for c in range(DC):
                act.wait_ge(S("yg_ready"), c + 1)
                act.activation(OH[:, c], Yc[:, c], ACT.Copy).then_inc(S("oh_ready"), 1)
            layer("rw_out", with_square(False))
            residual(4)
            scaled_hi(5, lambda c: col("norm_g2", 2 * DC + c))
            glu_up("glu0_up", 5)
            layer("glu0_down", with_square(True))
            residual(5)
            scaled_hi(6, lambda c: col("norm_g2", 4 * DC + c))

            def gelu_out(dst, first, k):
                act.wait_ge(S("gelu_input"), first + k + 1)
                act.activation(dst[:, k], tmp[:, k % 4, 0], ACT.Gelu, bias=col("sgu_b_in", (DC if dst is Vs_ else 0) + k)
                               ).then_inc(evac_done, 1)

            def gating_out(i, r, u):
                k = 4 * i + r
                if k == 1:
                    late_root(6)
                    gelu_out(Vs_, 0, 0)
                if k:
                    gelu_out(Vs_, 0, k)
            layer("sgu_v", gating_out, peel_first=True)

            def gate_norm(i, r, u):
                k = 4 * i + r
                gelu_out(Us_, DC, k)
                if k in (1, 2):
                    for c in range(4 * (k - 1), 4 * (k - 1) + 4):
                        act.wait_ge(S("sv_centred"), c + 1)
                        act.activation(SQ[:, c], Vs_[:, c], ACT.Square).then_inc(S("svsq_ready"), 1)
                if k == 4:
                    take_root(root[:, 0], PS[6][:, 0:T], 1 / D, ln_eps, S("sv_var"), 1, S("svroot_ready"))
                if k in (5, 6):
                    for c in range(4 * (k - 5), 4 * (k - 5) + 4):
                        act.wait_ge(S("v_scaled"), c + 1)
                        act.activation(Vs_[:, c], Vs_[:, c], ACT.Identity, bias=col("sgu_ln_b", c)).then_inc(S("vn_ready"), 1)
            layer("sgu_u", gate_norm, peel_first=True)
            for g in range(4):
                act.wait_ge(S("vnt_done"), g + 1)
                act.activation(VNT[:, g // 2, 4 * (g % 2):4 * (g % 2) + 4].rearrange("p g c -> p (g c)"),
                               PS[4 + g][:, :], ACT.Copy).then_inc(S("vnt_copied"), 1)
            for c in range(DC):
                act.wait_ge(S("us_ready"), c + 1)
                act.activation(OH[:, c], Us_[:, c], ACT.Copy).then_inc(S("oh_ready"), 1)
            layer("sgu_out", with_square(False))
            residual(6)
            scaled_hi(7, lambda c: col("norm_g2", 6 * DC + c))
            glu_up("glu1_up", 7)
            layer("glu1_down", with_square(True))
            residual(7)

        @block.vector
        def _(dve):
            chain = Chain(dve, S("dve_chain"))
            stt = dve.scalar_tensor_tensor

            def weights_lo(name, i, r, kt):
                u = START[name] + 4 * i + r + LEAD
                s = (r + LEAD) % SLOTS
                dve.wait_ge(hi_made, u + 1)
                dve.tensor_tensor(lo[:, s, 0:kt * P], raw[:, s, 0:kt * P], hi[:, s, 0:kt * P].bitcast(F32), ALU.subtract
                                  ).then_inc(lo_made, 1)

            def mod_unit(m, s, landed):
                dve.wait_ge(mod_landed[s], 16 * landed)
                stt(out=modraw[:, s], in0=modraw[:, s], scalar=1.0, in1=cond[:], op0=ALU.mult, op1=ALU.mult,
                    accum_out=mod_sums[:, ds(m, 1)]).then_inc(mod_done, 1)

            def layer(name, evacuate=None, peel_all=False, peel_first=False):
                start, kt, nxt = START[name], TILES[name], next_tiles(name)

                def body(i, last):
                    for r in range(SLOTS):
                        if not (last and r >= LEAD):
                            weights_lo(name, i, r, kt)
                        elif nxt:
                            weights_lo(name, i, r, nxt)
                        if evacuate:
                            evacuate(i, r, start + 4 * i + r)
                        if name in RIDES and name not in SHARED and not (name == "conv_down" and i):
                            for m, s, landed in riders(name, i, r):
                                mod_unit(m, s, landed)
                if peel_all:
                    for i in range(COUNT[name] // SLOTS):
                        body(i, i == COUNT[name] // SLOTS - 1)
                else:
                    bodies(dve, name, body, peel_first=peel_first, peel_last=(nxt != kt))

            def invert(dst, src, rooted, count):
                dve.wait_ge(rooted, count)
                chain.link(dve.reciprocal(dst, src))

            def residual(n, gain, next_gain=None):
                invert(inv[:, 0], root[:, 0], S("yroot_ready"), n + 1)
                for c in range(DC):
                    stt(out=Y[:, c], in0=Y[:, c], scalar=gain(c), in1=inv[:, 0], op0=ALU.mult, op1=ALU.mult
                        ).then_inc(S("y_scaled"), 1)
                    if c in ADDED_BY_VECTOR:
                        dve.wait_ge(S("y_scaled"), DC * n + c + 1)
                        dve.tensor_tensor(X[:, c], X[:, c], Y[:, c], ALU.add).then_inc(S("x_added_vector"), 1)
                    if next_gain and c >= 2:
                        scaled_lo(c - 2, next_gain)
                if next_gain:
                    for c in (DC - 2, DC - 1):
                        scaled_lo(c, next_gain)

            oh_count = [0]

            def scaled_lo(c, gain):
                oh_count[0] += 1
                dve.wait_ge(S("oh_ready"), oh_count[0])
                stt(out=OL[:, c], in0=X[:, c], scalar=gain(c), in1=OH[:, c].bitcast(F32), op0=ALU.mult, op1=ALU.subtract
                    ).then_inc(operand_ready, 1)

            def late_inverse(n):
                invert(inv[:, 1], root[:, 1], S("xroot_ready"), n + 1)

            def low_part(src, h, l, c, shift=None):
                oh_count[0] += 1
                dve.wait_ge(S("oh_ready"), oh_count[0])
                if shift is None:
                    ins = dve.tensor_tensor(l[:, c], src[:, c], h[:, c].bitcast(F32), ALU.subtract)
                else:
                    ins = stt(out=l[:, c], in0=src[:, c], scalar=mods[:, shift + c:shift + c + 1],
                              in1=h[:, c].bitcast(F32), op0=ALU.add, op1=ALU.subtract)
                ins.then_inc(operand_ready, 1)

            def norm(n, uses):
                if n:
                    invert(inv[:, 1], root[:, 1], S("xroot_ready"), n + 1)
                for gain, h, l, shift in uses:
                    for c in range(DC + 2):
                        if c < DC:
                            stt(out=HT[:, c], in0=X[:, c], scalar=gain(c), in1=inv[:, 1], op0=ALU.mult, op1=ALU.mult
                                ).then_inc(S("ht_ready"), 1)
                        if c >= 2 and h is not None:
                            low_part(HT, h, l, c - 2, shift)

            def par_gain(name, n):
                return lambda c: col(name, n + c)

            def own_gain(tile, n):
                return lambda c: tile[:, n, c:c + 1]

            def modulation(first, count, done):
                dve.wait_ge(mod_done, done)
                chain.link(dve.tensor_tensor(mods[:, first:first + count], mod_sums[:, first:first + count],
                                             cols("mod_b", first, count), ALU.add))

            def scale_gain(n, which):
                l, k = divmod(n, 2)
                chain.link(stt(out=ngain[:, n], in0=mods[:, 48 * l + 8 + 24 * k:48 * l + 16 + 24 * k], scalar=1.0,
                               in1=cols("norm_g", which, DC), op0=ALU.add, op1=ALU.mult))

            def gate_gain(n, which):
                l, k = divmod(n, 2)
                chain.link(dve.tensor_tensor(rgain[:, n], mods[:, 48 * l + 16 + 24 * k:48 * l + 24 + 24 * k],
                                             cols("norm_g", which, DC), ALU.mult))

            dve.wait_ge(S("cond_ready"), 1)
            for m in range(MOD_START - SLOTS):
                mod_unit(m, m % SLOTS, m // SLOTS + 1)
            dve.wait_ge(par_landed, 16)
            dve.wait_ge(x_landed, 16)
            chain.link(dve.tensor_tensor(small[:, 2:3], col("lam", 0), col("lam", 1), ALU.mult))
            chain.link(dve.tensor_tensor(small[:, 3:4], col("lam", 2), col("lam", 3), ALU.mult))
            dve.memset(upad[:, :, 0:PAD], 0.0).then_inc(S("upad_zero"), 1)
            invert(inv[:, 1], root[:, 1], S("xroot_ready"), 1)
            for s in range(LEAD):
                dve.wait_ge(hi_made, s + 1)
                dve.tensor_tensor(lo[:, s, 0:KT * P], raw[:, s, 0:KT * P], hi[:, s, 0:KT * P].bitcast(F32), ALU.subtract
                                  ).then_inc(lo_made, 1)
            for m in range(MOD_START - SLOTS, MOD_START):
                mod_unit(m, m % SLOTS, m // SLOTS + 1)
            modulation(0, 16, 16)
            scale_gain(0, 0)
            norm(0, [(own_gain(ngain, 0), OH, OL, 0)])
            def conv_up(i, r, u):
                if r % 2 == 0:
                    return
                c = 2 * i + r // 2
                dve.wait_ge(S("glu_gate"), c + 1)
                stt(out=upad[:, c, PAD:], in0=PS[r - 1][:, 0:T], scalar=col("cm_b1", c), in1=tmp[:, 0, r // 2],
                    op0=ALU.add, op1=ALU.mult).then_inc(evac_done, 2)
                dve.wait_ge(evac_done, u + 1)
                if c == 0:
                    dve.wait_ge(S("upad_zero"), 1)
                sums = cv[:, c], tmp[:, 1, r // 2]
                first = PE_TAPS
                chain.add(dve.tensor_scalar(sums[0], upad[:, c, first:first + T], col("cm_dw", first * DC + c),
                                            col("cm_dwb", c), ALU.mult, ALU.add))
                chain.add(dve.tensor_scalar(sums[1], upad[:, c, first + 1:first + 1 + T],
                                            col("cm_dw", (first + 1) * DC + c), None, ALU.mult))
                for j in range(first + 2, TAPS):
                    to = sums[(j - first) % 2]
                    chain.sync(1)
                    chain.add(stt(out=to, in0=upad[:, c, j:j + T], scalar=col("cm_dw", j * DC + c), in1=to,
                                  op0=ALU.mult, op1=ALU.add))
                chain.sync()
                chain.link(dve.tensor_tensor(cv[:, c], cv[:, c], sums[1], ALU.add))
                dve.wait_ge(S("taps_done"), c + 1)
                dve.tensor_tensor(cv[:, c], PS[5 + 2 * (r // 2)][:, 0:T], cv[:, c], ALU.add).then_inc(S("cv_ready"), 1)

            layer("conv_up", conv_up, peel_all=True)
            dve.wait_ge(S("cv_sum"), 1)
            for c in range(DC):
                stt(out=cv[:, c], in0=STAT[:, 0:T], scalar=-1 / D, in1=cv[:, c], op0=ALU.mult, op1=ALU.add
                    ).then_inc(S("cv_centred"), 1)
            invert(inv[:, 0], root[:, 0], S("cvroot_ready"), 1)
            for c in range(DC):
                stt(out=cv[:, c], in0=cv[:, c], scalar=col("cm_ln_g", c), in1=inv[:, 0], op0=ALU.mult, op1=ALU.mult
                    ).then_inc(S("cv_scaled"), 1)
                if c >= 3:
                    low_part(Y, OH, OL, c - 3)
            for c in range(DC - 3, DC):
                low_part(Y, OH, OL, c)
            modulation(16, 32, 48)
            scale_gain(1, 2 * DC)
            gate_gain(0, DC)
            gate_gain(1, 3 * DC)
            layer("conv_down", peel_all=True)
            residual(0, own_gain(rgain, 0))
            norm(1, [(own_gain(ngain, 1), OH, OL, 24)])
            dve.wait_ge(S("rows_done"), 1)
            dve.tensor_tensor(xt[0:HEADS].rearrange("p a t -> p (a t)")[:, 0:384], PS[6][0:HEADS, 0:384],
                              con_sb[0:HEADS, CCOL["future"]:CCOL["future"] + 384], ALU.add).then_inc(S("bias_rows"), 1)

            pair0 = {n: FC * k for k, n in enumerate(UP)}

            def product(q, pair, a, b):
                dve.wait_ge(S("silu_made"), pair + 1)
                wait(dve, S("hidden_split"), pair - 1)
                dve.tensor_tensor(tmp[:, 3, q], a, b, ALU.mult).then_inc(S("prod_made"), 1)

            def conv_ffn_up(name, l):
                units0 = 2 * FC * l

                def evacuate(i, r, u):
                    q, kind = r // 2, r % 2
                    unit = units0 + 4 * i + r
                    t = tmp[:, kind, q]
                    w = COL["ffn_dw"] + 3 * l * 2 * FC + kind * FC + 2 * i + q
                    dve.wait_ge(S("tap2_made"), unit + 1)
                    stt(out=t[:, 1:], in0=PS[r][:, 0:T - 1], scalar=par_sb[:, ds(w + 2 * FC, 1)], in1=t[:, 1:],
                        op0=ALU.mult, op1=ALU.add).then_inc(S("tap1_made"), 1)
                    dve.wait_ge(S("tap1_made"), unit + 1)
                    stt(out=t[:, 2:], in0=PS[r][:, 0:T - 2], scalar=par_sb[:, ds(w, 1)], in1=t[:, 2:],
                        op0=ALU.mult, op1=ALU.add).then_inc(evac_done, 1)
                    if kind == 1:
                        dve.wait_ge(evac_done, u + 1)
                        product(q, pair0[name] + 2 * i + q, tmp[:, 2, q], tmp[:, 1, q])
                layer(name, evacuate, peel_first=(l == 0))

            def glu_up(name, n):
                def evacuate(i, r, u):
                    q = r // 2
                    if r % 2 == 0:
                        return
                    if isinstance(i, int) and i == 0 and r == 1:
                        late_inverse(n)
                    pair = pair0[name] + 2 * i + q
                    dve.wait_ge(mm_done, u + 1)
                    dve.tensor_tensor(tmp[:, 0, q], PS[r - 1][:, 0:T], inv[:, 1], ALU.mult).then_inc(S("gate_scaled"), 1)
                    dve.tensor_tensor(tmp[:, 1, q], PS[r][:, 0:T], inv[:, 1], ALU.mult).then_inc(evac_done, 2)
                    dve.wait_ge(evac_done, u + 1)
                    product(q, pair, tmp[:, 2, q], tmp[:, 1, q])
                layer(name, evacuate, peel_first=True)

            conv_ffn_up("ffn0_up", 0)
            dve.wait_ge(mod_done, 9 * DC)
            layer("ffn0_down")
            modulation(48, 24, 72)
            scale_gain(2, 4 * DC)
            gate_gain(2, 5 * DC)
            residual(1, own_gain(rgain, 1), par_gain("kv_norm_g", 0))

            def normed_out(dst, k):
                dve.wait_ge(mm_done, START["att_v" if dst is V else "att_k"] + k + 1)
                dve.tensor_tensor(dst[:, k], PS[k % 4][:, 0:T], inv[:, 1], ALU.mult).then_inc(evac_done, 1)

            def values_out(i, r, u):
                k = 4 * i + r
                if k == 1:
                    late_inverse(2)
                    normed_out(V, 0)
                if k:
                    normed_out(V, k)
            layer("att_v", values_out, peel_all=True)
            modulation(72, 24, 96)
            scale_gain(3, 6 * DC)
            gate_gain(3, 7 * DC)

            def queries_input(i, r, u):
                c = 4 * i + r
                normed_out(K, c)
                stt(out=HT[:, c], in0=X[:, c], scalar=ngain[:, 2, c:c + 1], in1=inv[:, 1], op0=ALU.mult, op1=ALU.mult
                    ).then_inc(S("ht_ready"), 1)
                if c >= 2:
                    low_part(HT, PH, PL, c - 2, 48)
            layer("att_k", queries_input, peel_all=True)
            for c in (DC - 2, DC - 1):
                low_part(HT, PH, PL, c, 48)
            for g in range(4):
                dve.wait_ge(S("vt_done"), g + 1)
                dve.tensor_copy(VT[:, g // 2, (g % 2) * 512:(g % 2 + 1) * 512], PS[4 + g][:, :]
                                ).then_inc(S("vt_copied"), 1)

            def turn_bias(i, r, u):
                if 4 * i + r == COUNT["att_q"] - 1:
                    dve.wait_ge(S("bias_landed"), 16)
                    chain.link(dve.tensor_scalar(bias[:], biasrev[:, :, ::-1], -1.0, None, ALU.mult))
            layer("att_q", turn_bias, peel_all=True)
            dve.wait_ge(S("lam_exp"), 1)
            chain.link(dve.tensor_tensor(small[:, 6:7], small[:, 5:6], small[:, 4:5], ALU.subtract))
            dve.tensor_scalar(small[:, 7:8], small[:, 6:7], -LAMBDA_INIT, None, ALU.add).then_inc(S("lam_ready"), 1)
            dve.wait_ge(S("lam_ready"), 1)
            neg_lam = small[:, 7:8]
            NA = 2 * HEADS
            rs = small[:, 24:28]
            for n in range(NA + 1):
                if n < NA:
                    h, qb, s = n // 2, n % 2, n % 2
                    nk = P * (qb + 1)
                    wait(dve, S("att_exp"), 2 * n - 2)
                    dve.wait_ge(S("att_scores"), n + 1)
                    for c in range(2):
                        ins = stt(out=ss[:, s, c, 0:nk], in0=PS[2 * s + c][:, 0:nk], scalar=-HEAD_DIM ** -0.5,
                                  in1=bias[:, h, T - nk:T], op0=ALU.mult, op1=ALU.add)
                    ins.then_inc(S("att_scaled"), 1)
                    dve.wait_ge(S("att_scaled"), n + 1)
                    dve.tensor_reduce(small[:, 8 + 2 * s:10 + 2 * s], ss[:, s, :, 0:nk], AX_X, ALU.min
                                      ).then_inc(S("att_negmax"), 1)
                if n >= 1:
                    m, s = n - 1, (n - 1) % 2
                    nk = P * (s + 1)
                    dve.wait_ge(S("att_exp"), 2 * m + 2)
                    chain.link(dve.reciprocal(rs[:, 2 * s:2 * s + 2], small[:, 12 + 2 * s:14 + 2 * s]))
                    wait(dve, S("aT_done"), m - 1)
                    chain.link(dve.tensor_scalar(aa[:, s, 0:nk], pr[:, s, 1, 0:nk], rs[:, 2 * s + 1:2 * s + 2], neg_lam,
                                                 ALU.mult, ALU.mult))
                    stt(out=aa[:, s, 0:nk], in0=pr[:, s, 0, 0:nk], scalar=rs[:, 2 * s:2 * s + 1], in1=aa[:, s, 0:nk],
                        op0=ALU.mult, op1=ALU.add).then_inc(S("att_probs"), 1)
            chain.link(dve.tensor_scalar(small[:, 0:1], col("subln_g"), 1.0 - LAMBDA_INIT, None, ALU.mult))
            dve.wait_ge(S("oroot_ready"), 1)
            dve.reciprocal(inv[0:HEADS, 0], root[0:HEADS, 0]).then_inc(S("oinv_ready"), 1)
            for c in range(DC + 2):
                if c < DC:
                    dve.wait_ge(S("o_spread"), c + 1)
                    stt(out=O[:, c], in0=O[:, c], scalar=small[:, 0:1], in1=PS[1 + c % 3][:, 0:T], op0=ALU.mult, op1=ALU.mult
                        ).then_inc(S("o_normed"), 1)
                if c >= 2:
                    low_part(O, OH, OL, c - 2)
            layer("att_out")
            residual(2, own_gain(rgain, 2))
            norm(3, [(own_gain(ngain, 3), OH, OL, 48 + 24)])
            conv_ffn_up("ffn1_up", 1)
            layer("ffn1_down")
            residual(3, own_gain(rgain, 3))
            norm(4, [(par_gain("norm_g2", 0), None, None, None)])

            def mixed(dst, j, c, sem):
                stt(out=dst, in0=XX[:, c], scalar=col("mix", DC * j + c), in1=H[:, c], op0=ALU.mult, op1=ALU.add
                    ).then_inc(sem, 1)

            def mixed_operand(j, n, h, l):
                for c in range(DC + 2):
                    if c < DC:
                        dve.wait_ge(S("xx_ready"), c + 1)
                        dve.wait_ge(operand_ready, ready_at["rw_r"] + DC * n + c - 3)
                        mixed(xt[:, c % 4], j, c, S("xt_ready"))
                    if c >= 2:
                        dve.wait_ge(S("xh_ready"), DC * n + c - 1)
                        dve.tensor_tensor(l[:, c - 2], xt[:, (c - 2) % 4], h[:, c - 2].bitcast(F32), ALU.subtract
                                          ).then_inc(operand_ready, 1)

            def low_rank_inputs(i, r, u):
                for n in range(3):
                    mixed(xs[n][:, 4 * i + r], 3 + n, 4 * i + r, S("xs_ready"))

            mixed_operand(0, 0, OH, OL)
            layer("rw_r", low_rank_inputs, peel_all=True)
            mixed_operand(1, 1, RH2, RL2)
            dve.wait_ge(mm_done, START["rw_k"])
            mixed_operand(2, 2, OH, OL)
            dve.wait_ge(S("lora2_used"), 3 * DC)
            chain.link(dve.memset(cum[:, :, 0:1], 0.0))
            for j in range(2 * DC):
                chain.add(dve.tensor_tensor_scan(cum[:, j, 1:P + 1], ones, W_[:, j // 2, (j % 2) * P:(j % 2 + 1) * P], 0.0,
                                                 ALU.mult, ALU.add))
            chain.add(dve.tensor_scalar(mid_ka[:], cols("k_a", 0, DC), -1.0, 1.0, ALU.mult, ALU.add))
            chain.sync()
            chain.add(dve.tensor_scalar(mid[:, 0], cum[:, :, P // 2], KAPPA, None, ALU.mult))
            chain.add(dve.tensor_scalar(mid[:, 1], cum[:, :, P // 2], -KAPPA, None, ALU.mult))
            chain.sync()
            dve.sem_inc(S("cum_ready"), 1)
            layer("rw_k")

            def blocks(x, c):
                return x[:, c].rearrange("p (b t) -> p b t", b=2)

            def normalise(c):
                dve.wait_ge(S("kk_spread"), c + 1)
                dve.tensor_tensor(KK[:, c], PS[5 + c % 3][:, 0:T], KK[:, c], ALU.mult).then_inc(S("kk_ready"), 1)

            def scale_key(c):
                dve.wait_ge(S("kk_raw"), c + 1)
                dve.wait_ge(S("key_scale"), c + 1)
                dve.tensor_tensor(K_[:, c], K_[:, c], Kt_[:, c], ALU.mult).then_inc(S("k_scaled"), 1)

            def keys(i, r, u):
                k = 4 * i + r
                if k:
                    scale_key(k - 1)
                if k == 5:
                    dve.wait_ge(S("kkroot_ready"), 1)
                    chain.link(dve.tensor_scalar(root[0:RH, 0], root[0:RH, 0], 1e-12, None, ALU.max))
                    dve.reciprocal(inv[0:RH, 0], root[0:RH, 0]).then_inc(S("kkinv_ready"), 1)
                if k == 7:
                    for c in range(4):
                        normalise(c)
            layer("rw_v", keys, peel_all=True)
            scale_key(7)
            for c in range(4, DC):
                normalise(c)
            dve.wait_ge(S("e2_ready"), 2 * DC)
            chain.add(dve.tensor_tensor(dec[:], E1[:, 0::2, P], E2[:, 1::2, 0], ALU.mult))
            dve.wait_ge(evac_done, START["rw_out"])
            dve.wait_ge(S("kk_ready"), DC)
            for c in range(DC):
                chain.add(stt(out=AR[:, c, :, 0], in0=blocks(KK, c), scalar=-1.0, in1=E1[:, 2 * c:2 * c + 2, 0:P],
                              op0=ALU.mult, op1=ALU.mult))
                chain.add(dve.tensor_tensor(AR[:, c, :, 1], blocks(R_, c), E1[:, 2 * c:2 * c + 2, 1:P + 1], ALU.mult))
            dve.wait_ge(S("k_scaled"), DC)
            for c in range(DC):
                stt(out=BON[:, c], in0=R_[:, c], scalar=col("r_k", c), in1=K_[:, c], op0=ALU.mult, op1=ALU.mult
                    ).then_inc(S("bp_ready"), 1)
            chain.sync()
            dve.wait_ge(S("tilde_part"), 2 * DC)
            dve.sem_inc(S("rw_tilde"), 1)

            def flat(x):
                return x.rearrange("p q t -> p (q t)")

            def over_heads(m):
                return m.unsqueeze(1).to_broadcast([P, 4, P])

            def start_inverse(tb):
                for b in range(4):
                    dve.wait_ge(S("at_done"), 4 * tb + b + 1)
                    wait(dve, S("ml_made"), (20 + b + 1) * tb)
                    dve.tensor_tensor(AT[:, b], PS[b % 2][:, :].rearrange("p (q t) -> p q t", q=4),
                                      over_heads(const("before")), ALU.mult).then_inc(S("at_made"), 1)
                for b in range(4):
                    dve.wait_ge(S("tt_part"), 4 * tb + b + 1)
                    dve.tensor_tensor(TT[tb][:, b], TT[tb][:, b], over_heads(ident), ALU.add).then_inc(S("tt0_made"), 1)

            def t_add(tb, step):
                b, w = step % 4, 2 << (step // 4)
                dve.wait_ge(S("tx_done"), 24 * tb + step + 1)
                src = [PS[2 + b % 2][:, 256 * h:256 * h + 256].rearrange("p (m w) -> p m w", w=w) for h in range(2)]
                t, tt = (flat(x[:, b]).rearrange("p (m two w) -> p m two w", two=2, w=w) for x in (Tm, TT[tb]))
                if step < 20:
                    dve.tensor_tensor(t[:, :, 0], src[0], t[:, :, 0], ALU.add)
                dve.tensor_tensor(tt[:, :, 1], src[1], tt[:, :, 1], ALU.add).then_inc(S("t_added"), 1)

            both = con_sb[:, CCOL["before"]:CCOL["before"] + 2 * P].unsqueeze(1).to_broadcast([P, 2, 2 * P])

            def gram_masks(tb, b):
                n, p = 4 * tb + b, bank_set(tb, b)
                dve.wait_ge(S("gram_done"), n + 1)
                wait(dve, S("yc_done"), n - 1)
                for g in range(2):
                    chain.add(dve.tensor_tensor(apk[:, b % 2, 2 * g:2 * g + 2],
                                                PS[p + g][:, :].rearrange("p (q t) -> p q t", q=2), both, ALU.mult))
                dve.tensor_tensor(apb[:, b % 2], PS[p + 2][:, :].rearrange("p (q t) -> p q t", q=4),
                                  over_heads(const("upto")), ALU.mult).then_inc(S("apb_made"), 1)

            def state_out(tb, b):
                if tb:
                    return
                rows = slice(RN * (b % 2), RN * (b % 2 + 1))
                dve.wait_ge(S("state_done"), b + 1)
                first = 8 * (b // 2) + b % 2
                dve.tensor_tensor(SZ[rows, first:first + 7:2],
                                  PS[bank_set(0, b) + 1][rows, 0:4 * RN].rearrange("p (q i) -> p q i", q=4),
                                  dec[rows, 4 * (b // 2):4 * (b // 2) + 4].unsqueeze(2).to_broadcast([RN, 4, RN]),
                                  ALU.mult).then_inc(S("state_made"), 1)

            part = {"gram": gram_masks, "z": lambda tb, b: None, "u": lambda tb, b: None, "y": state_out}
            start_inverse(0)
            for g in range(4):
                dve.wait_ge(S("bpsum_done"), g + 1)
                b = BON[:, 2 * g:2 * g + 2].rearrange("p c t -> p (c t)")
                dve.tensor_tensor(b, PS[4 + g][:, :], V_[:, 2 * g:2 * g + 2].rearrange("p c t -> p (c t)"), ALU.mult
                                  ).then_inc(S("bon_ready"), 1)
            dve.wait_ge(S("rwt_copied"), 4)
            dve.wait_ge(S("bon_ready"), 4)
            chain.link(dve.memset(SZ[:], 0.0))
            for step in range(24):
                t_add(0, step)
            start_inverse(1)
            for step in range(24):
                if step:
                    t_add(1, step - 1)
                if step % 6 in BESIDE:
                    part[BESIDE[step % 6]](0, step // 6)
            t_add(1, 23)
            for what, b in SECOND_BLOCK:
                part[what](1, b)
            for g in range(4):
                dve.wait_ge(S("gnsum_done"), g + 1)
                y = Yc[:, 2 * g:2 * g + 2].rearrange("p c t -> p (c t)")
                stt(out=y, in0=PS[g][:, :], scalar=-1 / RN, in1=y, op0=ALU.mult, op1=ALU.add).then_inc(S("gn_centred"), 1)
            dve.wait_ge(S("gnroot_ready"), 1)
            dve.reciprocal(inv[0:RH, 0], root[0:RH, 0]).then_inc(S("gninv_ready"), 1)
            for c in range(DC + 1):
                if c < DC:
                    dve.wait_ge(S("gn_spread"), c + 1)
                    stt(out=Yc[:, c], in0=Yc[:, c], scalar=col("gn_w", c), in1=PS[5 + c % 3][:, 0:T], op0=ALU.mult,
                        op1=ALU.mult).then_inc(S("gn_scaled"), 1)
                    dve.wait_ge(S("gn_scaled"), c + 1)
                    chain.link(stt(out=Yc[:, c], in0=Yc[:, c], scalar=col("gn_b", c), in1=BON[:, c], op0=ALU.add, op1=ALU.add))
                    dve.tensor_tensor(Yc[:, c], Yc[:, c], G_[:, c], ALU.mult).then_inc(S("yg_ready"), 1)
                if c >= 1:
                    low_part(Yc, OH, OL, c - 1)
            layer("rw_out")
            residual(4, par_gain("norm_g2", DC), par_gain("norm_g2", 2 * DC))
            glu_up("glu0_up", 5)
            layer("glu0_down")
            residual(5, par_gain("norm_g2", 3 * DC), par_gain("norm_g2", 4 * DC))

            def gelu_input(k, start):
                dve.wait_ge(mm_done, start + k + 1)
                dve.wait_ge(evac_done, start + k - 3)
                dve.tensor_tensor(tmp[:, k % 4, 0], PS[k % 4][:, 0:T], inv[:, 1], ALU.mult).then_inc(S("gelu_input"), 1)

            def gating_out(i, r, u):
                k = 4 * i + r
                if k == 1:
                    late_inverse(6)
                    gelu_input(0, START["sgu_v"])
                if k:
                    gelu_input(k, START["sgu_v"])
            layer("sgu_v", gating_out, peel_all=True)
            for g in range(2):
                dve.wait_ge(S("ws_done"), g + 1)
                dve.tensor_copy(wsT[:, 4 * g:4 * g + 4].rearrange("p g i -> p (g i)"), PS[6 + g][:, :]
                                ).then_inc(S("ws_copied"), 1)
            dve.wait_ge(S("ws_copied"), 2)
            dve.memset(wsT[P // 2:P, :, 0:P // 2], 0.0).then_inc(S("wsT_ready"), 1)

            def gate_norm(i, r, u):
                k = 4 * i + r
                gelu_input(k, START["sgu_u"])
                if k == 1:
                    dve.wait_ge(S("sv_sum"), 1)
                    for c in range(DC):
                        stt(out=Vs_[:, c], in0=STAT[:, 0:T], scalar=-1 / D, in1=Vs_[:, c], op0=ALU.mult, op1=ALU.add
                            ).then_inc(S("sv_centred"), 1)
                if k == 4:
                    invert(inv[:, 0], root[:, 0], S("svroot_ready"), 1)
                if k in (5, 6):
                    for c in range(4 * (k - 5), 4 * (k - 5) + 4):
                        stt(out=Vs_[:, c], in0=Vs_[:, c], scalar=col("sgu_ln_w", c), in1=inv[:, 0], op0=ALU.mult, op1=ALU.mult
                            ).then_inc(S("v_scaled"), 1)
            layer("sgu_u", gate_norm, peel_all=True)
            for g in range(DC):
                dve.wait_ge(S("spatial_done"), g + 1)
                t = xt[:, g % 2].rearrange("p (n i) -> p n i", n=2)
                dve.tensor_tensor(t, PS[6 + g % 2][:, 0:T].rearrange("p (n i) -> p n i", n=2),
                                  bsb[:, g].unsqueeze(1).to_broadcast([P, 2, P]), ALU.add).then_inc(S("sgu_used"), 1)
                dve.wait_ge(S("sgu_used"), g + 1)
                dve.tensor_tensor(Us_[:, g], Us_[:, g], xt[:, g % 2], ALU.mult).then_inc(S("us_ready"), 1)
                if g:
                    low_part(Us_, OH, OL, g - 1)
            low_part(Us_, OH, OL, DC - 1)
            layer("sgu_out")
            residual(6, par_gain("norm_g2", 5 * DC), par_gain("norm_g2", 6 * DC))
            glu_up("glu1_up", 7)
            layer("glu1_down")
            residual(7, par_gain("norm_g2", 7 * DC))

        @block.gpsimd
        def _(pool):
            def add_squares(x, ready, n, of_x):
                for c in range(1, DC - 1):
                    pool.wait_ge(ready, DC * n + c + 1)
                    wait(pool, S("sq_added"), squares_added(n, of_x) + c - 1)
                    pool.tensor_tensor(x[:, 0], x[:, 0], x[:, c], ALU.add).then_inc(S("sq_added"), 1)

            def add_up(n):
                add_squares(SQ, S("ysq_ready"), n, False)
                for c in range(DC):
                    if c not in ADDED_BY_VECTOR:
                        pool.wait_ge(S("y_scaled"), DC * n + c + 1)
                        pool.tensor_tensor(X[:, c], X[:, c], Y[:, c], ALU.add).then_inc(S("x_added_gpsimd"), 1)
                if n + 1 in LATE_NORMS:
                    add_squares(Y, S("xsq_ready"), n + 1, True)

            def mod_product(s, landed):
                pool.wait_ge(mod_landed[s], 16 * landed)
                pool.tensor_tensor(modraw[:, s], modraw[:, s], cond[:], ALU.mult).then_inc(S("mod_product"), 1)

            flatH, flatL = (x[:].rearrange("p c t -> p (c t)") for x in (GH, GL))

            pool.wait_ge(S("cond_ready"), 1)
            with pool.Fori(0, COUNT["conv_up"] // SLOTS) as i:
                for r in range(SLOTS):
                    for m, s, landed in riders("conv_up", i, r):
                        mod_product(s, landed)

            def split_hidden(k):
                def step(i, q):
                    pair = FC * k + 2 * i + q
                    pool.wait_ge(S("prod_made"), pair + 1)
                    pool.tensor_copy(flatH[:, ds(2 * T * i + q * T, T)], tmp[:, 3, q]).then_inc(S("hidden_hi"), 1)
                    pool.wait_ge(S("hidden_hi"), pair + 1)
                    pool.tensor_tensor(flatL[:, ds(2 * T * i + q * T, T)], tmp[:, 3, q],
                                       flatH[:, ds(2 * T * i + q * T, T)].bitcast(F32), ALU.subtract
                                       ).then_inc(S("hidden_split"), 1)
                with pool.Fori(0, FC // 2) as i:
                    for q in range(2):
                        if k == 0:
                            for m, s, landed in riders("ffn0_up", i, 2 * q + 1):
                                mod_product(s, landed)
                        step(i, q)

            add_up(0)
            split_hidden(0)
            add_up(1)
            add_up(2)
            split_hidden(1)
            add_up(3)
            for c in range(DC):
                pool.wait_ge(S("ht_ready"), 4 * DC + c + 1)
                pool.tensor_tensor(XX[:, c, 1:], H[:, c, 0:T - 1], H[:, c, 1:], ALU.subtract)
                pool.tensor_scalar(XX[:, c, 0:1], H[:, c, 0:1], -1.0, None, ALU.mult).then_inc(S("xx_ready"), 1)
            pool.wait_ge(operand_ready, ready_at["rw_v"] + DC)
            pool.wait_ge(evac_done, START["rw_v"])
            for c in range(DC):
                pool.tensor_tensor(KK[:, c], K_[:, c], col("k_k", c).to_broadcast([P, T]), ALU.mult).then_inc(S("kk_raw"), 1)

            def make_head_rows(dst):
                pool.tensor_copy(dst[:].rearrange("p (h i) -> p h i", h=RH),
                                 ident[0:RH, 0:RH].unsqueeze(2).to_broadcast([RH, RH, RN])).then_inc(S("head_rows_made"), 1)
            make_head_rows(head_rows_k)
            pool.wait_ge(S("e2_ready"), 2 * DC)

            def blocks(x, c):
                return x[:, c].rearrange("p (b t) -> p b t", b=2)

            def scaled_key(c):
                pool.wait_ge(S("k_scaled"), c + 1)
                pool.tensor_tensor(blocks(Kt_, c), blocks(K_, c), E2[:, 2 * c:2 * c + 2, 1:P + 1], ALU.mult
                                   ).then_inc(S("tilde_part"), 1)
            for c in range(4):
                scaled_key(c)
            for c in range(DC):
                pool.wait_ge(S("kk_ready"), c + 1)
                pool.wait_ge(S("key_scale"), c + 1)
                pool.tensor_tensor(A_[:, c], KK[:, c], A_[:, c], ALU.mult).then_inc(S("ka_ready"), 1)
                pool.wait_ge(S("ka_ready"), c + 1)
                pool.tensor_tensor(blocks(Bt_, c), blocks(A_, c), E2[:, 2 * c:2 * c + 2, 1:P + 1], ALU.mult
                                   ).then_inc(S("tilde_part"), 1)
                if c % 2:
                    scaled_key(4 + c // 2)

            def over_heads(m):
                return m.unsqueeze(1).to_broadcast([P, 4, P])

            for tb in range(2):
                for b in range(4):
                    pool.wait_ge(S("at_made"), 4 * tb + b + 1)
                    pool.tensor_tensor(TT[tb][:, b], AT[:, b], over_heads(const("level0")), ALU.mult).then_inc(S("tt_part"), 1)
                for step in range(24):
                    n, b = 24 * tb + step, step % 4
                    wait(pool, S("x_done"), n - 1)
                    pool.tensor_tensor(ML[:, b % 2], AT[:, b], over_heads(const(f"level{step // 4 + 1}")), ALU.mult
                                       ).then_inc(S("ml_made"), 1)
            pool.wait_ge(S("t_added"), 48)
            make_head_rows(head_rows_y)
            add_up(4)
            split_hidden(2)
            add_up(5)
            add_up(6)
            split_hidden(3)
            add_up(7)


def _columns(x):
    x = np.asarray(x).reshape(-1)
    return x.reshape(-1, P).T


def _units(w, order, parts):
    k, n = w.shape
    t = w.reshape(parts, k // P // parts, P, n // P, P).transpose(3, 0, 2, 1, 4)
    return t[order].reshape(len(order) * parts, P, k // parts)


def _paired(n):
    return [c + n * h for c in range(n) for h in range(2)]


def kernel(**inputs):
    import concourse.bacc as bacc
    from concourse.bass_utils import run_bass_kernel_spmd

    a = {k: np.asarray(v) for k, v in inputs.items()}
    eight = list(range(DC))
    w8 = np.concatenate([
        _units(a["cm_w1"][0], _paired(DC), 1), _units(a["cm_w2"][0], eight, 1),
        _units(a["ffn_w_in"][0], _paired(FC), 1),
        _units(a["w_v"], eight, 1), _units(a["w_k"], eight, 1), _units(a["w_q"][0], eight, 1),
        _units(a["w_o"][0], eight, 1), _units(a["ffn_w_in"][1], _paired(FC), 1),
        _units(a["rwkv_w_rkv_2"][0, 0], eight, 1), _units(a["rwkv_w_rkv_2"][0, 1], eight, 1),
        _units(a["rwkv_w_rkv_2"][0, 2], eight, 1), _units(a["rwkv_w_o_2"][0], eight, 1),
        _units(np.concatenate([a["ffn_w_gate_2"][0], a["ffn_w_up_2"][0]], 1), _paired(FC), 1),
        _units(a["sgu_w_in_2"][0], [c + DC for c in eight], 1), _units(a["sgu_w_in_2"][0], eight, 1),
        _units(a["sgu_w_out_2"][0], eight, 1),
        _units(np.concatenate([a["ffn_w_gate_2"][1], a["ffn_w_up_2"][1]], 1), _paired(FC), 1),
    ])
    w11 = np.concatenate([_units(w, eight, 2) for w in (a["ffn_w_out"][0], a["ffn_w_out"][1],
                                                        a["ffn_w_down_2"][0], a["ffn_w_down_2"][1])])
    wmod = np.concatenate([w.reshape(D, 6 * DC, P).transpose(1, 2, 0) for w in a["mod_w"]])
    lam = np.zeros((P, 4), np.float32)
    lam[:HEAD_DIM] = a["lam"][0].T
    given = {
        "mod_b": _columns(a["mod_b"]), "norm_g": _columns(a["norm_g"]),
        "cm_b1": _columns(a["cm_b1"]), "cm_dw": _columns(a["cm_dw"]), "cm_dwb": _columns(a["cm_dwb"]),
        "cm_ln_g": _columns(a["cm_ln_g"]), "cm_ln_b": _columns(a["cm_ln_b"]), "cm_b2": _columns(a["cm_b2"]),
        "kv_norm_g": _columns(a["kv_norm_g"]), "lam": lam, "subln_g": _columns(a["subln_g"]),
        "ffn_dw": _columns(a["ffn_dw"]), "ffn_dwb": _columns(a["ffn_dwb"]), "norm_g2": _columns(a["norm_gains_2"]),
        "mix": _columns(a["rwkv_mix_2"]), "w0": _columns(a["rwkv_w0_2"]), "a0": _columns(a["rwkv_a0_2"]),
        "k_k": _columns(a["rwkv_k_k_2"]), "k_a": _columns(a["rwkv_k_a_2"]), "r_k": _columns(a["rwkv_r_k_2"]),
        "gn_w": _columns(a["rwkv_gn_w_2"]), "gn_b": _columns(a["rwkv_gn_b_2"]), "sgu_b_in": _columns(a["sgu_b_in_2"]),
        "sgu_ln_w": _columns(a["sgu_ln_w_2"]), "sgu_ln_b": _columns(a["sgu_ln_b_2"]),
    }
    rest = 2 * P - GATE
    first = np.concatenate([a["rwkv_w1_2"][0], a["rwkv_a1_2"][0], np.pad(a["rwkv_g1_2"][0], ((0, 0), (0, rest)))], 1)
    g2 = np.pad(a["rwkv_g2_2"][0], ((0, rest), (0, 0)))
    arrays = {
        "w8": w8, "w11": w11, "wmod": wmod,
        "par": np.concatenate([given[n] for n, _ in PARAMS], 1),
        "con": constants(),
        "xin": a["x"][0].T.reshape(DC, P, T).transpose(1, 0, 2).reshape(P, DC * T),
        "relb": a["rel_bias"],
        "crow": a["c"].reshape(1, D),
        "lora_in": first.reshape(DC, P, 2 * LORA + 2 * P).transpose(1, 0, 2).reshape(P, -1),
        "lora_out": np.concatenate([np.concatenate([a["rwkv_w2_2"][0], a["rwkv_a2_2"][0]], 0), g2[:P], g2[P:]], 1),
        "sgu_ws": a["sgu_ws_2"][0].transpose(1, 0, 2).reshape(P, -1),
        "sgu_bs": a["sgu_bs_2"][0].reshape(1, -1),
    }
    nc = bacc.Bacc("TRN2", target_bir_lowering=False, num_devices=1)
    sent, args = {}, []
    for name, x in arrays.items():
        x = np.ascontiguousarray(x)
        sent[f"in_{name}"] = x
        args.append(nc.dram_tensor(f"in_{name}", x.shape, mybir.dt.from_np(x.dtype), kind="ExternalInput").ap())
    args.append(nc.dram_tensor("out", (P, DC * T), F32, kind="ExternalOutput").ap())
    program(nc, *args)
    r = run_bass_kernel_spmd(nc, [sent], core_ids=[0])
    got = r.results[0]["out"]
    return np.ascontiguousarray(got.reshape(P, DC, T).transpose(2, 1, 0).reshape(1, T, D))
```
